# Optimizing a Trainium2 kernel written in Bass

```python
import functools
import jax, jax.numpy as jnp
from jax import lax
import numpy as np

D_MODEL = 1024
BATCH = 1
SEQ = 128
DEPTH = 2
DEC_BATCH = 1
DEC_SEQ = 512
PAST_LEN = 128

GRID_W = 64
HEAD_DIM = 64
Q_BLOCK = 128
EPS = 1e-6
ROPE_THETA = 10000.0
MIX_WIDTH = D_MODEL
N_EVEN = (DEPTH + 1) // 2
N_ODD = DEPTH // 2

POOL_WINDOWS = (2, 4, 8, 16)
POOL_GROUPS = len(POOL_WINDOWS)
POOL_WIDTH = MIX_WIDTH // 4
POOL_GW = POOL_WIDTH // POOL_GROUPS
B_HEADS = (MIX_WIDTH - POOL_WIDTH) // HEAD_DIM
B_KV = B_HEADS // 3
EVEN_SIZES = (POOL_WIDTH, B_HEADS * HEAD_DIM, B_KV * HEAD_DIM, B_KV * HEAD_DIM)
C_HEADS = MIX_WIDTH // 2 // HEAD_DIM
C_KV = C_HEADS // 4
C_WINDOW = 128
D_HEADS = MIX_WIDTH // 2 // HEAD_DIM
NA_ROWS = 8
NA_COLS = 16
ODD_SIZES = (C_HEADS * HEAD_DIM, C_KV * HEAD_DIM, C_KV * HEAD_DIM,
             D_HEADS * HEAD_DIM, D_HEADS * HEAD_DIM, D_HEADS * HEAD_DIM)
D_FF = 2816
CONV_W = 3

kernel_name = 'hybrid_diffusion_prefix_trunk_step'

def split_cols(u, sizes):
    offs, acc = [], 0
    for s in sizes[:-1]:
        acc += s
        offs.append(acc)
    return jnp.split(u, offs, axis=-1)

def rmsnorm(x, g):
    x32 = x.astype(jnp.float32)
    y = x32 * lax.rsqrt(jnp.mean(x32 * x32, axis=-1, keepdims=True) + EPS)
    return (y * g.astype(jnp.float32)).astype(x.dtype)

def modulation(cvec, w_mod, b_mod):
    m = jax.nn.silu(cvec) @ w_mod + b_mod
    return tuple(t[:, None, :] for t in jnp.split(m, 6, axis=-1))

def axial_rope(n_tokens):
    t = jnp.arange(n_tokens)
    row = (t // GRID_W).astype(jnp.float32)
    col = (t % GRID_W).astype(jnp.float32)
    axis_dim = HEAD_DIM // 2
    inv_freq = ROPE_THETA ** (-jnp.arange(0, axis_dim, 2, dtype=jnp.float32) / axis_dim)
    ang = jnp.concatenate([row[:, None] * inv_freq, col[:, None] * inv_freq], axis=-1)
    return jnp.cos(ang)[None, :, None, :], jnp.sin(ang)[None, :, None, :]

def apply_rope(x, cos, sin):
    x32 = x.astype(jnp.float32)
    x1, x2 = x32[..., 0::2], x32[..., 1::2]
    out = jnp.stack([x1 * cos - x2 * sin, x1 * sin + x2 * cos], axis=-1).reshape(x.shape)
    return out.astype(x.dtype)

def softmax_logits(s, sink):
    if sink is None:
        return jax.nn.softmax(s, axis=-1)
    m = jnp.maximum(jnp.max(s, axis=-1, keepdims=True), sink)
    e = jnp.exp(s - m)
    return e / (jnp.sum(e, axis=-1, keepdims=True) + jnp.exp(sink - m))

def attend_blocked(q, k, v, sink=None):
    Bn, Sq, H, dh = q.shape
    KV = k.shape[2]
    G = H // KV
    scale = dh ** -0.5
    qb = jnp.moveaxis(q.reshape(Bn, Sq // Q_BLOCK, Q_BLOCK, KV, G, dh), 1, 0)
    sink_b = None if sink is None else sink.astype(jnp.float32).reshape(KV, G)[None, :, :, None, None]

    def one_block(qblk):
        s = jnp.einsum('bqkgd,bskd->bkgqs', qblk, k, preferred_element_type=jnp.float32) * scale
        p = softmax_logits(s, sink_b).astype(v.dtype)
        return jnp.einsum('bkgqs,bskd->bqkgd', p, v)

    o = lax.map(one_block, qb)
    return jnp.moveaxis(o, 0, 1).reshape(Bn, Sq, H, dh)

def window_attention(q, k, v, ctx_k, ctx_v, sink):
    Bn, N, H, dh = q.shape
    KV = k.shape[2]
    G = H // KV
    nb = N // Q_BLOCK
    scale = dh ** -0.5

    def band(x):
        xb = jnp.pad(x.reshape(Bn, nb, Q_BLOCK, KV, dh), ((0, 0), (1, 1), (0, 0), (0, 0), (0, 0)))
        return jnp.concatenate([xb[:, :-2], xb[:, 1:-1], xb[:, 2:]], axis=2)

    kb, vb = band(k), band(v)
    qb = q.reshape(Bn, nb, Q_BLOCK, KV, G, dh)
    q_pos = jnp.arange(N).reshape(nb, Q_BLOCK)
    k_pos = (jnp.arange(nb)[:, None] - 1) * Q_BLOCK + jnp.arange(3 * Q_BLOCK)[None, :]
    valid = ((jnp.abs(q_pos[:, :, None] - k_pos[:, None, :]) <= C_WINDOW)
             & (k_pos >= 0)[:, None, :] & (k_pos < N)[:, None, :])
    s_loc = jnp.einsum('bnqkgd,bnskd->bnkgqs', qb, kb, preferred_element_type=jnp.float32) * scale
    s_loc = jnp.where(valid[None, :, None, None], s_loc, -jnp.inf)
    s_ctx = jnp.einsum('bnqkgd,bskd->bnkgqs', qb, ctx_k, preferred_element_type=jnp.float32) * scale
    sink_b = sink.astype(jnp.float32).reshape(KV, G)[None, None, :, :, None, None]
    p = softmax_logits(jnp.concatenate([s_loc, s_ctx], axis=-1), sink_b).astype(v.dtype)
    n_loc = 3 * Q_BLOCK
    o = (jnp.einsum('bnkgqs,bnskd->bnqkgd', p[..., :n_loc], vb)
         + jnp.einsum('bnkgqs,bskd->bnqkgd', p[..., n_loc:], ctx_v))
    return o.reshape(Bn, N, H, dh)

def neighbourhood_attention(q, k, v, ctx_k, ctx_v, rpb):
    Bn, N, H, dh = q.shape
    rows = N // GRID_W
    kh = min(NA_ROWS, rows)
    kw = NA_COLS
    scale = dh ** -0.5
    qg = q.reshape(Bn, rows, GRID_W, H, dh)
    kg = k.reshape(Bn, rows, GRID_W, H, dh)
    vg = v.reshape(Bn, rows, GRID_W, H, dh)
    col = jnp.arange(GRID_W)
    col_start = jnp.clip(col - kw // 2, 0, GRID_W - kw)
    col_idx = col_start[:, None] + jnp.arange(kw)[None, :]
    ix = (col_idx - col[:, None] + NA_COLS - 1)[:, None, :]
    n_loc = kh * kw

    def one_row(r):
        row_start = jnp.clip(r - kh // 2, 0, rows - kh)
        iy = (row_start + jnp.arange(kh) - r + NA_ROWS - 1)[None, :, None]
        bias = rpb[:, iy, ix].reshape(H, GRID_W, n_loc)

        def gather(x):
            xr = lax.dynamic_slice_in_dim(x, row_start, kh, axis=1)
            xn = xr[:, :, col_idx]
            return jnp.swapaxes(xn, 1, 2).reshape(Bn, GRID_W, n_loc, H, dh)

        kn, vn = gather(kg), gather(vg)
        qr = lax.dynamic_index_in_dim(qg, r, axis=1, keepdims=False)
        s_loc = jnp.einsum('bwhd,bwnhd->bhwn', qr, kn, preferred_element_type=jnp.float32) * scale + bias
        s_ctx = jnp.einsum('bwhd,bshd->bhws', qr, ctx_k, preferred_element_type=jnp.float32) * scale
        p = jax.nn.softmax(jnp.concatenate([s_loc, s_ctx], axis=-1), axis=-1).astype(v.dtype)
        return (jnp.einsum('bhwn,bwnhd->bwhd', p[..., :n_loc], vn)
                + jnp.einsum('bhws,bshd->bwhd', p[..., n_loc:], ctx_v))

    out = lax.map(one_row, jnp.arange(rows))
    return jnp.moveaxis(out, 0, 1).reshape(Bn, N, H, dh)

def pool_mixer(a, w_pool, pool_scale):
    Bn, N, _ = a.shape
    a32 = a.reshape(Bn, N, POOL_GROUPS, POOL_GW).astype(jnp.float32)
    csum = jnp.pad(jnp.cumsum(a32, axis=1), ((0, 0), (1, 0), (0, 0), (0, 0)))
    t = jnp.arange(N)[:, None]
    w = jnp.array(POOL_WINDOWS)[None, :]
    lo = jnp.clip(t - w // 2, 0, N)
    hi = jnp.clip(t - w // 2 + w, 0, N)
    grp = jnp.arange(POOL_GROUPS)[None, :]
    win_sum = csum[:, hi, grp] - csum[:, lo, grp]
    mean = win_sum / (hi - lo).astype(jnp.float32)[None, :, :, None]
    pooled = (mean - a32).astype(a.dtype)
    y = jnp.einsum('bngc,gcd->bngd', pooled, w_pool)
    return y.reshape(Bn, N, POOL_WIDTH) * pool_scale

def even_mixer(h, w_in, w_out, w_pool, pool_scale, g_q, g_k, rope=None, ctx=None):
    Bn, N, _ = h.shape
    a, q, k, v = split_cols(h @ w_in, EVEN_SIZES)
    q = rmsnorm(q.reshape(Bn, N, B_HEADS, HEAD_DIM), g_q)
    k = rmsnorm(k.reshape(Bn, N, B_KV, HEAD_DIM), g_k)
    v = v.reshape(Bn, N, B_KV, HEAD_DIM)
    ya = pool_mixer(a, w_pool, pool_scale)
    if ctx is None:
        yb = attend_blocked(q, k, v)
    else:
        cos, sin = rope
        ctx_k, ctx_v = ctx
        yb = attend_blocked(apply_rope(q, cos, sin),
                            jnp.concatenate([apply_rope(k, cos, sin), ctx_k], axis=1),
                            jnp.concatenate([v, ctx_v], axis=1))
    y = jnp.concatenate([ya, yb.reshape(Bn, N, -1)], axis=-1) @ w_out
    return y, (k, v)

def odd_mixer(h, w_in, w_out, sink, rpb, rope=None, ctx=None):
    Bn, N, _ = h.shape
    qc, kc, vc, qd, kd, vd = split_cols(h @ w_in, ODD_SIZES)
    qc = qc.reshape(Bn, N, C_HEADS, HEAD_DIM)
    kc = kc.reshape(Bn, N, C_KV, HEAD_DIM)
    vc = vc.reshape(Bn, N, C_KV, HEAD_DIM)
    qd = qd.reshape(Bn, N, D_HEADS, HEAD_DIM)
    kd = kd.reshape(Bn, N, D_HEADS, HEAD_DIM)
    vd = vd.reshape(Bn, N, D_HEADS, HEAD_DIM)
    if ctx is None:
        yc = attend_blocked(qc, kc, vc, sink)
        yd = attend_blocked(qd, kd, vd)
    else:
        cos, sin = rope
        ck_c, cv_c, ck_d, cv_d = ctx
        yc = window_attention(apply_rope(qc, cos, sin), apply_rope(kc, cos, sin), vc, ck_c, cv_c, sink)
        yd = neighbourhood_attention(qd, kd, vd, ck_d, cv_d, rpb)
    y = jnp.concatenate([yc.reshape(Bn, N, -1), yd.reshape(Bn, N, -1)], axis=-1) @ w_out
    return y, (kc, vc, kd, vd)

def conv_ffn(h, w_in, w_conv, w_out):
    N = h.shape[1]
    u = h @ w_in
    pad = CONV_W // 2
    up = jnp.pad(u, ((0, 0), (pad, pad), (0, 0)))
    u = sum(up[:, j:j + N] * w_conv[j] for j in range(CONV_W))
    gate, val = jnp.split(u, 2, axis=-1)
    return (jax.nn.silu(gate) * val) @ w_out

def trunk_layer(x, mod, g_mix_pre, g_mix_post, g_ffn_pre, g_ffn_post, w_ffn_in, w_ffn_conv, w_ffn_out, mixer):
    shift1, scale1, gate1, shift2, scale2, gate2 = mod
    h = rmsnorm(x, g_mix_pre) * (1 + scale1) + shift1
    y, ctx_state = mixer(h)
    x = x + gate1 * rmsnorm(y, g_mix_post)
    h = rmsnorm(x, g_ffn_pre) * (1 + scale2) + shift2
    x = x + gate2 * rmsnorm(conv_ffn(h, w_ffn_in, w_ffn_conv, w_ffn_out), g_ffn_post)
    return x, ctx_state

def setup_inputs(seed: int = 0) -> dict:
    key = jax.random.key(seed)
    ks = jax.random.split(key, 28)

    def nrm(k, shape, scale=1.0):
        return jax.random.normal(k, shape, jnp.float32) * scale

    even_in = sum(EVEN_SIZES)
    odd_in = sum(ODD_SIZES)
    return {
        'x_prompt': nrm(ks[0], (BATCH, SEQ, D_MODEL)),
        'x_sample': nrm(ks[1], (DEC_BATCH, DEC_SEQ, D_MODEL)),
        'cache_b_k': nrm(ks[2], (DEC_BATCH, N_EVEN, PAST_LEN, B_KV, HEAD_DIM)),
        'cache_b_v': nrm(ks[3], (DEC_BATCH, N_EVEN, PAST_LEN, B_KV, HEAD_DIM)),
        'cache_c_k': nrm(ks[4], (DEC_BATCH, N_ODD, PAST_LEN, C_KV, HEAD_DIM)),
        'cache_c_v': nrm(ks[5], (DEC_BATCH, N_ODD, PAST_LEN, C_KV, HEAD_DIM)),
        'cache_d_k': nrm(ks[6], (DEC_BATCH, N_ODD, PAST_LEN, D_HEADS, HEAD_DIM)),
        'cache_d_v': nrm(ks[7], (DEC_BATCH, N_ODD, PAST_LEN, D_HEADS, HEAD_DIM)),
        'c': nrm(ks[8], (DEC_BATCH, D_MODEL)),
        'c_ctx': nrm(ks[9], (D_MODEL,)),
        'w_mod': nrm(ks[10], (DEPTH, D_MODEL, 6 * D_MODEL), 0.5 * D_MODEL ** -0.5),
        'b_mod': nrm(ks[11], (DEPTH, 6 * D_MODEL), 0.01),
        'g_mix_pre': 1.0 + nrm(ks[12], (DEPTH, D_MODEL), 0.05),
        'g_mix_post': 1.0 + nrm(ks[13], (DEPTH, D_MODEL), 0.05),
        'g_ffn_pre': 1.0 + nrm(ks[14], (DEPTH, D_MODEL), 0.05),
        'g_ffn_post': 1.0 + nrm(ks[15], (DEPTH, D_MODEL), 0.05),
        'w_in_even': nrm(ks[16], (N_EVEN, D_MODEL, even_in), D_MODEL ** -0.5),
        'w_pool': nrm(ks[17], (N_EVEN, POOL_GROUPS, POOL_GW, POOL_GW), POOL_GW ** -0.5),
        'pool_scale': 1.0 + nrm(ks[18], (N_EVEN, POOL_WIDTH), 0.1),
        'g_q_b': 1.0 + nrm(ks[19], (N_EVEN, HEAD_DIM), 0.05),
        'g_k_b': 1.0 + nrm(ks[20], (N_EVEN, HEAD_DIM), 0.05),
        'w_in_odd': nrm(ks[21], (N_ODD, D_MODEL, odd_in), D_MODEL ** -0.5),
        'sink_c': nrm(ks[22], (N_ODD, C_HEADS)),
        'rpb_d': nrm(ks[23], (N_ODD, D_HEADS, 2 * NA_ROWS - 1, 2 * NA_COLS - 1), 0.2),
        'w_mix_out': nrm(ks[24], (DEPTH, MIX_WIDTH, D_MODEL), MIX_WIDTH ** -0.5),
        'w_ffn_in': nrm(ks[25], (DEPTH, D_MODEL, 2 * D_FF), D_MODEL ** -0.5),
        'w_ffn_conv': nrm(ks[26], (DEPTH, CONV_W, 2 * D_FF), CONV_W ** -0.5),
        'w_ffn_out': nrm(ks[27], (DEPTH, D_FF, D_MODEL), D_FF ** -0.5),
    }

def reference(x_prompt, x_sample, cache_b_k, cache_b_v, cache_c_k, cache_c_v, cache_d_k, cache_d_v,
              c, c_ctx, w_mod, b_mod, g_mix_pre, g_mix_post, g_ffn_pre, g_ffn_post,
              w_in_even, w_pool, pool_scale, g_q_b, g_k_b, w_in_odd, sink_c, rpb_d,
              w_mix_out, w_ffn_in, w_ffn_conv, w_ffn_out):
    cos, sin = axial_rope(x_sample.shape[1])
    xp, xs = x_prompt, x_sample
    b_k, b_v, c_k, c_v, d_k, d_v = [], [], [], [], [], []
    for l in range(DEPTH):
        i = l // 2
        ffn = (g_mix_pre[l], g_mix_post[l], g_ffn_pre[l], g_ffn_post[l], w_ffn_in[l], w_ffn_conv[l], w_ffn_out[l])
        mod_p = modulation(c_ctx[None, :], w_mod[l], b_mod[l])
        mod_s = modulation(c, w_mod[l], b_mod[l])
        if l % 2 == 0:
            mix = functools.partial(even_mixer, w_in=w_in_even[i], w_out=w_mix_out[l], w_pool=w_pool[i],
                                    pool_scale=pool_scale[i], g_q=g_q_b[i], g_k=g_k_b[i])
            xp, (kb, vb) = trunk_layer(xp, mod_p, *ffn, mixer=mix)
            xs, _ = trunk_layer(xs, mod_s, *ffn, mixer=functools.partial(
                mix, rope=(cos, sin), ctx=(cache_b_k[:, i], cache_b_v[:, i])))
            b_k.append(kb)
            b_v.append(vb)
        else:
            mix = functools.partial(odd_mixer, w_in=w_in_odd[i], w_out=w_mix_out[l], sink=sink_c[i], rpb=rpb_d[i])
            xp, (kc, vc, kd, vd) = trunk_layer(xp, mod_p, *ffn, mixer=mix)
            xs, _ = trunk_layer(xs, mod_s, *ffn, mixer=functools.partial(
                mix, rope=(cos, sin),
                ctx=(cache_c_k[:, i], cache_c_v[:, i], cache_d_k[:, i], cache_d_v[:, i])))
            c_k.append(kc)
            c_v.append(vc)
            d_k.append(kd)
            d_v.append(vd)
    new_b_k = jnp.stack(b_k, axis=1)
    new_b_v = jnp.stack(b_v, axis=1)
    new_c_k = jnp.stack(c_k, axis=1)
    new_c_v = jnp.stack(c_v, axis=1)
    new_d_k = jnp.stack(d_k, axis=1)
    new_d_v = jnp.stack(d_v, axis=1)
    return (xp, xs, new_b_k, new_b_v, new_c_k, new_c_v, new_d_k, new_d_v)


_drawn_inputs = setup_inputs


def setup_inputs(seed=0):
    import zlib

    import numpy as np

    out = dict(_drawn_inputs(seed))
    spreads = {}
    factors = {'cache_b_k': 4.464,
     'cache_b_v': 3.277,
     'g_mix_post': 2.762,
     'g_ffn_post': 2.929,
     'g_q_b': 8.0,
     'sink_c': 8.0,
     'rpb_d': 3.929}
    for name, (base, spread) in spreads.items():
        noise = np.random.default_rng([zlib.crc32(name.encode()), seed]).standard_normal(out[name].shape)
        drawn = base * np.exp(spread * noise) if base else spread * noise
        out[name] = __import__('jax').numpy.asarray(drawn.astype(out[name].dtype))
    for name, factor in factors.items():
        out[name] = (out[name] * factor).astype(out[name].dtype)
    return out
```

```python
from contextlib import ExitStack

import concourse.bass as bass
from concourse import mybir
from concourse.alu_op_type import AluOpType as ALU

F32 = mybir.dt.float32
F32R = mybir.dt.float32r
ACT = mybir.ActivationFunctionType
AX = mybir.AxisListType

P = 128
D = 1024
KD = D // P
NS = 512
NP = 128
NT = NS + NP
HT = NT // 2
DH = 64
SCALE = DH ** -0.5
EPS = 1e-6
FH = 11
PAD = 8
AW = PAD + NS + 2 * PAD + NP + PAD
AP0 = PAD + NS + 2 * PAD
UW = 1 + NS + 2 + NP + 1
UP0 = 1 + NS + 2
CW = UW - 2
CP0 = UP0 - 1
SLOT = FH * P
CTX0, PR0 = NS, NS + NP
POOL_STEPS = 18
RPB = 15 * 64

UNITS = {}
NU = 0
for _l, _in in ((0, 12), (1, 18)):
    for _kind, _count in (("in", _in), ("mix", 8), ("fin0", 22), ("fout0", 8), ("fin1", 22), ("fout1", 8)):
        UNITS[(_l, _kind)] = (NU, _count)
        NU += _count
PHASES = list(UNITS)
RUNS = [(8, 42), (FH, 8), (8, 22), (FH, 8), (8, 48), (FH, 8), (8, 22), (FH, 8)]
GROUPS = {"B": (0, 2, 3, 1), "C": (6, 2, 2, 1), "D": (10, 2, 2, 2)}
JOBS = 10


class Job:

    def __init__(self, kind, step):
        self.kind, self.pair, self.half = kind, step // JOBS, step % 2
        self.t = step % JOBS // 2
        self.prompt = self.t == 4
        near = (max(self.t - 1, 0), min(self.t + 1, 3)) if kind == "C" else (0, 3)
        self.tiles = [] if self.prompt else list(range(near[0], near[1] + 1))
        self.lo = NS - P * len(self.tiles)
        self.scaled = kind == "C" or (kind == "D" and not self.prompt)
        self.rows = slice(DH * self.half, DH * self.half + DH)
        self.q0 = P * self.t
        self.vctx = 5 if self.prompt else 4
        self.kctx = PR0 if self.prompt else CTX0
        self.latent = 8 * self.pair + min(step % JOBS, 8)

    def head_col(self, it):
        if self.kind == "B":
            return DH * 6 * it + DH * (self.pair + 3 * self.half)
        if self.kind == "C":
            return DH * 2 * it + DH * (self.pair + 4 * self.half)
        return 4 * DH * it + (512 + DH * (2 * self.pair + self.half))

    def v_col(self, it):
        if self.kind == "B":
            return P * it + DH * self.half
        if self.kind == "C":
            return DH * self.half
        return 4 * DH * it + (P + DH * (2 * self.pair + self.half))

    def mask_from(self):
        return {0: P, 1: 0, 2: 0, 3: 4 * P, 4: 3 * P}[self.t]


def kchunks(phase):
    return FH if phase[1].startswith("fout") else KD


def program(nc, a, o):
    with ExitStack() as ctx:
        place = [16512]

        def at(name, shape, dt, byte):
            return nc.alloc_sbuf_tensor_at(name, shape, dt, offset=byte)

        def sb(name, shape, dt=F32):
            n = 4
            for s in shape[1:]:
                n *= s
            t = at(name, shape, dt, place[0])
            place[0] += (n + 31) // 32 * 32
            return t

        def sem(name):
            return ctx.enter_context(nc.semaphore(name))

        x = sb("x", [P, KD, NT])
        y = sb("y", [P, KD, NT])
        raw = sb("raw", [P, 2, SLOT])
        whi = sb("whi", [P, 2, SLOT], F32R)
        wlo = sb("wlo", [P, 2, SLOT], F32R)
        region_h = place[0]
        hh = sb("hh", [P, KD, NT], F32R)
        hl = sb("hl", [P, KD, NT], F32R)
        region_f = place[0]
        ffh = sb("ffh", [P, FH, NT], F32R)
        ffl = sb("ffl", [P, FH, NT], F32R)
        work = sb("work", [P, 5120])
        cos = sb("cos", [P, NS])
        sin = sb("sin", [P, NS])
        maskc = sb("maskc", [P, 7 * P])
        maskd = sb("maskd", [P, 64])
        ident = sb("ident", [P, P])
        onesd = sb("onesd", [P, P])
        onesh = sb("onesh", [P, P])
        wpool = sb("wpool", [P, 2, P])
        wconv = sb("wconv", [P, 88, 3])
        cvec = sb("cvec", [P, 2 * KD])
        csilu = sb("csilu", [P, 2 * KD])
        bmod = sb("bmod", [P, 96])
        mod = sb("mod", [P, 2, 96, ])
        gains = sb("gains", [P, 2, 4, KD])
        coef = sb("coef", [P, 2, 2, 4, KD])
        small = sb("small", [P, 2 + 2 + 8])
        pscale = small[:, 0:2]
        gqk = small[:, 2:4]
        sink = small[:, 4:12]
        stat8 = sb("stat8", [P, 7, 2])
        assert place[0] <= 229368, place[0]
        pos = [region_h]

        def over(name, shape, dt=F32):
            n = 4
            for s in shape[1:]:
                n *= s
            t = at(name, shape, dt, pos[0])
            pos[0] += n
            return t
        qs = over("qs", [P, 3, NT])
        ks = over("ks", [P, 2, 6 * P])
        ssb = over("ssb", [P, 2, NT])
        pb = over("pb", [P, 2, NT])
        pts = over("pts", [P, 2, NT])
        assert pos[0] <= region_f
        pos[0] = region_f
        qk = over("qk", [P, 13, 6 * P])
        v = over("v", [P, 6, NT])
        assert pos[0] <= region_f + 2 * FH * NT * 4
        osb = y[:, :, :].rearrange("p k n -> p (k n)").rearrange("p (t d) -> p t d", t=5)
        yf = y[:, :, :].rearrange("p k n -> p (k n)")

        def ring(base, n, width, where=work):
            return [where[:, base + i * width:base + (i + 1) * width] for i in range(n)]
        sq = ring(0, 2, NT)
        tn = ring(1280, 2, NT)
        hf = ring(2560, 2, NT)
        std = work[:, 3840:4480]
        rec = work[:, 4480:5120]
        ub = ring(0, 2, UW)
        cb = ring(2 * UW, 2, CW)
        sg = work[:, 2 * UW + 2 * CW:2 * UW + 3 * CW]
        fft = work[:, 2 * UW + 3 * CW:2 * UW + 3 * CW + NT]
        mraw = [work[:, i * 1024:(i + 1) * 1024] for i in range(4)]
        apad = ring(0, 2, AW)
        ptmp = ring(2 * AW, 2, AW)
        pfo = [work[:, i * AW:i * AW + NT] for i in range(2)]
        icnt = ring(4 * AW, 2, NT)
        erow = [work[:, i * 1024:i * 1024 + RPB] for i in range(4)]
        fsq = [yf[:, i * NT:(i + 1) * NT] for i in range(2)]
        fstd = yf[:, 1280:1920]
        frec = yf[:, 1920:2560]
        fsh = yf[:, 2560:3072]
        ft1 = yf[:, 3072:3584]
        ft2 = yf[:, 3584:4096]
        fqn = yf[:, 4096:4608]

        ps = ctx.enter_context(nc.psum_tensor("ps", [P, 8, 512], F32))
        psf = ps[:, :, :].rearrange("p b n -> p (b n)")
        bankA = [ps[:, 0, 0:HT], ps[:, 2, 0:HT]]
        bankB = [ps[:, 1, 0:HT], ps[:, 3, 0:HT]]
        latent = [ps[:, 0, :], ps[:, 2, :]]
        context = [ps[:, 1, 0:NP], ps[:, 3, 0:NP]]
        statA, statB = ps[:, 5, 0:HT], ps[:, 6, 0:HT]

        s_raw = [sem("weights_loaded_0"), sem("weights_loaded_1")]
        s_hi = sem("weights_hi")
        s_lo = sem("weights_lo")
        s_unit = sem("unit_multiplied")
        s_fa = sem("first_half_read")
        s_fb = sem("second_half_read")
        s_const = sem("constants_loaded")
        s_ctx = sem("cached_context_loaded")
        s_ctx1 = sem("cached_context_1_loaded")
        s_cvec = sem("c_loaded")
        s_x = sem("x_loaded")
        s_azero = sem("pool_pads_zeroed")
        s_uzero = sem("conv_pads_zeroed")
        s_csilu = sem("c_activated")
        s_mraw = [sem(f"mod_weights_loaded_{i}") for i in range(4)]
        s_mod = sem("mod_multiplied")
        s_modb = sem("mod_biased")
        s_coef = sem("coefficients_ready")
        s_sq = sem("square_ready")
        s_stat = sem("square_summed")
        s_std = sem("deviation_ready")
        s_rec = sem("reciprocal_ready")
        s_t = sem("normed_ready")
        s_tu = sem("normed_used")
        s_hh = sem("h_hi")
        s_hl = sem("h_lo")
        s_pool = sem("pool_step")
        s_icnt = sem("pool_counts_loaded")
        s_fsq = sem("head_square")
        s_fst = sem("head_square_summed")
        s_fstd = sem("head_deviation")
        s_frec = sem("head_reciprocal")
        s_fn = sem("head_normed")
        s_fsh = sem("rope_swapped")
        s_ft1 = sem("rope_sin_part")
        s_ft2 = sem("rope_cos_part")
        s_fro = sem("rope_done")
        s_stage = sem("pair_staged")
        s_sc = sem("scores_ready")
        s_ss = sem("scores_scaled")
        s_mx = sem("max_ready")
        s_neg = sem("neg_max_ready")
        s_es = sem("sink_exp")
        s_p = sem("exp_ready")
        s_pt = sem("probs_turned")
        s_pta = sem("turned_latent_copied")
        s_ptb = sem("turned_ctx_copied")
        s_o = sem("values_summed")
        s_den = sem("denominator_ready")
        s_rinv = sem("inverse_denominator")
        s_oe = sem("attention_out_ready")
        s_otp = sem("out_turned")
        s_pf = sem("pool_out_scaled")
        s_oth = sem("mix_in_hi")
        s_otl = sem("mix_in_lo")
        s_eload = [sem(f"bias_rows_loaded_{i}") for i in range(4)]
        s_e = sem("bias_rows_masked")
        s_c2 = sem("conv_two_taps")
        s_c1 = sem("conv_mid_tap")
        s_cv = sem("conv_done")
        s_sg = sem("gate_activated")
        s_ffm = sem("gated")
        s_ffh = sem("ff_hi")
        s_ffl = sem("ff_lo")
        s_out = sem("new_kv_stored")
        s_outx = sem("x_stored")

        block = ctx.enter_context(nc.Block())

        def slot(t, s, k):
            return t[:, s, k * P:(k + 1) * P]

        CONSTS = [("cos", cos[:, :]), ("sin", sin[:, :]), ("maskc", maskc[:, :]), ("maskd", maskd[:, :]),
                  ("ident", ident[:, :]), ("onesd", onesd[:, :]), ("onesh", onesh[:, :]), ("wpool", wpool[:, :, :]),
                  ("wconv", wconv[:, :, :]), ("bmod", bmod[:, :]), ("gains", gains[:, :, :, :]),
                  ("small", small[:, :])]
        n_const = len(CONSTS)

        def chunk(t, k):
            return t[:, bass.ds(k, 1), :].rearrange("p a n -> p (a n)")

        def part(t, k, f, n):
            return t[:, bass.ds(k, 1), f:f + n].rearrange("p a n -> p (a n)")

        def mod_col(layer, part, stream):
            c = 48 * layer + 8 * part
            return mod[:, stream, c:c + KD]

        SEG = ((0, 0, NS), (1, NS, NT))

        def norm_index(layer, which):
            return 4 * layer + which

        @block.sync
        def _(sp):
            w8, w11 = a["w8"], a["w11"]

            def load(src, s, width):
                return sp.dma_start(raw[:, s, 0:width], src.rearrange("a p n -> (a p) n")).then_inc(s_raw[s], 16)

            sp.dma_start(cvec[:, :], a["cvec"]).then_inc(s_cvec, 16)
            for s in range(4):
                sp.dma_start(mraw[s], a["wmod"][s]).then_inc(s_mraw[s], 16)
            for s in range(2):
                load(w8[s:s + 1], s, KD * P)
            sp.dma_start(x[:, :, :].rearrange("p k n -> p (k n)"), a["x"]).then_inc(s_x, 16)
            with sp.Fori(1, 24) as it:
                for s in range(4):
                    sp.wait_ge(s_mod, 4 * it + s + 1)
                    sp.dma_start(mraw[s], a["wmod"][bass.ds(4 * it + s, 1)].rearrange("a p n -> (a p) n")
                                 ).then_inc(s_mraw[s], 16)
            u = 0
            base = {8: 0, FH: 0}
            for kk, n in RUNS:
                src = w8 if kk == 8 else w11
                first = 1 if u == 0 else 0
                with sp.Fori(first, n // 2) as h:
                    for s in range(2):
                        sp.wait_ge(s_lo, 2 * h + (u + s - 1))
                        load(src[bass.ds(2 * h + (base[kk] + s), 1)], s, kk * P)
                base[kk] += n
                u += n
            sp.wait_ge(s_tu, 64 + 2)
            sp.dma_start(o["x"], x[:, :, :].rearrange("p k n -> p (k n)")).then_inc(s_outx, 16)
            sp.wait_ge(s_out, 16 * 4)
            sp.wait_ge(s_outx, 16)

        @block.scalar
        def _(act):
            def hi(s, kk, pair):
                act.wait_ge(s_raw[s], 16 * pair + 16)
                act.wait_ge(s_unit, 2 * pair + (s + 1))
                nc.scalar.activation(whi[:, s, 0:kk * P], raw[:, s, 0:kk * P], ACT.Copy).then_inc(s_hi, 1)

            def pairs(phase, evac, skip_first=0):
                u0, n = UNITS[phase]
                nxt = PHASES.index(phase) + 1
                kk = kchunks(phase)
                knext = kchunks(PHASES[nxt]) if nxt < len(PHASES) else None

                def body(h, k2):
                    for s in range(2):
                        act.wait_ge(s_unit, 2 * h + (u0 + s + 3))
                        if k2 is not None:
                            hi(s, k2, h + (u0 // 2 + 1))
                        evac(h, s, 2 * h + (u0 + s))
                return body, n // 2, kk, knext

            def run(phase, evac):
                body, n, kk, knext = pairs(phase, evac)
                if knext == kk:
                    with act.Fori(0, n) as h:
                        body(h, kk)
                else:
                    with act.Fori(0, n - 1) as h:
                        body(h, kk)
                    body(n - 1, knext)

            def copy_a(dst, s):
                nc.scalar.activation(dst, bankA[s], ACT.Copy).then_inc(s_fa, 1)

            def square(k, n, src, s):
                act.wait_ge(s_stat, k + (8 * n + 1))
                act.nop(nofuse=True)
                nc.scalar.activation(sq[s], src, ACT.Square).then_inc(s_sq, 1)

            def deviation(n):
                act.wait_ge(s_stat, 8 * n + 10)
                if n:
                    act.wait_ge(s_rec, n)
                nc.scalar.activation(std[:, 0:HT], statA, ACT.Sqrt, bias=EPS).then_inc(s_std, 1)
                nc.scalar.activation(std[:, HT:NT], statB, ACT.Sqrt, bias=EPS).then_inc(s_std, 1)

            def pre_norm(layer, which):
                n = norm_index(layer, which)
                part = 0 if which == 0 else 3
                hidx = 8 * (2 * layer + which // 2)
                deviation(n)
                with act.Fori(0, KD // 2) as h:
                    for s in range(2):
                        act.wait_ge(s_t, 2 * h + (8 * n + s + 1))
                        act.wait_ge(s_hl, 2 * h + (hidx + s + 1))
                        for st, f, t in SEG:
                            last = nc.scalar.activation(
                                hf[s][:, f:t], tn[s][:, f:t], ACT.Identity,
                                scale=coef[:, layer, st, which, bass.ds(2 * h + s, 1)],
                                bias=mod_col(layer, part, st)[:, bass.ds(2 * h + s, 1)])
                        last.then_inc(s_tu, 1)
                        act.wait_ge(s_tu, 2 * h + (8 * n + s + 3))
                        nc.scalar.activation(chunk(hh, 2 * h + s), hf[s], ACT.Copy).then_inc(s_hh, 1)

            def post_norm(layer, which, squares):
                n = norm_index(layer, which)
                deviation(n)
                if squares:
                    with act.Fori(0, 4) as h:
                        for s in range(2):
                            act.wait_ge(s_tu, 2 * h + (8 * n + s + 3))
                            square(2 * h + s, n + 1, chunk(x, 2 * h + s), s)

            for name, dst in CONSTS:
                act.dma_start(dst, a[name]).then_inc(s_const, 16)
            act.dma_start(qk[:, 6:8, CTX0:PR0], a["kctx0"]).then_inc(s_ctx, 16)
            act.dma_start(v[:, 4, 0:2 * P], a["vctx0"]).then_inc(s_ctx, 16)
            act.wait_ge(s_cvec, 16)
            nc.scalar.activation(csilu[:, :], cvec[:, :], ACT.Silu).then_inc(s_csilu, 1)
            for s in range(2):
                hi(s, KD, 0)
            act.wait_ge(s_mod, 96 + 4)
            act.wait_ge(s_x, 16)
            with act.Fori(0, 4) as h:
                for s in range(2):
                    square(2 * h + s, 0, chunk(x, 2 * h + s), s)
            act.wait_ge(s_coef, 16)
            pre_norm(0, 0)

            def unit_pair(pair, dsts, k2=KD):
                for s in range(2):
                    act.wait_ge(s_unit, 2 * pair + (s + 3))
                    hi(s, k2, pair + 1)
                    copy_a(dsts[s], s)

            def value_pair(pair, col):
                act.wait_ge(s_unit, 2 * pair + 4)
                for s in range(2):
                    hi(s, KD, pair + 1)
                nc.scalar.activation(v[:, 0:2, bass.ds(col, 2 * P)], ps[:, 0, :], ACT.Copy).then_inc(s_fa, 2)

            act.wait_ge(s_azero, 1)
            unit_pair(0, [apad[s][:, PAD:PAD + HT] for s in range(2)])
            with act.Fori(0, 4) as h:
                unit_pair(h + 1, [part(qk, 2 * h + s, 0, HT) for s in range(2)])
            value_pair(5, 0)

            with act.Fori(0, 4) as h:
                for s in range(2):
                    c = 2 * h + s
                    act.wait_ge(s_fa, c + 5)
                    act.wait_ge(s_fb, c + 5)
                    act.wait_ge(s_fst, c + 1)
                    qc = qk[:, bass.ds(c, 1), :].rearrange("p a n -> p (a n)")
                    nc.scalar.activation(fsq[s][:, 0:NS], qc[:, 0:NS], ACT.Square).then_inc(s_fsq, 1)
                    nc.scalar.activation(fsq[s][:, NS:NT], qc[:, PR0:PR0 + NP], ACT.Square).then_inc(s_fsq, 1)
                    act.wait_ge(s_fst, c + 3)
                    act.wait_ge(s_frec, c + 1)
                    nc.scalar.activation(fstd[:, 0:HT], statA, ACT.Sqrt, bias=EPS).then_inc(s_fstd, 1)
                    nc.scalar.activation(fstd[:, HT:NT], statB, ACT.Sqrt, bias=EPS).then_inc(s_fstd, 1)

            def attention(kind):
                g0, its, npair, nk = GROUPS[kind]
                with act.Fori(0, its) as it:
                    nj = JOBS * npair
                    jb = JOBS * g0
                    for step in range(nj + 1):
                        if step < nj:
                            job = Job(kind, step)
                            jv = nj * it + (jb + step)
                            s = step % 2
                            act.wait_ge(s_neg, jv + 1)
                            act.wait_ge(s_pt, jv + 1)
                            act.wait_ge(s_rinv, jv + 1)
                            if kind == "C":
                                act.nop(nofuse=True)
                                nc.scalar.activation(stat8[:, 2, s:s + 1], sink[:, bass.ds(2 * it + (job.pair + 4 * job.half), 1)], ACT.Exp,
                                                     bias=stat8[:, 1, s:s + 1]).then_inc(s_es, 1)
                            src, sc = (ssb[:, s, job.lo:NT], 1.0) if job.scaled else (
                                psf[:, 1024 * s + job.lo:1024 * s + NT], SCALE)
                            nc.scalar.activation(pb[:, s, job.lo:NT], src, ACT.Exp, bias=stat8[:, 1, s:s + 1],
                                                 scale=sc, accum_out=stat8[:, 3, s:s + 1]).then_inc(s_p, 1)
                        if step >= 1:
                            job = Job(kind, step - 1)
                            jv = nj * it + (jb + step - 1)
                            if not job.prompt:
                                act.wait_ge(s_pt, jv + 3)
                                act.wait_ge(s_o, jv + 1)
                                nc.scalar.activation(pts[:, (step - 1) % 2, job.lo:NS], ps[:, 4, job.lo:NS],
                                                     ACT.Copy).then_inc(s_pta, 1)

            attention("B")

            def mix_in_hi(n, first_event, dst0, wait_pool=False):
                for c in range(n):
                    e = first_event + c
                    s = c % 2
                    act.wait_ge(s_otp, e + 1)
                    nc.scalar.activation(hh[:, dst0 + c, 0:NS], latent[s], ACT.Copy).then_inc(s_oth, 1)
                    nc.scalar.activation(hh[:, dst0 + c, NS:NT], context[s], ACT.Copy).then_inc(s_oth, 1)

            for c in range(2):
                act.wait_ge(s_otp, c + 1)
                nc.scalar.activation(pfo[c][:, 0:NS], latent[c], ACT.Copy, scale=pscale[:, c:c + 1]).then_inc(s_pf, 1)
                nc.scalar.activation(pfo[c][:, NS:NT], context[c], ACT.Copy, scale=pscale[:, c:c + 1]).then_inc(s_pf, 1)
                act.wait_ge(s_pf, 2 * c + 2)
                nc.scalar.activation(hh[:, c, :], pfo[c], ACT.Copy).then_inc(s_oth, 1)
            mix_in_hi(6, 2, 2)

            def y_phase(phase, norm, copies, squares):
                u0, n = UNITS[phase]

                def f(h, s, u):
                    if copies:
                        copy_a(part(y, 2 * h + s, 0, HT), s)
                    if squares:
                        act.wait_ge(s_fa, u + 3)
                        act.wait_ge(s_fb, u + 3)
                        square(2 * h + s, norm, chunk(y, 2 * h + s), s)
                run(phase, f)

            def ffn_half(layer, half):
                phase = (layer, f"fin{half}")
                u0 = UNITS[phase][0]
                f0 = 22 * layer + FH * half

                def f(h, s, u):
                    fp = h + f0
                    act.wait_ge(s_cv, 2 * h + (2 * f0 + s + 1))
                    copy_a(ub[s][:, 1:1 + HT], s)
                    act.wait_ge(s_fa, u + 3)
                    act.wait_ge(s_fb, u + 3)
                    if s == 0:
                        act.wait_ge(s_sg, fp + 1)
                    act.wait_ge(s_ffm, fp + 1)
                    nc.scalar.activation(cb[s], ub[s][:, 1:1 + CW], ACT.Copy,
                                         scale=wconv[:, bass.ds(2 * h + (2 * f0 + s), 1), 1]).then_inc(s_c1, 1)
                    if s == 1:
                        act.wait_ge(s_cv, 2 * h + (2 * f0 + 3))
                        nc.scalar.activation(sg, cb[0], ACT.Silu).then_inc(s_sg, 1)
                        act.wait_ge(s_ffm, fp + 2)
                        nc.scalar.activation(ffh[:, bass.ds(h, 1), :].rearrange("p a n -> p (a n)"), fft,
                                             ACT.Copy).then_inc(s_ffh, 1)
                run(phase, f)

            def ffn(layer):
                act.wait_ge(s_uzero, 6 * (layer + 1))
                act.wait_ge(s_out, 32 * (layer + 1))
                ffn_half(layer, 0)
                y_phase((layer, "fout0"), None, True, False)
                ffn_half(layer, 1)
                y_phase((layer, "fout1"), norm_index(layer, 3), False, True)

            y_phase((0, "mix"), 1, True, True)
            post_norm(0, 1, True)
            pre_norm(0, 2)
            ffn(0)
            post_norm(0, 3, True)
            pre_norm(1, 0)

            p1 = UNITS[(1, "in")][0] // 2
            with act.Fori(0, 6) as h:
                unit_pair(h + p1, [part(qk, 2 * h + s, 0, HT) for s in range(2)])
            act.wait_ge(s_unit, 2 * p1 + 12 + 3)
            hi(0, KD, p1 + 7)
            copy_a(qk[:, 12, 0:HT], 0)
            act.wait_ge(s_unit, 2 * p1 + 13 + 3)
            hi(1, KD, p1 + 7)
            nc.scalar.activation(v[:, 0:4, 0:P], latent[1], ACT.Copy).then_inc(s_fa, 1)
            with act.Fori(0, 2) as h:
                value_pair(h + (p1 + 7), 256 * h + P)
            attention("C")
            attention("D")
            mix_in_hi(8, 8, 0)
            y_phase((1, "mix"), 5, True, True)
            post_norm(1, 1, True)
            pre_norm(1, 2)
            ffn(1)
            post_norm(1, 3, False)

        @block.vector
        def _(dve):
            V = nc.vector

            def lo(s, kk, u):
                dve.wait_ge(s_hi, u + 1)
                V.tensor_tensor(wlo[:, s, 0:kk * P], raw[:, s, 0:kk * P], whi[:, s, 0:kk * P].bitcast(F32),
                                ALU.subtract).then_inc(s_lo, 1)

            def run(phase, evac):
                u0, n = UNITS[phase]
                nxt = PHASES.index(phase) + 1
                kk = kchunks(phase)
                knext = kchunks(PHASES[nxt]) if nxt < len(PHASES) else None

                def body(h, k2):
                    for s in range(2):
                        u = 2 * h + (u0 + s)
                        dve.wait_ge(s_unit, u + 3)
                        evac(h, s, u, lambda: lo(s, k2, u + 2) if k2 is not None else None)
                if knext == kk:
                    with dve.Fori(0, n // 2) as h:
                        body(h, kk)
                else:
                    with dve.Fori(0, n // 2 - 1) as h:
                        body(h, kk)
                    body(n // 2 - 1, knext)

            def copy_b(dsts, s):
                f = 0
                for dst in dsts:
                    n = HT if len(dsts) == 1 else (NS - HT, NP)[f > 0]
                    last = V.tensor_copy(dst, bankB[s][:, f:f + n])
                    f += n
                last.then_inc(s_fb, 1)

            def unit_pair(pair, dsts, k2=KD):
                for s in range(2):
                    dve.wait_ge(s_unit, 2 * pair + (s + 3))
                    copy_b(dsts[s], s)
                    lo(s, k2, 2 * pair + (s + 2))

            def reciprocal(n):
                dve.wait_ge(s_std, 2 * n + 2)
                if n:
                    dve.wait_ge(s_t, 8 * n)
                V.reciprocal(rec, std).then_inc(s_rec, 1)

            def pre_norm(layer, which):
                n = norm_index(layer, which)
                hidx = 8 * (2 * layer + which // 2)
                reciprocal(n)
                with dve.Fori(0, KD // 2) as h:
                    for s in range(2):
                        dve.wait_ge(s_hh, 2 * h + (hidx + s + 1))
                        V.tensor_tensor(chunk(hl, 2 * h + s), hf[s], chunk(hh, 2 * h + s).bitcast(F32),
                                        ALU.subtract).then_inc(s_hl, 1)

            def post_norm(layer, which):
                n = norm_index(layer, which)
                reciprocal(n)
                with dve.Fori(0, KD // 2) as h:
                    for s in range(2):
                        dve.wait_ge(s_t, 2 * h + (8 * n + s + 1))
                        for st, f, t in SEG:
                            xs = part(x, 2 * h + s, f, t - f)
                            last = V.scalar_tensor_tensor(
                                out=xs, in0=tn[s][:, f:t], scalar=coef[:, layer, st, which, bass.ds(2 * h + s, 1)],
                                in1=xs, op0=ALU.mult, op1=ALU.add)
                        last.then_inc(s_tu, 1)

            for s in range(2):
                lo(s, KD, s)
            dve.wait_ge(s_mod, 96 + 4)
            dve.wait_ge(s_const, 16 * n_const)
            for st in range(2):
                V.tensor_tensor(mod[:, st, :], ps[:, 4, 0:192].rearrange("p (c s) -> p s c", s=2)[:, st, :], bmod[:, :],
                                ALU.add).then_inc(s_modb, 1)
            dve.wait_ge(s_modb, 2)
            for layer in range(2):
                for st in range(2):
                    for w in range(4):
                        m = mod_col(layer, (1, 2, 4, 5)[w], st)
                        V.scalar_tensor_tensor(out=coef[:, layer, st, w, :], in0=m, scalar=1.0 if w % 2 == 0 else 0.0,
                                               in1=gains[:, layer, w, :], op0=ALU.add, op1=ALU.mult).then_inc(s_coef, 1)
            pre_norm(0, 0)

            def value_pair(pair, col):
                dve.wait_ge(s_unit, 2 * pair + 4)
                V.tensor_copy(v[:, 2:4, bass.ds(col, 2 * P)], ps[:, 1, :].rearrange("p (t n) -> p t n", t=2))
                V.tensor_copy(v[:, 5, bass.ds(col, 2 * P)], ps[:, 2, 0:2 * P]).then_inc(s_fb, 2)
                for s in range(2):
                    lo(s, KD, 2 * pair + (s + 2))

            dve.wait_ge(s_azero, 1)
            unit_pair(0, [(apad[s][:, PAD + HT:PAD + NS], apad[s][:, AP0:AP0 + NP]) for s in range(2)])
            with dve.Fori(0, 4) as h:
                unit_pair(h + 1, [(part(qk, 2 * h + s, HT, NS - HT), part(qk, 2 * h + s, PR0, NP)) for s in range(2)])
            value_pair(5, 0)

            def head_norm(c, g):
                dve.wait_ge(s_fstd, 2 * c + 4)
                V.reciprocal(frec, fstd).then_inc(s_frec, 1)
                dve.wait_ge(s_frec, c + 2)
                dve.wait_ge(s_fro, c + 1)
                pr = part(qk, c, PR0, NP)
                V.scalar_tensor_tensor(out=fqn, in0=part(qk, c, 0, NS), scalar=g, in1=frec[:, 0:NS], op0=ALU.mult,
                                       op1=ALU.mult).then_inc(s_fn, 1)
                V.scalar_tensor_tensor(out=pr, in0=pr, scalar=g, in1=frec[:, NS:NT], op0=ALU.mult,
                                       op1=ALU.mult).then_inc(s_fn, 1)

            def rope(c, r):
                q = part(qk, c, 0, NS)
                dve.wait_ge(s_fro, r + 1)
                dve.wait_ge(s_fn, 2 * r + 2)
                dve.nop(nofuse=True)
                V.stream_shuffle(fsh, fqn, [i ^ 1 for i in range(32)]).then_inc(s_fsh, 1)
                V.tensor_tensor(ft2, fqn, cos[:, :], ALU.mult).then_inc(s_ft2, 1)
                dve.wait_ge(s_ft1, r + 1)
                dve.wait_ge(s_ft2, r + 1)
                V.tensor_tensor(q, ft1, ft2, ALU.add).then_inc(s_fro, 1)

            with dve.Fori(0, 6) as c:
                head_norm(c, gqk[:, 0:1])
                rope(c, c)
            with dve.Fori(6, 8) as c:
                head_norm(c, gqk[:, 1:2])
                rope(c, c)

            def attention(kind):
                g0, its, npair, nk = GROUPS[kind]
                nj, jb = JOBS * npair, JOBS * g0
                lat = 8 * npair
                with dve.Fori(0, its) as it:
                    ss0 = {"B": None, "C": nj * it, "D": 2 * lat * it + 2 * 20}[kind]
                    mx = 0
                    for step in range(nj + 2):
                        if step < nj:
                            job = Job(kind, step)
                            s = step % 2
                            jv = nj * it + (jb + step)
                            dve.wait_ge(s_sc, jv + 31)
                            dve.wait_ge(s_p, jv + 1)
                            scores = psf[:, 1024 * s + job.lo:1024 * s + NT]
                            negm = stat8[:, 1, s:s + 1]
                            if kind == "C":
                                m0 = job.mask_from()
                                V.scalar_tensor_tensor(out=ssb[:, s, job.lo:NT], in0=scores, scalar=SCALE,
                                                       in1=maskc[:, m0:m0 + NT - job.lo], op0=ALU.mult,
                                                       op1=ALU.add).then_inc(s_ss, 1)
                                dve.wait_ge(s_ss, nj * it + (step + 1))
                                V.tensor_reduce(stat8[:, 0, s:s + 1], ssb[:, s, job.lo:NT], AX.X,
                                                ALU.max).then_inc(s_mx, 1)
                                dve.wait_ge(s_mx, jv + 1)
                                V.tensor_scalar(negm, stat8[:, 0, s:s + 1],
                                                sink[:, bass.ds(2 * it + (job.pair + 4 * job.half), 1)], -1.0,
                                                ALU.max, ALU.mult).then_inc(s_neg, 1)
                            else:
                                if job.scaled:
                                    e = 2 * job.pair + job.half
                                    dve.wait_ge(s_e, 4 * it + (e + 1))
                                    r0 = (7 - 2 * job.t) * 64
                                    V.scalar_tensor_tensor(out=ssb[:, s, 0:NS], in0=psf[:, 1024 * s:1024 * s + NS],
                                                           scalar=SCALE, in1=erow[e][:, r0:r0 + NS], op0=ALU.mult,
                                                           op1=ALU.add).then_inc(s_ss, 1)
                                    V.tensor_scalar(ssb[:, s, NS:NT], psf[:, 1024 * s + NS:1024 * s + NT], SCALE,
                                                    None, ALU.mult).then_inc(s_ss, 1)
                                    dve.wait_ge(s_ss, 2 * lat * it + (40 + 2 * job.latent + 2))
                                    scores = ssb[:, s, :]
                                V.tensor_reduce(stat8[:, 0, s:s + 1], scores, AX.X, ALU.max).then_inc(s_mx, 1)
                                dve.wait_ge(s_mx, jv + 1)
                                V.tensor_scalar(negm, stat8[:, 0, s:s + 1], -1.0 if job.scaled else -SCALE, None,
                                                ALU.mult).then_inc(s_neg, 1)
                        if 1 <= step <= nj:
                            job = Job(kind, step - 1)
                            s = (step - 1) % 2
                            jv = nj * it + (jb + step - 1)
                            dve.wait_ge(s_p, jv + 3)
                            dve.wait_ge(s_oe, jv + 1)
                            total = stat8[:, 3, s:s + 1]
                            if kind == "C":
                                V.tensor_tensor(stat8[:, 4, s:s + 1], total, stat8[:, 2, s:s + 1],
                                                ALU.add).then_inc(s_den, 1)
                                dve.wait_ge(s_den, nj * it + step)
                                total = stat8[:, 4, s:s + 1]
                            V.reciprocal(stat8[:, 5, s:s + 1], total).then_inc(s_rinv, 1)
                            dve.wait_ge(s_pt, jv + 3)
                            dve.wait_ge(s_o, jv + 1)
                            V.tensor_copy(pts[:, s, NS:NT], ps[:, 5, 0:NP]).then_inc(s_ptb, 1)
                        if step >= 2:
                            job = Job(kind, step - 2)
                            s = step % 2
                            jv = nj * it + (jb + step - 2)
                            dve.wait_ge(s_o, jv + 3)
                            dve.wait_ge(s_rinv, jv + 3)
                            V.tensor_scalar(osb[:, job.t, bass.ds(job.head_col(it), DH)], ps[:, 6 + s, 0:DH],
                                            stat8[:, 5, s:s + 1], None, ALU.mult).then_inc(s_oe, 1)

            attention("B")

            def mix_in_lo(n, oth0, dst0):
                for c in range(n):
                    s = c % 2
                    dve.wait_ge(s_oth, oth0 + 2 * c + 2)
                    V.tensor_tensor(hl[:, dst0 + c, 0:NS], latent[s], hh[:, dst0 + c, 0:NS].bitcast(F32),
                                    ALU.subtract).then_inc(s_otl, 1)
                    V.tensor_tensor(hl[:, dst0 + c, NS:NT], context[s], hh[:, dst0 + c, NS:NT].bitcast(F32),
                                    ALU.subtract).then_inc(s_otl, 1)

            for c in range(2):
                dve.wait_ge(s_oth, c + 1)
                V.tensor_tensor(hl[:, c, :], pfo[c], hh[:, c, :].bitcast(F32), ALU.subtract).then_inc(s_otl, 1)
            mix_in_lo(6, 2, 2)

            def y_phase(phase, add):
                u0, n = UNITS[phase]
                if add:
                    dve.wait_ge(s_fa, u0 + 2)
                    dve.wait_ge(s_fb, u0 + 2)

                def f(h, s, u, split):
                    if add:
                        ya = part(y, 2 * h + s, 0, HT)
                        yb = part(y, 2 * h + s, HT, HT)
                        V.tensor_tensor(ya, bankA[s], ya, ALU.add).then_inc(s_fa, 1)
                        V.tensor_tensor(yb, bankB[s], yb, ALU.add).then_inc(s_fb, 1)
                    else:
                        copy_b([part(y, 2 * h + s, HT, HT)], s)
                    split()
                run(phase, f)

            def ffn_half(layer, half):
                f0 = 22 * layer + FH * half

                def f(h, s, u, split):
                    fp = h + f0
                    cu = 2 * h + (2 * f0 + s)
                    dve.wait_ge(s_cv, cu + 1)
                    copy_b([ub[s][:, 1 + HT:1 + NS], ub[s][:, UP0:UP0 + NP]], s)
                    split()
                    dve.wait_ge(s_c1, cu + 1)
                    V.scalar_tensor_tensor(out=cb[s], in0=ub[s][:, 0:CW], scalar=wconv[:, bass.ds(cu, 1), 0], in1=cb[s],
                                           op0=ALU.mult, op1=ALU.add).then_inc(s_c2, 1)
                    dve.wait_ge(s_c2, cu + 1)
                    V.scalar_tensor_tensor(out=cb[s], in0=ub[s][:, 2:UW], scalar=wconv[:, bass.ds(cu, 1), 2], in1=cb[s],
                                           op0=ALU.mult, op1=ALU.add).then_inc(s_cv, 1)
                    if s == 1:
                        dve.wait_ge(s_cv, cu + 3)
                        dve.wait_ge(s_sg, fp + 2)
                        dve.wait_ge(s_ffl, fp + 1)
                        V.tensor_tensor(fft[:, 0:NS], sg[:, 0:NS], cb[1][:, 0:NS], ALU.mult)
                        V.tensor_tensor(fft[:, NS:NT], sg[:, CP0:CW], cb[1][:, CP0:CW], ALU.mult).then_inc(s_ffm, 1)
                        dve.wait_ge(s_ffh, fp + 1)
                        V.tensor_tensor(chunk(ffl, h), fft, chunk(ffh, h).bitcast(F32), ALU.subtract).then_inc(s_ffl, 1)
                run((layer, f"fin{half}"), f)

            def ffn(layer):
                dve.wait_ge(s_hl, 8 * (2 * layer + 2) + 2)
                for s in range(2):
                    for f, n in ((0, 1), (1 + NS, 2), (UW - 1, 1)):
                        V.memset(ub[s][:, f:f + n], 0.0).then_inc(s_uzero, 1)
                dve.wait_ge(s_uzero, 6 * (layer + 1))
                dve.wait_ge(s_out, 32 * (layer + 1))
                ffn_half(layer, 0)
                y_phase((layer, "fout0"), False)
                ffn_half(layer, 1)
                y_phase((layer, "fout1"), True)

            y_phase((0, "mix"), False)
            post_norm(0, 1)
            pre_norm(0, 2)
            ffn(0)
            post_norm(0, 3)
            pre_norm(1, 0)
            p1 = UNITS[(1, "in")][0] // 2
            with dve.Fori(0, 6) as h:
                unit_pair(h + p1, [(part(qk, 2 * h + s, HT, NS - HT), part(qk, 2 * h + s, PR0, NP)) for s in range(2)])
            dve.wait_ge(s_unit, 2 * p1 + 12 + 3)
            copy_b((qk[:, 12, HT:NS], qk[:, 12, PR0:PR0 + NP]), 0)
            lo(0, KD, 2 * p1 + 14)
            dve.wait_ge(s_unit, 2 * p1 + 13 + 3)
            V.tensor_copy(v[:, 5, 0:P], context[1]).then_inc(s_fb, 1)
            lo(1, KD, 2 * p1 + 15)
            with dve.Fori(0, 2) as h:
                value_pair(h + (p1 + 7), 256 * h + P)
            u1 = UNITS[(1, "mix")][0]
            dve.wait_ge(s_fa, u1 + 2)
            dve.wait_ge(s_fb, u1 + 2)
            def rope_plain(c, r):
                dve.wait_ge(s_fro, r + 1)
                V.tensor_copy(fqn, part(qk, c, 0, NS)).then_inc(s_fn, 2)
                rope(c, r)

            with dve.Fori(0, 4) as c:
                rope_plain(c, c + 8)
            rope_plain(12, 12)
            attention("C")
            attention("D")
            mix_in_lo(8, 14, 0)
            y_phase((1, "mix"), False)
            post_norm(1, 1)
            pre_norm(1, 2)
            ffn(1)
            post_norm(1, 3)

        @block.gpsimd
        def _(pool):
            G = nc.gpsimd

            def scale_rows(n, src):
                pool.wait_ge(s_rec, n + 1)
                with pool.Fori(0, KD // 2) as h:
                    for s in range(2):
                        pool.wait_ge(s_tu, 2 * h + (8 * n + s + 1))
                        G.tensor_tensor(tn[s], chunk(src, 2 * h + s), rec, ALU.mult).then_inc(s_t, 1)

            def rope_sin(n, r0):
                with pool.Fori(r0, r0 + n) as r:
                    pool.wait_ge(s_fsh, r + 1)
                    G.tensor_tensor(ft1, fsh, sin[:, :], ALU.mult).then_inc(s_ft1, 1)

            def stage(kind, it, i):
                g0, its, npair, nk = GROUPS[kind]
                g = npair * it + (g0 + i)
                qc = {"B": 3 * it + i, "C": 2 * it + i, "D": 2 * it + (4 + i)}[kind]
                kc = {"B": it + 6, "C": 12, "D": 2 * it + (8 + i)}[kind]
                back = i if (kind == "B" and i == 0) else npair
                if kind == "B" and i == 0:
                    pool.wait_ge(s_sc, JOBS * 3 * it + 30)
                else:
                    pool.wait_ge(s_sc, JOBS * npair * it + (JOBS * (g0 + i - npair + 1) + 30))
                for f, src, w in ((0, 0, NS), (NS, PR0, NP)):
                    last = G.tensor_copy(qs[:, i, f:f + w], part(qk, qc, src, w))
                    if f == 0:
                        last.then_inc(s_stage, 1)
                if (kind == "B" and i == 0) or kind == "D":
                    last.then_inc(s_stage, 1)
                    G.tensor_copy(ks[:, i if kind == "D" else 0, :], chunk(qk, kc)).then_inc(s_stage, 1)
                else:
                    last.then_inc(s_stage, 2)

            scale_rows(0, x)
            pool.wait_ge(s_hl, 8 + 2)
            G.memset(work[:, 0:2 * AW], 0.0).then_inc(s_azero, 1)
            for c in range(2):
                pool.dma_start(icnt[c], a["icnt"][c]).then_inc(s_icnt, 16)
            pool.wait_ge(s_icnt, 32)
            steps = [0]

            def step(ins):
                steps[0] += 1
                ins.then_inc(s_pool, 1)
                pool.wait_ge(s_pool, steps[0])

            for c in range(2):
                pool.wait_ge(s_fa, c + 3)
                pool.wait_ge(s_fb, c + 3)
                t0, t1 = ptmp
                step(G.tensor_tensor(t0[:, 1:AW], apad[c][:, 0:AW - 1], apad[c][:, 1:AW], ALU.add))
                if c == 1:
                    step(G.tensor_tensor(t1[:, 2:AW - 1], t0[:, 1:AW - 2], t0[:, 3:AW], ALU.add))
                    step(G.tensor_tensor(t0[:, 4:AW - 3], t1[:, 2:AW - 5], t1[:, 6:AW - 1], ALU.add))
                w = 1 << (2 * c)
                lo_edge, hi_edge = 2 * w, AW - 2 * w + 1
                step(G.tensor_tensor(t1[64:P, lo_edge:hi_edge], t0[64:P, lo_edge - w:hi_edge - w],
                                     t0[64:P, lo_edge + w:hi_edge + w], ALU.add))
                for f, src, n in ((0, PAD, NS), (NS, AP0, NP)):
                    for rows, t in ((slice(0, 64), t0), (slice(64, P), t1)):
                        step(G.tensor_tensor(icnt[c][rows, f:f + n], t[rows, src:src + n], icnt[c][rows, f:f + n],
                                             ALU.mult))
                    step(G.tensor_tensor(icnt[c][:, f:f + n], icnt[c][:, f:f + n], apad[c][:, src:src + n],
                                         ALU.subtract))
            assert steps[0] == POOL_STEPS
            rope_sin(8, 0)
            pool.wait_ge(s_fro, 8 + 1)
            pool.wait_ge(s_fn, 16)
            pool.wait_ge(s_fa, 12 + 2)
            pool.wait_ge(s_fb, 12 + 2)
            pool.wait_ge(s_ctx, 32)
            pool.dma_start(o["k0"], qk[:, 6:8, PR0:PR0 + NP]).then_inc(s_out, 16)
            pool.dma_start(o["v0"], v[:, 5, 0:2 * P]).then_inc(s_out, 16)
            with pool.Fori(0, 2) as it:
                for i in range(3):
                    stage("B", it, i)
            scale_rows(1, y)
            scale_rows(2, x)
            scale_rows(3, y)
            scale_rows(4, x)
            pool.wait_ge(s_unit, UNITS[(1, "in")][0] + 2)
            pool.dma_start(qk[:, 8:13, CTX0:PR0], a["kctx1"]).then_inc(s_ctx1, 16)
            pool.dma_start(v[:, 4, :], a["vctx1"]).then_inc(s_ctx1, 16)
            pool.wait_ge(s_hl, 24 + 2)

            def load_bias(e, head):
                pool.dma_start(erow[e], a["rpb"][head]).then_inc(s_eload[e], 16)

            def mask_bias(e, n):
                pool.wait_ge(s_eload[e], 16 * n)
                r = erow[e].rearrange("p (r c) -> p r c", c=64)
                G.tensor_tensor(r, r, maskd[:, :].unsqueeze(1).to_broadcast([P, 15, 64]), ALU.add).then_inc(s_e, 1)

            for e in range(4):
                load_bias(e, e)
            rope_sin(5, 8)
            u1 = UNITS[(1, "mix")][0]
            pool.wait_ge(s_fro, 13 + 1)
            pool.wait_ge(s_fa, u1 + 2)
            pool.wait_ge(s_fb, u1 + 2)
            pool.wait_ge(s_ctx1, 32)
            pool.dma_start(o["k1"], qk[:, 8:13, PR0:PR0 + NP]).then_inc(s_out, 16)
            pool.dma_start(o["v1"], v[:, 5, :]).then_inc(s_out, 16)
            pool.wait_ge(s_sc, JOBS * 6 + 30)
            G.tensor_copy(ks[:, 0, :], qk[:, 12, :]).then_inc(s_stage, 1)
            for e in range(4):
                mask_bias(e, 1)
            with pool.Fori(0, 2) as it:
                for i in range(2):
                    stage("C", it, i)
            pool.wait_ge(s_sc, JOBS * 10 + 30)
            for i in range(2):
                stage("D", 0, i)
            for i in range(2):
                pool.wait_ge(s_neg, JOBS * (10 + i + 1))
                for half in range(2):
                    load_bias(2 * i + half, 4 + 2 * i + half)
                stage("D", 1, i)
                for half in range(2):
                    mask_bias(2 * i + half, 2)
            scale_rows(5, y)
            scale_rows(6, x)
            scale_rows(7, y)

        @block.tensor
        def _(pe):
            T = nc.tensor
            for s, credit in ((s_unit, 2), (s_fa, 2), (s_fb, 2), (s_mod, 4), (s_stat, 2), (s_tu, 2), (s_hl, 2),
                              (s_fst, 2), (s_fstd, 2), (s_frec, 1), (s_fro, 1), (s_sc, 30), (s_p, 2), (s_pt, 2),
                              (s_pta, 1), (s_ptb, 1), (s_o, 2), (s_rinv, 2), (s_oe, 2), (s_cv, 2), (s_sg, 1),
                              (s_ffm, 1), (s_ffl, 1)):
                pe.sem_inc(s, credit)

            def unit(s, u, kk, hi, lo):
                pe.wait_ge(s_lo, u + 1)
                pe.wait_ge(s_fa, u + 1)
                pe.wait_ge(s_fb, u + 1)
                for k in range(kk):
                    for n, (w, h) in enumerate(((whi, hi), (whi, lo), (wlo, hi))):
                        st, sp_ = k == 0 and n == 0, k == kk - 1 and n == 2
                        T.matmul(bankA[s], slot(w, s, k), h[:, k, 0:HT], start=st, stop=sp_)
                        last = T.matmul(bankB[s], slot(w, s, k), h[:, k, HT:NT], start=st, stop=sp_)
                last.then_inc(s_unit, 1)

            def unit_v(s, u):
                pe.wait_ge(s_lo, u + 1)
                pe.wait_ge(s_fa, u + 1)
                pe.wait_ge(s_fb, u + 1)
                for t in range(5):
                    out = latent[s][:, t * P:(t + 1) * P] if t < 4 else context[s]
                    for k in range(KD):
                        for n, (w, h) in enumerate(((whi, hh), (whi, hl), (wlo, hh))):
                            last = T.matmul(out, h[:, k, t * P:(t + 1) * P], slot(w, s, k),
                                            start=k == 0 and n == 0, stop=k == KD - 1 and n == 2)
                last.then_inc(s_unit, 1)

            def pair_v(u):
                pe.wait_ge(s_lo, u + 2)
                pe.wait_ge(s_fa, u + 2)
                pe.wait_ge(s_fb, u + 2)
                for t in range(5):
                    out = ps[:, t // 2, t % 2 * 2 * P:(t % 2 + 1) * 2 * P].rearrange("p (a n) -> p a n", a=2)
                    for k in range(KD):
                        for n, (w, h) in enumerate(((whi, hh), (whi, hl), (wlo, hh))):
                            last = T.matmul(out, h[:, k, t * P:(t + 1) * P], w[:, :, k * P:(k + 1) * P],
                                            start=k == 0 and n == 0, stop=k == KD - 1 and n == 2)
                last.then_inc(s_unit, 2)

            def dense(s, u):
                unit(s, u, KD, hh, hl)

            def stat(n, k, s):
                first, last = (k == 0, k == KD - 1) if isinstance(k, int) else (False, False)
                if first and n:
                    pe.wait_ge(s_std, 2 * n)
                pe.wait_ge(s_sq, k + (8 * n + 1))
                T.matmul(statA, onesd[:, :], sq[s][:, 0:HT], start=first, stop=last)
                T.matmul(statB, onesd[:, :], sq[s][:, HT:NT], start=first, stop=last).then_inc(s_stat, 1)

            pe.wait_ge(s_csilu, 1)
            with pe.Fori(0, 24) as it:
                for s in range(4):
                    pe.wait_ge(s_mraw[s], 16 * it + 16)
                    for k in range(KD):
                        last = T.matmul(ps[:, 4, bass.ds(8 * it + 2 * s, 2)], mraw[s][:, k * P:(k + 1) * P],
                                        csilu[:, 2 * k:2 * k + 2], start=k == 0, stop=k == KD - 1)
                    last.then_inc(s_mod, 1)
            pe.wait_ge(s_const, 16 * n_const)
            for k in range(KD):
                stat(0, k, k % 2)

            def dense_pairs(u0, n):
                with pe.Fori(0, n) as h:
                    for s in range(2):
                        dense(s, 2 * h + (u0 + s))

            pe.wait_ge(s_hl, 8 + 2)
            dense_pairs(0, 5)
            pair_v(10)
            with pe.Fori(0, 4) as h:
                for s in range(2):
                    c = 2 * h + s
                    pe.wait_ge(s_fsq, 2 * c + 2)
                    pe.wait_ge(s_fstd, 2 * c + 2)
                    T.matmul(statA, onesh[:, :], fsq[s][:, 0:HT], start=True, stop=True)
                    T.matmul(statB, onesh[:, :], fsq[s][:, HT:NT], start=True, stop=True).then_inc(s_fst, 1)

            def attention(kind):
                g0, its, npair, nk = GROUPS[kind]
                nj, jb = JOBS * npair, JOBS * g0
                lat = 8 * npair
                st0 = {"B": 0, "C": 18 + 1, "D": 18 + 1 + 12}[kind]
                with pe.Fori(0, its) as it:
                    for step in range(-1, nj + 1):
                        if step + 1 < nj:
                            job = Job(kind, step + 1)
                            s = (step + 1) % 2
                            jv = nj * it + (jb + step + 1)
                            if (step + 1) % JOBS == 0:
                                pe.wait_ge(s_stage, 3 * npair * it + (st0 + 3 * job.pair + 3))
                            pe.wait_ge(s_p, jv + 1)
                            kslot = job.pair if kind == "D" else 0
                            q = qs[job.rows, job.pair, job.q0:job.q0 + P]
                            if not job.prompt:
                                k0 = job.tiles[0] * P
                                T.matmul(psf[:, 1024 * s + job.lo:1024 * s + NS], q,
                                         ks[job.rows, kslot, k0:k0 + NS - job.lo], start=True, stop=True)
                            T.matmul(psf[:, 1024 * s + NS:1024 * s + NT], q,
                                     ks[job.rows, kslot, job.kctx:job.kctx + P], start=True, stop=True
                                     ).then_inc(s_sc, 1)
                        if 0 <= step < nj:
                            job = Job(kind, step)
                            s = step % 2
                            jv = nj * it + (jb + step)
                            pe.wait_ge(s_p, jv + 3)
                            pe.wait_ge(s_ptb, jv + 1)
                            if not job.prompt:
                                pe.wait_ge(s_pta, lat * it + (8 * g0 + job.latent + 1))
                                for c in range(job.lo, NS, P):
                                    T.transpose(ps[:, 4, c:c + P], pb[:, s, c:c + P], ident[:, :])
                            T.transpose(ps[:, 5, 0:P], pb[:, s, NS:NT], ident[:, :]).then_inc(s_pt, 1)
                        if step >= 1:
                            job = Job(kind, step - 1)
                            s = (step - 1) % 2
                            jv = nj * it + (jb + step - 1)
                            pe.wait_ge(s_ptb, jv + 2)
                            if not job.prompt:
                                pe.wait_ge(s_pta, lat * it + (8 * g0 + job.latent + 2))
                            pe.wait_ge(s_oe, jv + 1)
                            keys = [(job.lo + P * i, t) for i, t in enumerate(job.tiles)] + [(NS, job.vctx)]
                            for i, (c, t) in enumerate(keys):
                                last = T.matmul(ps[:, 6 + s, 0:DH], pts[:, s, c:c + P],
                                                v[:, t, bass.ds(job.v_col(it), DH)], start=i == 0,
                                                stop=i == len(keys) - 1)
                            last.then_inc(s_o, 1)

            attention("B")

            def turn(n, e0, otl0, chunk0):
                for c in range(n):
                    s = c % 2
                    if c >= 2:
                        pe.wait_ge(s_otl, otl0 + 2 * (c - 1) + 2)
                    for t in range(5):
                        out = latent[s][:, t * P:(t + 1) * P] if t < 4 else context[s]
                        last = T.transpose(out, osb[:, t, c * P:(c + 1) * P], ident[:, :])
                    last.then_inc(s_otp, 1)

            pe.wait_ge(s_pool, POOL_STEPS)
            for c in range(2):
                T.matmul(latent[c], wpool[:, c, :], icnt[c][:, 0:NS], start=True, stop=True)
                T.matmul(context[c], wpool[:, c, :], icnt[c][:, NS:NT], start=True, stop=True).then_inc(s_otp, 1)
            pe.wait_ge(s_oe, 60 + 2)
            pe.wait_ge(s_pf, 4)
            turn(6, 2, 0 + 2, 2)

            def y_units(phase, n):
                u0, _ = UNITS[phase]

                def one(h, s):
                    if phase[1] == "mix":
                        dense(s, 2 * h + (u0 + s))
                    else:
                        unit(s, 2 * h + (u0 + s), FH, ffh, ffl)

                one(0, 0)
                one(0, 1)
                stat(n, 0, 0)
                with pe.Fori(1, 3) as h:
                    one(h, 0)
                    stat(n, 2 * h - 1, 1)
                    one(h, 1)
                    stat(n, 2 * h, 0)
                one(3, 0)
                stat(n, 5, 1)
                one(3, 1)
                stat(n, 6, 0)
                stat(n, 7, 1)

            def ffn(layer):
                pe.wait_ge(s_hl, 8 * (2 * layer + 2) + 2)
                for half in range(2):
                    dense_pairs(UNITS[(layer, f"fin{half}")][0], FH)
                    f0 = 22 * layer + FH * half
                    pe.wait_ge(s_ffl, f0 + FH + 1)
                    if half == 0:
                        u0, n = UNITS[(layer, "fout0")]
                        with pe.Fori(0, n // 2) as h:
                            for s in range(2):
                                unit(s, 2 * h + (u0 + s), FH, ffh, ffl)
                    else:
                        y_units((layer, "fout1"), norm_index(layer, 3))

            def stats(n):
                for k in range(KD):
                    stat(n, k, k % 2)

            pe.wait_ge(s_otl, 14 + 2 - 2)
            y_units((0, "mix"), 1)
            stats(2)
            ffn(0)
            stats(4)
            pe.wait_ge(s_hl, 24 + 2)
            u1 = UNITS[(1, "in")][0]
            dense_pairs(u1, 6)
            dense(0, u1 + 12)
            unit_v(1, u1 + 13)
            with pe.Fori(0, 2) as h:
                pair_v(2 * h + (u1 + 14))
            attention("C")
            attention("D")
            pe.wait_ge(s_oe, 140 + 2)
            turn(8, 8, 14, 0)
            pe.wait_ge(s_otl, 30)
            y_units((1, "mix"), 5)
            stats(6)
            ffn(1)


def kernel(x_prompt, x_sample, cache_b_k, cache_b_v, cache_c_k, cache_c_v, cache_d_k, cache_d_v,
           c, c_ctx, w_mod, b_mod, g_mix_pre, g_mix_post, g_ffn_pre, g_ffn_post,
           w_in_even, w_pool, pool_scale, g_q_b, g_k_b, w_in_odd, sink_c, rpb_d,
           w_mix_out, w_ffn_in, w_ffn_conv, w_ffn_out):
    import numpy as np
    import concourse.bacc as bacc
    from concourse.bass_utils import run_bass_kernel_spmd as run

    (x_prompt, x_sample, cache_b_k, cache_b_v, cache_c_k, cache_c_v, cache_d_k, cache_d_v, c, c_ctx, w_mod, b_mod,
     g_mix_pre, g_mix_post, g_ffn_pre, g_ffn_post, w_in_even, w_pool, pool_scale, g_q_b, g_k_b, w_in_odd, sink_c,
     rpb_d, w_mix_out, w_ffn_in, w_ffn_conv, w_ffn_out) = map(np.asarray, (
         x_prompt, x_sample, cache_b_k, cache_b_v, cache_c_k, cache_c_v, cache_d_k, cache_d_v, c, c_ctx, w_mod, b_mod,
         g_mix_pre, g_mix_post, g_ffn_pre, g_ffn_post, w_in_even, w_pool, pool_scale, g_q_b, g_k_b, w_in_odd, sink_c,
         rpb_d, w_mix_out, w_ffn_in, w_ffn_conv, w_ffn_out))

    def units(w):
        k, n = w.shape
        return w.reshape(k // P, P, n // P, P).transpose(2, 1, 0, 3).reshape(n // P, P, k)

    def feature_major(t):
        return t.T.reshape(-1, P, t.shape[0]).transpose(1, 0, 2)

    def cols(vec):
        return vec.reshape(-1, P).T

    order = [0, 3, 1, 4, 2, 5, 6, 9, 7, 10, 8, 11]
    e = w_in_even[0]
    q = e[:, 256:1024].reshape(D, 12, DH)[:, order].reshape(D, 768)
    even = np.concatenate([e[:, 0:256], q, e[:, 1024:]], axis=1)
    w = w_in_odd[0]
    qc, kc, vc, qd, kd, vd = (w[:, i:j] for i, j in ((0, 512), (512, 640), (640, 768), (768, 1280), (1280, 1792),
                                                     (1792, 2304)))
    qc = qc.reshape(D, 8, DH)[:, [0, 4, 1, 5, 2, 6, 3, 7]].reshape(D, 512)
    odd = np.concatenate([qc, qd, kd, kc, vc, vd], axis=1)
    w8, w11, conv = [], [], []
    for layer, w_in in ((0, even), (1, odd)):
        gate_val = units(w_ffn_in[layer])
        gv = np.stack([gate_val[0:22], gate_val[22:44]], axis=1).reshape(44, P, D)
        down = w_ffn_out[layer].reshape(2, FH * P, D)
        w8 += [units(w_in), units(w_mix_out[layer]), gv]
        w11 += [units(down[0]), units(down[1])]
        taps = w_ffn_conv[layer].reshape(3, 2, 22, P).transpose(3, 2, 1, 0)
        conv.append(taps.reshape(P, 44, 3))

    t = np.arange(NS)
    inv_freq = 10000.0 ** (-np.arange(0, 32, 2) / 32.0)
    ang = np.concatenate([(t // 64)[:, None] * inv_freq, (t % 64)[:, None] * inv_freq], axis=-1)
    feat = np.arange(P) % DH // 2
    cos_t = np.cos(ang)[:, feat].T
    sin_t = np.sin(ang)[:, feat].T * np.where(np.arange(P) % 2 == 0, -1.0, 1.0)[:, None]
    low = -1e30
    i, j = np.arange(P)[:, None], np.arange(P)[None, :]
    before, after, zero = np.where(j >= i, 0.0, low), np.where(j <= i, 0.0, low), np.zeros((P, P))
    maskc_t = np.concatenate([before, zero, after, zero, before, zero, zero], axis=1)
    qcol, kcol = (np.arange(P) % 64)[:, None], np.arange(64)[None, :]
    start = np.clip(qcol - 8, 0, 48)
    maskd_t = np.where((kcol >= start) & (kcol < start + 16), 0.0, low)
    counts = np.zeros((2, P, NT))
    for g, win in enumerate((2, 4, 8, 16)):
        for f, n in ((0, NS), (NS, NP)):
            tt = np.arange(n)
            cnt = np.clip(tt - win // 2 + win, 0, n) - np.clip(tt - win // 2, 0, n)
            counts[g // 2, 64 * (g % 2):64 * (g % 2) + 64, f:f + n] = 1.0 / cnt
    half = np.arange(P) // 64

    padded = np.zeros((8, 17, 31 + 96), np.float32)
    padded[:, 1:16, 48:79] = rpb_d[0]
    qp = np.arange(P)
    row = 1 + np.arange(15)[None, :, None] - (qp // 64)[:, None, None]
    off = np.arange(64)[None, None, :] - (qp % 64)[:, None, None] + 15 + 48
    rpb_rows = padded[:, row, off].reshape(8, P, RPB)

    wp = np.zeros((P, 2, P), np.float32)
    for g in range(4):
        r = 64 * (g % 2)
        wp[r:r + 64, g // 2, r:r + 64] = w_pool[0, g]
    small_in = np.concatenate([cols(pool_scale[0]), np.tile(g_q_b[0], 2)[:, None], np.tile(g_k_b[0], 2)[:, None],
                               np.broadcast_to(sink_c[0], (P, 8))], axis=1)
    gains_in = np.stack([np.stack([cols(g[layer]) for g in (g_mix_pre, g_mix_post, g_ffn_pre, g_ffn_post)], axis=1)
                         for layer in range(2)], axis=1)
    tokens = np.concatenate([x_sample[0], x_prompt[0]], axis=0)
    odd_k = np.concatenate([cache_d_k[0, 0].reshape(NP, 512), cache_c_k[0, 0].reshape(NP, 128)], axis=1)
    odd_v = np.concatenate([cache_c_v[0, 0].reshape(NP, 128), cache_d_v[0, 0].reshape(NP, 512)], axis=1)
    arrays = {
        "x": feature_major(tokens).reshape(P, KD * NT),
        "w8": np.concatenate(w8, axis=0), "w11": np.concatenate(w11, axis=0),
        "wmod": np.concatenate([units(w_mod[0]), units(w_mod[1])], axis=0),
        "bmod": np.concatenate([cols(b_mod[0]), cols(b_mod[1])], axis=1),
        "cvec": np.stack([cols(c[0]), cols(c_ctx)], axis=2).reshape(P, 2 * KD),
        "gains": gains_in, "small": small_in, "wpool": wp, "wconv": np.concatenate(conv, axis=1),
        "kctx0": feature_major(cache_b_k[0, 0].reshape(NP, 256)), "vctx0": cache_b_v[0, 0].reshape(NP, 256),
        "kctx1": feature_major(odd_k), "vctx1": odd_v, "rpb": rpb_rows,
        "cos": cos_t, "sin": sin_t, "maskc": maskc_t, "maskd": maskd_t, "icnt": counts, "ident": np.eye(P),
        "onesd": np.full((P, P), 1.0 / D), "onesh": (half[:, None] == half[None, :]) / 64.0,
    }
    arrays = {n: np.ascontiguousarray(t, dtype=np.float32) for n, t in arrays.items()}
    shapes = {"x": (P, KD * NT), "k0": (P, 2, NP), "v0": (P, 256), "k1": (P, 5, NP), "v1": (P, NT)}

    nc = bacc.Bacc("TRN2", target_bir_lowering=False, num_devices=1)
    ins = {n: nc.dram_tensor(f"in_{n}", t.shape, F32, kind="ExternalInput").ap() for n, t in arrays.items()}
    outs = {n: nc.dram_tensor(f"out_{n}", s, F32, kind="ExternalOutput").ap() for n, s in shapes.items()}
    program(nc, ins, outs)
    r = run(nc, [{f"in_{n}": t for n, t in arrays.items()}], core_ids=[0]).results[0]

    def token_major(t):
        return t.transpose(2, 1, 0).reshape(t.shape[2], -1)

    xo = token_major(r["out_x"].reshape(P, KD, NT))
    k0, v0 = token_major(r["out_k0"]), r["out_v0"]
    k1, v1 = token_major(r["out_k1"]), r["out_v1"]
    return (xo[NS:][None], xo[:NS][None],
            k0.reshape(1, 1, NP, 4, DH), v0.reshape(1, 1, NP, 4, DH),
            k1[:, 512:].reshape(1, 1, NP, 2, DH), v1[:, :128].reshape(1, 1, NP, 2, DH),
            k1[:, :512].reshape(1, 1, NP, 8, DH), v1[:, 128:].reshape(1, 1, NP, 8, DH))
```

```python
from contextlib import ExitStack

import concourse.bass as bass
from concourse import mybir
from concourse.alu_op_type import AluOpType as ALU

F32 = mybir.dt.float32
F32R = mybir.dt.float32r
ACT = mybir.ActivationFunctionType
AX = mybir.AxisListType

P = 128
D = 1024
KD = D // P
NS = 512
NP = 128
NT = NS + NP
HT = NT // 2
DH = 64
SCALE = DH ** -0.5
EPS = 1e-6
FH = 11
PAD = 8
AW = PAD + NS + 2 * PAD + NP + PAD
AP0 = PAD + NS + 2 * PAD
UW = 1 + NS + 2 + NP + 1
UP0 = 1 + NS + 2
CW = UW - 2
CP0 = UP0 - 1
SLOT = FH * P
CTX0, PR0 = NS, NS + NP
POOL_STEPS = 18
RPB = 15 * 64

UNITS = {}
NU = 0
for _l, _in in ((0, 12), (1, 18)):
    for _kind, _count in (("in", _in), ("mix", 8), ("fin0", 22), ("fout0", 8), ("fin1", 22), ("fout1", 8)):
        UNITS[(_l, _kind)] = (NU, _count)
        NU += _count
PHASES = list(UNITS)
RUNS = [(8, 42), (FH, 8), (8, 22), (FH, 8), (8, 48), (FH, 8), (8, 22), (FH, 8)]
GROUPS = {"B": (0, 3, 4), "C": (6, 2, 54), "D": (10, 2, 86)}
JOBS = 10


class Job:

    def __init__(self, kind, step):
        self.kind, self.pair, self.half = kind, step // JOBS, step % 2
        self.t = step % JOBS // 2
        self.prompt = self.t == 4
        near = (max(self.t - 1, 0), min(self.t + 1, 3)) if kind == "C" else (0, 3)
        self.tiles = [] if self.prompt else list(range(near[0], near[1] + 1))
        self.lo = NS - P * len(self.tiles)
        self.scaled = kind != "B"
        self.split = kind != "C" and not self.prompt
        self.q0 = P * self.t
        self.vctx = 5 if self.prompt else 4
        self.kctx = PR0 if self.prompt else CTX0
        self.latent = 8 * self.pair + min(step % JOBS, 8)

    def head_col(self, it):
        if self.kind == "B":
            return DH * it + DH * (6 * self.pair + 3 * self.half)
        if self.kind == "C":
            return DH * 2 * it + DH * (self.pair + 4 * self.half)
        return 4 * DH * it + (512 + DH * (2 * self.pair + self.half))

    def v_col(self, it):
        if self.kind == "B":
            return 0 * it + P * self.pair + DH * self.half
        if self.kind == "C":
            return DH * self.half
        return 4 * DH * it + (P + DH * (2 * self.pair + self.half))

    def mask_from(self):
        return {0: P, 1: 0, 2: 0, 3: 4 * P, 4: 3 * P}[self.t]


def kchunks(phase):
    return FH if phase[1].startswith("fout") else KD


def program(nc, a, o):
    with ExitStack() as ctx:
        place = [16512]

        def at(name, shape, dt, byte):
            return nc.alloc_sbuf_tensor_at(name, shape, dt, offset=byte)

        def sb(name, shape, dt=F32):
            n = 4
            for s in shape[1:]:
                n *= s
            t = at(name, shape, dt, place[0])
            place[0] += (n + 31) // 32 * 32
            return t

        def sem(name):
            return ctx.enter_context(nc.semaphore(name))

        x = sb("x", [P, KD, NT])
        y = sb("y", [P, KD, NT])
        raw = sb("raw", [P, 2, SLOT])
        whi = sb("whi", [P, 2, SLOT], F32R)
        wlo = sb("wlo", [P, 2, SLOT], F32R)
        region_h = place[0]
        hh = sb("hh", [P, KD, NT], F32R)
        hl = sb("hl", [P, KD, NT], F32R)
        region_f = place[0]
        ffh = sb("ffh", [P, FH, NT], F32R)
        ffl = sb("ffl", [P, FH, NT], F32R)
        work = sb("work", [P, 5248])
        cos = sb("cos", [P, NS])
        sin = sb("sin", [P, NS])
        maskc = sb("maskc", [P, 7 * P])
        maskd = sb("maskd", [P, 64])
        ident = sb("ident", [P, P])
        onesd = sb("onesd", [P, P])
        onesh = sb("onesh", [P, P])
        wpool = sb("wpool", [P, 2, P])
        wconv = sb("wconv", [P, 88, 3])
        cvec = sb("cvec", [P, 2 * KD])
        csilu = sb("csilu", [P, 2 * KD])
        cst = sb("cst", [P, KD, 4], F32R)
        sel = sb("sel", [4, 2])
        bmod = sb("bmod", [P, 96])
        mod = sb("mod", [P, 2, 96, ])
        gains = sb("gains", [P, 2, 4, KD])
        coef = sb("coef", [P, 2, 2, 4, KD])
        small = sb("small", [P, 2 + 2 + 8])
        pscale = small[:, 0:2]
        gqk = small[:, 2:4]
        sink = small[:, 4:12]
        pb4 = sb("pb4", [P, NT])
        stat8 = sb("stat8", [P, 7, 2])
        assert place[0] <= 229368, place[0]
        pos = [region_h]

        def over(name, shape, dt=F32):
            n = 4
            for s in shape[1:]:
                n *= s
            t = at(name, shape, dt, pos[0])
            pos[0] += n
            return t
        qh = over("qh", [P, 2, 2, NT], F32R)
        ql = over("ql", [P, 2, 2, NT], F32R)
        kh = over("kh", [P, 2, 6 * P], F32R)
        kl = over("kl", [P, 2, 6 * P], F32R)
        pb3 = over("pb3", [P, 3, NT])
        pb = [pb3[:, 0, :], pb3[:, 1, :], pb3[:, 2, :], pb4[:, :]]
        assert pos[0] <= region_f
        pos[0] = region_h
        mh = over("mh", [P, 2, 1024], F32R)
        ml = over("ml", [P, 2, 1024], F32R)
        pos[0] = region_f
        qk = over("qk", [P, 13, 6 * P])
        v = over("v", [P, 6, NT])
        assert pos[0] <= region_f + 2 * FH * NT * 4
        osb = y[:, :, :].rearrange("p k n -> p (k n)").rearrange("p (t d) -> p t d", t=5)
        yf = y[:, :, :].rearrange("p k n -> p (k n)")

        def ring(base, n, width, where=work):
            return [where[:, base + i * width:base + (i + 1) * width] for i in range(n)]
        sq = ring(0, 2, NT)
        tn = ring(1280, 2, NT)
        hf = ring(2560, 2, NT)
        std = work[:, 3840:4480]
        rec = work[:, 4480:5120]
        ub = ring(0, 2, UW)
        cb = ring(2 * UW, 2, CW)
        sg = work[:, 2 * UW + 2 * CW:2 * UW + 3 * CW]
        fft = work[:, 2 * UW + 3 * CW:2 * UW + 3 * CW + NT]
        mraw = [work[:, i * 1024:(i + 1) * 1024] for i in range(4)]
        apad = ring(0, 2, AW)
        ptmp = ring(2 * AW, 2, AW)
        pfo = [work[:, i * AW:i * AW + NT] for i in range(2)]
        icnt = ring(4 * AW, 2, NT)
        erow = ring(0, 4, RPB)
        pts = work[:, 3968:5248].rearrange("p (s n) -> p s n", s=2)
        mrow = [yf[0:4, i * 512:(i + 1) * 512] for i in range(2)]
        fsq = [yf[:, i * NT:(i + 1) * NT] for i in range(2)]
        fstd = yf[:, 1280:1920]
        frec = yf[:, 1920:2560]
        fsh = yf[:, 2560:3072]
        ft1 = yf[:, 3072:3584]
        ft2 = yf[:, 3584:4096]
        fqn = yf[:, 4096:4608]

        ps = ctx.enter_context(nc.psum_tensor("ps", [P, 8, 512], F32))
        psf = ps[:, :, :].rearrange("p b n -> p (b n)")
        bankA = [ps[:, 0, 0:HT], ps[:, 2, 0:HT]]
        bankB = [ps[:, 1, 0:HT], ps[:, 3, 0:HT]]
        latent = [ps[:, 0, :], ps[:, 2, :]]
        context = [ps[:, 1, 0:NP], ps[:, 3, 0:NP]]
        statA, statB = ps[:, 5, 0:HT], ps[:, 6, 0:HT]

        s_raw = [sem("weights_loaded_0"), sem("weights_loaded_1")]
        s_hi = sem("weights_hi")
        s_lo = sem("weights_lo")
        s_unit = sem("unit_multiplied")
        s_fa = sem("first_half_read")
        s_fb = sem("second_half_read")
        s_const = sem("constants_loaded")
        s_ctx = sem("cached_context_loaded")
        s_ctx1 = sem("cached_context_1_loaded")
        s_cvec = sem("c_loaded")
        s_x = sem("x_loaded")
        s_azero = sem("pool_pads_zeroed")
        s_uzero = sem("conv_pads_zeroed")
        s_csilu = sem("c_activated")
        s_mraw = [sem(f"mod_weights_loaded_{i}") for i in range(4)]
        s_cst = sem("c_split")
        s_mhi = sem("mod_weights_hi")
        s_mlo = sem("mod_weights_lo")
        s_mod = sem("mod_multiplied")
        s_mrow = sem("mod_rows_copied")
        s_mt = sem("mod_rows_turned")
        s_modb = sem("mod_biased")
        s_coef = sem("coefficients_ready")
        s_sq = sem("square_ready")
        s_stat = sem("square_summed")
        s_std = sem("deviation_ready")
        s_rec = sem("reciprocal_ready")
        s_t = sem("normed_ready")
        s_tu = sem("normed_used")
        s_hh = sem("h_hi")
        s_hl = sem("h_lo")
        s_pool = sem("pool_step")
        s_icnt = sem("pool_counts_loaded")
        s_fsq = sem("head_square")
        s_fst = sem("head_square_summed")
        s_fstd = sem("head_deviation")
        s_frec = sem("head_reciprocal")
        s_fn = sem("head_normed")
        s_fsh = sem("rope_swapped")
        s_ft1 = sem("rope_sin_part")
        s_ft2 = sem("rope_cos_part")
        s_fro = sem("rope_done")
        s_qzero = sem("staged_q_zeroed")
        s_stage = sem("pair_staged")
        s_sc = sem("scores_ready")
        s_ss = sem("scores_scaled")
        s_mx = sem("max_ready")
        s_neg = sem("neg_max_ready")
        s_es = sem("sink_exp")
        s_p = sem("exp_ready")
        s_pt = sem("probs_turned")
        s_pta = sem("turned_latent_copied")
        s_ptb = sem("turned_ctx_copied")
        s_o = sem("values_summed")
        s_den = sem("denominator_ready")
        s_rinv = sem("inverse_denominator")
        s_oe = sem("attention_out_ready")
        s_otp = sem("out_turned")
        s_pf = sem("pool_out_scaled")
        s_oth = sem("mix_in_hi")
        s_otl = sem("mix_in_lo")
        s_eload = [sem(f"bias_rows_loaded_{i}") for i in range(4)]
        s_e = sem("bias_rows_masked")
        s_c2 = sem("conv_two_taps")
        s_c1 = sem("conv_mid_tap")
        s_cv = sem("conv_done")
        s_sg = sem("gate_activated")
        s_ffm = sem("gated")
        s_ffh = sem("ff_hi")
        s_ffl = sem("ff_lo")
        s_out = sem("new_kv_stored")
        s_outx = sem("x_stored")

        block = ctx.enter_context(nc.Block())

        def slot(t, s, k):
            return t[:, s, k * P:(k + 1) * P]

        CONSTS = [("cos", cos[:, :]), ("sin", sin[:, :]), ("maskc", maskc[:, :]), ("maskd", maskd[:, :]),
                  ("ident", ident[:, :]), ("onesd", onesd[:, :]), ("onesh", onesh[:, :]), ("wpool", wpool[:, :, :]), ("sel", sel[:, :]),
                  ("wconv", wconv[:, :, :]), ("bmod", bmod[:, :]), ("gains", gains[:, :, :, :]),
                  ("small", small[:, :])]
        n_const = len(CONSTS)

        def chunk(t, k):
            return t[:, bass.ds(k, 1), :].rearrange("p a n -> p (a n)")

        def part(t, k, f, n):
            return t[:, bass.ds(k, 1), f:f + n].rearrange("p a n -> p (a n)")

        def scores_of(job, s):
            if job.split:
                return ps[:, 2 * s:2 * s + 2, 0:HT]
            return psf[:, 1024 * s + job.lo:1024 * s + NT]

        def mod_col(layer, part, stream):
            c = 48 * layer + 8 * part
            return mod[:, stream, c:c + KD]

        SEG = ((0, 0, NS), (1, NS, NT))

        def norm_index(layer, which):
            return 4 * layer + which

        @block.sync
        def _(sp):
            w8, w11 = a["w8"], a["w11"]

            def load(src, s, width):
                return sp.dma_start(raw[:, s, 0:width], src.rearrange("a p n -> (a p) n")).then_inc(s_raw[s], 16)

            sp.dma_start(cvec[:, :], a["cvec"]).then_inc(s_cvec, 16)
            for s in range(4):
                sp.dma_start(mraw[s], a["wmod"][s]).then_inc(s_mraw[s], 16)
            for s in range(2):
                load(w8[s:s + 1], s, KD * P)
            sp.dma_start(x[:, :, :].rearrange("p k n -> p (k n)"), a["x"]).then_inc(s_x, 16)
            with sp.Fori(1, 24) as it:
                for s in range(4):
                    sp.wait_ge(s_mlo, 4 * it + s - 3)
                    sp.dma_start(mraw[s], a["wmod"][bass.ds(4 * it + s, 1)].rearrange("a p n -> (a p) n")
                                 ).then_inc(s_mraw[s], 16)
            u = 0
            base = {8: 0, FH: 0}
            for kk, n in RUNS:
                src = w8 if kk == 8 else w11
                first = 1 if u == 0 else 0
                with sp.Fori(first, n // 2) as h:
                    for s in range(2):
                        sp.wait_ge(s_lo, 2 * h + (u + s - 1))
                        load(src[bass.ds(2 * h + (base[kk] + s), 1)], s, kk * P)
                base[kk] += n
                u += n
            sp.wait_ge(s_tu, 64 + 2)
            sp.dma_start(o["x"], x[:, :, :].rearrange("p k n -> p (k n)")).then_inc(s_outx, 16)
            sp.wait_ge(s_out, 16 * 4)
            sp.wait_ge(s_outx, 16)

        @block.scalar
        def _(act):
            def hi(s, kk, pair):
                act.wait_ge(s_raw[s], 16 * pair + 16)
                act.wait_ge(s_unit, 2 * pair + (s + 1))
                nc.scalar.activation(whi[:, s, 0:kk * P], raw[:, s, 0:kk * P], ACT.Copy).then_inc(s_hi, 1)

            def pairs(phase, evac, skip_first=0):
                u0, n = UNITS[phase]
                nxt = PHASES.index(phase) + 1
                kk = kchunks(phase)
                knext = kchunks(PHASES[nxt]) if nxt < len(PHASES) else None

                def body(h, k2):
                    for s in range(2):
                        act.wait_ge(s_unit, 2 * h + (u0 + s + 3))
                        if k2 is not None:
                            hi(s, k2, h + (u0 // 2 + 1))
                        evac(h, s, 2 * h + (u0 + s))
                return body, n // 2, kk, knext

            def run(phase, evac):
                body, n, kk, knext = pairs(phase, evac)
                if knext == kk:
                    with act.Fori(0, n) as h:
                        body(h, kk)
                else:
                    with act.Fori(0, n - 1) as h:
                        body(h, kk)
                    body(n - 1, knext)

            def copy_a(dst, s):
                nc.scalar.activation(dst, bankA[s], ACT.Copy).then_inc(s_fa, 1)

            def square(k, n, src, s):
                act.wait_ge(s_stat, k + (8 * n + 1))
                act.nop(nofuse=True)
                nc.scalar.activation(sq[s], src, ACT.Square).then_inc(s_sq, 1)

            def deviation(n):
                act.wait_ge(s_stat, 8 * n + 10)
                if n:
                    act.wait_ge(s_rec, n)
                nc.scalar.activation(std[:, 0:HT], statA, ACT.Sqrt, bias=EPS).then_inc(s_std, 1)
                nc.scalar.activation(std[:, HT:NT], statB, ACT.Sqrt, bias=EPS).then_inc(s_std, 1)

            def pre_norm(layer, which):
                n = norm_index(layer, which)
                part = 0 if which == 0 else 3
                hidx = 8 * (2 * layer + which // 2)
                deviation(n)
                with act.Fori(0, KD // 2) as h:
                    for s in range(2):
                        act.wait_ge(s_t, 2 * h + (8 * n + s + 1))
                        act.wait_ge(s_hl, 2 * h + (hidx + s + 1))
                        for st, f, t in SEG:
                            last = nc.scalar.activation(
                                hf[s][:, f:t], tn[s][:, f:t], ACT.Identity,
                                scale=coef[:, layer, st, which, bass.ds(2 * h + s, 1)],
                                bias=mod_col(layer, part, st)[:, bass.ds(2 * h + s, 1)])
                        last.then_inc(s_tu, 1)
                        act.wait_ge(s_tu, 2 * h + (8 * n + s + 3))
                        nc.scalar.activation(chunk(hh, 2 * h + s), hf[s], ACT.Copy).then_inc(s_hh, 1)

            def post_norm(layer, which, squares):
                n = norm_index(layer, which)
                deviation(n)
                if squares:
                    with act.Fori(0, 4) as h:
                        for s in range(2):
                            act.wait_ge(s_tu, 2 * h + (8 * n + s + 3))
                            square(2 * h + s, n + 1, chunk(x, 2 * h + s), s)

            for name, dst in CONSTS:
                act.dma_start(dst, a[name]).then_inc(s_const, 16)
            act.dma_start(qk[:, 6:8, CTX0:PR0], a["kctx0"]).then_inc(s_ctx, 16)
            act.dma_start(v[:, 4, 0:2 * P], a["vctx0"]).then_inc(s_ctx, 16)
            act.wait_ge(s_cvec, 16)
            nc.scalar.activation(csilu[:, :], cvec[:, :], ACT.Silu).then_inc(s_csilu, 1)
            act.wait_ge(s_csilu, 1)
            nc.scalar.activation(cst[:, :, 0:2], csilu[:, :].rearrange("p (k s) -> p k s", s=2),
                                 ACT.Copy).then_inc(s_cst, 1)
            with act.Fori(0, 24) as b:
                for s in range(4):
                    act.wait_ge(s_mraw[s], 16 * b + 16)
                    act.wait_ge(s_mod, 4 * b + s + 1)
                    nc.scalar.activation(mh[:, s % 2, :], mraw[s], ACT.Copy).then_inc(s_mhi, 1)
            for s in range(2):
                hi(s, KD, 0)
            act.wait_ge(s_mlo, 96)
            act.wait_ge(s_x, 16)
            with act.Fori(0, 4) as h:
                for s in range(2):
                    square(2 * h + s, 0, chunk(x, 2 * h + s), s)
            act.wait_ge(s_coef, 16)
            pre_norm(0, 0)

            def unit_pair(pair, dsts, k2=KD):
                for s in range(2):
                    act.wait_ge(s_unit, 2 * pair + (s + 3))
                    hi(s, k2, pair + 1)
                    copy_a(dsts[s], s)

            def value_pair(pair, col):
                act.wait_ge(s_unit, 2 * pair + 4)
                for s in range(2):
                    hi(s, KD, pair + 1)
                nc.scalar.activation(v[:, 0:2, bass.ds(col, 2 * P)], ps[:, 0, :], ACT.Copy).then_inc(s_fa, 2)

            act.wait_ge(s_azero, 1)
            unit_pair(0, [apad[s][:, PAD:PAD + HT] for s in range(2)])
            with act.Fori(0, 4) as h:
                unit_pair(h + 1, [part(qk, 2 * h + s, 0, HT) for s in range(2)])
            value_pair(5, 0)

            with act.Fori(0, 4) as h:
                for s in range(2):
                    c = 2 * h + s
                    act.wait_ge(s_fa, c + 5)
                    act.wait_ge(s_fb, c + 5)
                    act.wait_ge(s_fst, c + 1)
                    qc = qk[:, bass.ds(c, 1), :].rearrange("p a n -> p (a n)")
                    nc.scalar.activation(fsq[s][:, 0:NS], qc[:, 0:NS], ACT.Square).then_inc(s_fsq, 1)
                    nc.scalar.activation(fsq[s][:, NS:NT], qc[:, PR0:PR0 + NP], ACT.Square).then_inc(s_fsq, 1)
                    act.wait_ge(s_fst, c + 3)
                    act.wait_ge(s_frec, c + 1)
                    nc.scalar.activation(fstd[:, 0:HT], statA, ACT.Sqrt, bias=EPS).then_inc(s_fstd, 1)
                    nc.scalar.activation(fstd[:, HT:NT], statB, ACT.Sqrt, bias=EPS).then_inc(s_fstd, 1)

            def attention(kind):
                g0, its, _ = GROUPS[kind]
                nj, jb = 2 * JOBS, JOBS * g0
                with act.Fori(0, its) as it:
                    for step in range(nj + 1):
                        if step < nj:
                            job = Job(kind, step)
                            jv = nj * it + (jb + step)
                            s = step % 2
                            act.wait_ge(s_neg, jv + 1)
                            act.wait_ge(s_pt, jv + 1)
                            act.wait_ge(s_rinv, jv + 1)
                            if kind == "C":
                                act.nop(nofuse=True)
                                nc.scalar.activation(stat8[:, 2, s:s + 1], sink[:, bass.ds(2 * it + (job.pair + 4 * job.half), 1)], ACT.Exp,
                                                     bias=stat8[:, 1, s:s + 1]).then_inc(s_es, 1)
                            dst = pb[step % 4][:, job.lo:NT]
                            src, sc = (dst, 1.0) if job.scaled else (scores_of(job, s), SCALE)
                            if job.split:
                                dst = dst.rearrange("p (b n) -> p b n", b=2)
                                src = src if not job.scaled else dst
                            nc.scalar.activation(dst, src, ACT.Exp, bias=stat8[:, 1, s:s + 1],
                                                 scale=sc, accum_out=stat8[:, 3, s:s + 1]).then_inc(s_p, 1)
                        if step >= 1:
                            job = Job(kind, step - 1)
                            jv = nj * it + (jb + step - 1)
                            if not job.prompt:
                                act.wait_ge(s_pt, jv + 3)
                                act.wait_ge(s_o, jv + 1)
                                nc.scalar.activation(pts[:, (step - 1) % 2, job.lo:NS], ps[:, 4, job.lo:NS],
                                                     ACT.Copy).then_inc(s_pta, 1)

            attention("B")

            def mix_in_hi(n, first_event, dst0, wait_pool=False):
                for c in range(n):
                    e = first_event + c
                    s = c % 2
                    act.wait_ge(s_otp, e + 1)
                    nc.scalar.activation(hh[:, dst0 + c, 0:NS], latent[s], ACT.Copy).then_inc(s_oth, 1)
                    nc.scalar.activation(hh[:, dst0 + c, NS:NT], context[s], ACT.Copy).then_inc(s_oth, 1)

            for c in range(2):
                act.wait_ge(s_otp, c + 1)
                nc.scalar.activation(pfo[c][:, 0:NS], latent[c], ACT.Copy, scale=pscale[:, c:c + 1]).then_inc(s_pf, 1)
                nc.scalar.activation(pfo[c][:, NS:NT], context[c], ACT.Copy, scale=pscale[:, c:c + 1]).then_inc(s_pf, 1)
                act.wait_ge(s_pf, 2 * c + 2)
                nc.scalar.activation(hh[:, c, :], pfo[c], ACT.Copy).then_inc(s_oth, 1)
            mix_in_hi(6, 2, 2)

            def y_phase(phase, norm, copies, squares):
                u0, n = UNITS[phase]

                def f(h, s, u):
                    if copies:
                        copy_a(part(y, 2 * h + s, 0, HT), s)
                    if squares:
                        act.wait_ge(s_fa, u + 3)
                        act.wait_ge(s_fb, u + 3)
                        square(2 * h + s, norm, chunk(y, 2 * h + s), s)
                run(phase, f)

            def ffn_half(layer, half):
                phase = (layer, f"fin{half}")
                u0 = UNITS[phase][0]
                f0 = 22 * layer + FH * half

                def f(h, s, u):
                    fp = h + f0
                    act.wait_ge(s_cv, 2 * h + (2 * f0 + s + 1))
                    copy_a(ub[s][:, 1:1 + HT], s)
                    act.wait_ge(s_fa, u + 3)
                    act.wait_ge(s_fb, u + 3)
                    if s == 0:
                        act.wait_ge(s_sg, fp + 1)
                    act.wait_ge(s_ffm, fp + 1)
                    nc.scalar.activation(cb[s], ub[s][:, 1:1 + CW], ACT.Copy,
                                         scale=wconv[:, bass.ds(2 * h + (2 * f0 + s), 1), 1]).then_inc(s_c1, 1)
                    if s == 1:
                        act.wait_ge(s_cv, 2 * h + (2 * f0 + 3))
                        nc.scalar.activation(sg, cb[0], ACT.Silu).then_inc(s_sg, 1)
                        act.wait_ge(s_ffm, fp + 2)
                        nc.scalar.activation(ffh[:, bass.ds(h, 1), :].rearrange("p a n -> p (a n)"), fft,
                                             ACT.Copy).then_inc(s_ffh, 1)
                run(phase, f)

            def ffn(layer):
                act.wait_ge(s_uzero, 6 * (layer + 1))
                act.wait_ge(s_out, 32 * (layer + 1))
                ffn_half(layer, 0)
                y_phase((layer, "fout0"), None, True, False)
                ffn_half(layer, 1)
                y_phase((layer, "fout1"), norm_index(layer, 3), False, True)

            y_phase((0, "mix"), 1, True, True)
            post_norm(0, 1, True)
            pre_norm(0, 2)
            ffn(0)
            post_norm(0, 3, True)
            pre_norm(1, 0)

            p1 = UNITS[(1, "in")][0] // 2
            with act.Fori(0, 6) as h:
                unit_pair(h + p1, [part(qk, 2 * h + s, 0, HT) for s in range(2)])
            act.wait_ge(s_unit, 2 * p1 + 12 + 3)
            hi(0, KD, p1 + 7)
            copy_a(qk[:, 12, 0:HT], 0)
            act.wait_ge(s_unit, 2 * p1 + 13 + 3)
            hi(1, KD, p1 + 7)
            nc.scalar.activation(v[:, 0:4, 0:P], latent[1], ACT.Copy).then_inc(s_fa, 1)
            with act.Fori(0, 2) as h:
                value_pair(h + (p1 + 7), 256 * h + P)
            attention("C")
            attention("D")
            mix_in_hi(8, 8, 0)
            y_phase((1, "mix"), 5, True, True)
            post_norm(1, 1, True)
            pre_norm(1, 2)
            ffn(1)
            post_norm(1, 3, False)

        @block.vector
        def _(dve):
            V = nc.vector

            def lo(s, kk, u):
                dve.wait_ge(s_hi, u + 1)
                V.tensor_tensor(wlo[:, s, 0:kk * P], raw[:, s, 0:kk * P], whi[:, s, 0:kk * P].bitcast(F32),
                                ALU.subtract).then_inc(s_lo, 1)

            def run(phase, evac):
                u0, n = UNITS[phase]
                nxt = PHASES.index(phase) + 1
                kk = kchunks(phase)
                knext = kchunks(PHASES[nxt]) if nxt < len(PHASES) else None

                def body(h, k2):
                    for s in range(2):
                        u = 2 * h + (u0 + s)
                        dve.wait_ge(s_unit, u + 3)
                        evac(h, s, u, lambda: lo(s, k2, u + 2) if k2 is not None else None)
                if knext == kk:
                    with dve.Fori(0, n // 2) as h:
                        body(h, kk)
                else:
                    with dve.Fori(0, n // 2 - 1) as h:
                        body(h, kk)
                    body(n // 2 - 1, knext)

            def copy_b(dsts, s):
                f = 0
                for dst in dsts:
                    n = HT if len(dsts) == 1 else (NS - HT, NP)[f > 0]
                    last = V.tensor_copy(dst, bankB[s][:, f:f + n])
                    f += n
                last.then_inc(s_fb, 1)

            def unit_pair(pair, dsts, k2=KD):
                for s in range(2):
                    dve.wait_ge(s_unit, 2 * pair + (s + 3))
                    copy_b(dsts[s], s)
                    lo(s, k2, 2 * pair + (s + 2))

            def reciprocal(n):
                dve.wait_ge(s_std, 2 * n + 2)
                if n:
                    dve.wait_ge(s_t, 8 * n)
                V.reciprocal(rec, std).then_inc(s_rec, 1)

            def pre_norm(layer, which):
                n = norm_index(layer, which)
                hidx = 8 * (2 * layer + which // 2)
                reciprocal(n)
                with dve.Fori(0, KD // 2) as h:
                    for s in range(2):
                        dve.wait_ge(s_hh, 2 * h + (hidx + s + 1))
                        V.tensor_tensor(chunk(hl, 2 * h + s), hf[s], chunk(hh, 2 * h + s).bitcast(F32),
                                        ALU.subtract).then_inc(s_hl, 1)

            def post_norm(layer, which):
                n = norm_index(layer, which)
                reciprocal(n)
                with dve.Fori(0, KD // 2) as h:
                    for s in range(2):
                        dve.wait_ge(s_t, 2 * h + (8 * n + s + 1))
                        for st, f, t in SEG:
                            xs = part(x, 2 * h + s, f, t - f)
                            last = V.scalar_tensor_tensor(
                                out=xs, in0=tn[s][:, f:t], scalar=coef[:, layer, st, which, bass.ds(2 * h + s, 1)],
                                in1=xs, op0=ALU.mult, op1=ALU.add)
                        last.then_inc(s_tu, 1)

            dve.wait_ge(s_cst, 1)
            V.tensor_tensor(cst[:, :, 2:4], csilu[:, :].rearrange("p (k s) -> p k s", s=2), cst[:, :, 0:2].bitcast(F32),
                            ALU.subtract).then_inc(s_cst, 1)

            def mod_rows(n, b):
                dve.wait_ge(s_mod, 4 * n + 6)
                dve.wait_ge(s_mt, n + 1)
                V.tensor_copy(mrow[b], ps[0:4, 5 + b, :]).then_inc(s_mrow, 1)

            def mod_blocks(h, first=False):
                for b in range(2):
                    for s in range(4):
                        dve.wait_ge(s_mhi, 8 * h + (4 * b + s + 1))
                        V.tensor_tensor(ml[:, s % 2, :], mraw[s], mh[:, s % 2, :].bitcast(F32),
                                        ALU.subtract).then_inc(s_mlo, 1)
                        if s == 1 and not (first and b == 0):
                            mod_rows(2 * h + (b - 1), 1 - b)

            mod_blocks(0, True)
            with dve.Fori(1, 12) as h:
                mod_blocks(h)
            mod_rows(23, 1)
            for s in range(2):
                lo(s, KD, s)
            dve.wait_ge(s_mt, 24 + 2)
            dve.wait_ge(s_const, 16 * n_const)
            for st in range(2):
                V.tensor_tensor(mod[:, st, :], ps[:, 4, 0:192].rearrange("p (c s) -> p s c", s=2)[:, st, :], bmod[:, :],
                                ALU.add).then_inc(s_modb, 1)
            dve.wait_ge(s_modb, 2)
            for layer in range(2):
                for st in range(2):
                    for w in range(4):
                        m = mod_col(layer, (1, 2, 4, 5)[w], st)
                        V.scalar_tensor_tensor(out=coef[:, layer, st, w, :], in0=m, scalar=1.0 if w % 2 == 0 else 0.0,
                                               in1=gains[:, layer, w, :], op0=ALU.add, op1=ALU.mult).then_inc(s_coef, 1)
            pre_norm(0, 0)

            def value_pair(pair, col):
                dve.wait_ge(s_unit, 2 * pair + 4)
                V.tensor_copy(v[:, 2:4, bass.ds(col, 2 * P)], ps[:, 1, :].rearrange("p (t n) -> p t n", t=2))
                V.tensor_copy(v[:, 5, bass.ds(col, 2 * P)], ps[:, 2, 0:2 * P]).then_inc(s_fb, 2)
                for s in range(2):
                    lo(s, KD, 2 * pair + (s + 2))

            dve.wait_ge(s_azero, 1)
            unit_pair(0, [(apad[s][:, PAD + HT:PAD + NS], apad[s][:, AP0:AP0 + NP]) for s in range(2)])
            with dve.Fori(0, 4) as h:
                unit_pair(h + 1, [(part(qk, 2 * h + s, HT, NS - HT), part(qk, 2 * h + s, PR0, NP)) for s in range(2)])
            value_pair(5, 0)

            def head_norm(c, g):
                dve.wait_ge(s_fstd, 2 * c + 4)
                V.reciprocal(frec, fstd).then_inc(s_frec, 1)
                dve.wait_ge(s_frec, c + 2)
                dve.wait_ge(s_fro, c + 1)
                pr = part(qk, c, PR0, NP)
                V.scalar_tensor_tensor(out=fqn, in0=part(qk, c, 0, NS), scalar=g, in1=frec[:, 0:NS], op0=ALU.mult,
                                       op1=ALU.mult).then_inc(s_fn, 1)
                V.scalar_tensor_tensor(out=pr, in0=pr, scalar=g, in1=frec[:, NS:NT], op0=ALU.mult,
                                       op1=ALU.mult).then_inc(s_fn, 1)

            def rope(c, r):
                q = part(qk, c, 0, NS)
                dve.wait_ge(s_fro, r + 1)
                dve.wait_ge(s_fn, 2 * r + 2)
                dve.nop(nofuse=True)
                V.stream_shuffle(fsh, fqn, [i ^ 1 for i in range(32)]).then_inc(s_fsh, 1)
                V.tensor_tensor(ft2, fqn, cos[:, :], ALU.mult).then_inc(s_ft2, 1)
                dve.wait_ge(s_ft1, r + 1)
                dve.wait_ge(s_ft2, r + 1)
                V.tensor_tensor(q, ft1, ft2, ALU.add).then_inc(s_fro, 1)

            with dve.Fori(0, 6) as c:
                head_norm(c, gqk[:, 0:1])
                rope(c, c)
            with dve.Fori(6, 8) as c:
                head_norm(c, gqk[:, 1:2])
                rope(c, c)

            def scale_values(job, jv, it, t):
                dve.wait_ge(s_o, jv)
                dve.wait_ge(s_rinv, jv)
                V.tensor_scalar(osb[:, job.t, bass.ds(job.head_col(it), DH)], ps[:, 6 + t, 0:DH],
                                stat8[:, 5, t:t + 1], None, ALU.mult).then_inc(s_oe, 1)

            def attention(kind):
                g0, its, _ = GROUPS[kind]
                nj, jb = 2 * JOBS, JOBS * g0
                with dve.Fori(0, its) as it:
                    for step in range(nj + 3):
                        now, last, old = (Job(kind, i) if 0 <= i < nj else None for i in (step, step - 1, step - 3))
                        jv = nj * it + (jb + step)
                        s, t = step % 2, (step - 1) % 2
                        negm = stat8[:, 1, s:s + 1]
                        sums = stat8[:, 3, t:t + 1]
                        if now:
                            dve.wait_ge(s_sc, jv + 31)
                            dve.wait_ge(s_p, jv + 1)
                            scores = scores_of(now, s)
                            if now.scaled:
                                dve.wait_ge(s_pt, jv - 1)
                                sbuf = pb[step % 4]
                                if kind == "C":
                                    m0 = now.mask_from()
                                    V.scalar_tensor_tensor(out=sbuf[:, now.lo:NT], in0=scores, scalar=SCALE,
                                                           in1=maskc[:, m0:m0 + NT - now.lo], op0=ALU.mult,
                                                           op1=ALU.add).then_inc(s_ss, 1)
                                else:
                                    if not now.prompt:
                                        e = 2 * now.pair + now.half
                                        dve.wait_ge(s_e, 4 * it + (e + 1))
                                        r0 = (7 - 2 * now.t) * 64
                                        for b, f, n in ((0, 0, HT), (1, HT, NS - HT)):
                                            V.scalar_tensor_tensor(out=sbuf[:, f:f + n], in0=ps[:, 2 * s + b, 0:n],
                                                                   scalar=SCALE, in1=erow[e][:, r0 + f:r0 + f + n],
                                                                   op0=ALU.mult, op1=ALU.add)
                                        scores = ps[:, 2 * s + 1, NS - HT:HT]
                                    V.tensor_scalar(sbuf[:, NS:NT], scores, SCALE, None, ALU.mult).then_inc(s_ss, 1)
                                scores = sbuf[:, now.lo:NT]
                        if old and kind != "B":
                            scale_values(old, jv, it, t)
                        if now:
                            if now.scaled:
                                dve.wait_ge(s_ss, jv - 60 + 3)
                            V.tensor_reduce(stat8[:, 0, s:s + 1], scores, AX.XY if now.split and not now.scaled
                                            else AX.X, ALU.max).then_inc(s_mx, 1)
                        if last and kind == "C":
                            dve.wait_ge(s_p, jv + 2)
                            V.tensor_tensor(stat8[:, 4, t:t + 1], sums, stat8[:, 2, t:t + 1],
                                            ALU.add).then_inc(s_den, 1)
                        if now:
                            dve.wait_ge(s_mx, jv + 1)
                            if kind == "C":
                                V.tensor_scalar(negm, stat8[:, 0, s:s + 1],
                                                sink[:, bass.ds(2 * it + (now.pair + 4 * now.half), 1)], -1.0,
                                                ALU.max, ALU.mult).then_inc(s_neg, 1)
                            else:
                                V.tensor_scalar(negm, stat8[:, 0, s:s + 1], -1.0 if now.scaled else -SCALE, None,
                                                ALU.mult).then_inc(s_neg, 1)
                        if old and kind == "B":
                            scale_values(old, jv, it, t)
                        if last:
                            if kind == "C":
                                dve.wait_ge(s_den, nj * it + step)
                                sums = stat8[:, 4, t:t + 1]
                            dve.wait_ge(s_p, jv + 2)
                            dve.wait_ge(s_oe, jv)
                            V.reciprocal(stat8[:, 5, t:t + 1], sums).then_inc(s_rinv, 1)
                            dve.wait_ge(s_pt, jv + 2)
                            dve.wait_ge(s_o, jv)
                            V.tensor_copy(pts[:, t, NS:NT], ps[:, 5, 0:NP]).then_inc(s_ptb, 1)

            attention("B")

            def mix_in_lo(n, oth0, dst0):
                for c in range(n):
                    s = c % 2
                    dve.wait_ge(s_oth, oth0 + 2 * c + 2)
                    V.tensor_tensor(hl[:, dst0 + c, 0:NS], latent[s], hh[:, dst0 + c, 0:NS].bitcast(F32),
                                    ALU.subtract).then_inc(s_otl, 1)
                    V.tensor_tensor(hl[:, dst0 + c, NS:NT], context[s], hh[:, dst0 + c, NS:NT].bitcast(F32),
                                    ALU.subtract).then_inc(s_otl, 1)

            for c in range(2):
                dve.wait_ge(s_oth, c + 1)
                V.tensor_tensor(hl[:, c, :], pfo[c], hh[:, c, :].bitcast(F32), ALU.subtract).then_inc(s_otl, 1)
            mix_in_lo(6, 2, 2)

            def y_phase(phase, add):
                u0, n = UNITS[phase]
                if add:
                    dve.wait_ge(s_fa, u0 + 2)
                    dve.wait_ge(s_fb, u0 + 2)

                def f(h, s, u, split):
                    if add:
                        ya = part(y, 2 * h + s, 0, HT)
                        yb = part(y, 2 * h + s, HT, HT)
                        V.tensor_tensor(ya, bankA[s], ya, ALU.add).then_inc(s_fa, 1)
                        V.tensor_tensor(yb, bankB[s], yb, ALU.add).then_inc(s_fb, 1)
                    else:
                        copy_b([part(y, 2 * h + s, HT, HT)], s)
                    split()
                run(phase, f)

            def ffn_half(layer, half):
                f0 = 22 * layer + FH * half

                def f(h, s, u, split):
                    fp = h + f0
                    cu = 2 * h + (2 * f0 + s)
                    dve.wait_ge(s_cv, cu + 1)
                    copy_b([ub[s][:, 1 + HT:1 + NS], ub[s][:, UP0:UP0 + NP]], s)
                    split()
                    dve.wait_ge(s_c1, cu + 1)
                    V.scalar_tensor_tensor(out=cb[s], in0=ub[s][:, 0:CW], scalar=wconv[:, bass.ds(cu, 1), 0], in1=cb[s],
                                           op0=ALU.mult, op1=ALU.add).then_inc(s_c2, 1)
                    dve.wait_ge(s_c2, cu + 1)
                    V.scalar_tensor_tensor(out=cb[s], in0=ub[s][:, 2:UW], scalar=wconv[:, bass.ds(cu, 1), 2], in1=cb[s],
                                           op0=ALU.mult, op1=ALU.add).then_inc(s_cv, 1)
                    if s == 1:
                        dve.wait_ge(s_cv, cu + 3)
                        dve.wait_ge(s_sg, fp + 2)
                        dve.wait_ge(s_ffl, fp + 1)
                        V.tensor_tensor(fft[:, 0:NS], sg[:, 0:NS], cb[1][:, 0:NS], ALU.mult)
                        V.tensor_tensor(fft[:, NS:NT], sg[:, CP0:CW], cb[1][:, CP0:CW], ALU.mult).then_inc(s_ffm, 1)
                        dve.wait_ge(s_ffh, fp + 1)
                        V.tensor_tensor(chunk(ffl, h), fft, chunk(ffh, h).bitcast(F32), ALU.subtract).then_inc(s_ffl, 1)
                run((layer, f"fin{half}"), f)

            def ffn(layer):
                dve.wait_ge(s_hl, 8 * (2 * layer + 2) + 2)
                for s in range(2):
                    for f, n in ((0, 1), (1 + NS, 2), (UW - 1, 1)):
                        V.memset(ub[s][:, f:f + n], 0.0).then_inc(s_uzero, 1)
                dve.wait_ge(s_uzero, 6 * (layer + 1))
                dve.wait_ge(s_out, 32 * (layer + 1))
                ffn_half(layer, 0)
                y_phase((layer, "fout0"), False)
                ffn_half(layer, 1)
                y_phase((layer, "fout1"), True)

            y_phase((0, "mix"), False)
            post_norm(0, 1)
            pre_norm(0, 2)
            ffn(0)
            post_norm(0, 3)
            pre_norm(1, 0)
            p1 = UNITS[(1, "in")][0] // 2
            with dve.Fori(0, 6) as h:
                unit_pair(h + p1, [(part(qk, 2 * h + s, HT, NS - HT), part(qk, 2 * h + s, PR0, NP)) for s in range(2)])
            dve.wait_ge(s_unit, 2 * p1 + 12 + 3)
            copy_b((qk[:, 12, HT:NS], qk[:, 12, PR0:PR0 + NP]), 0)
            lo(0, KD, 2 * p1 + 14)
            dve.wait_ge(s_unit, 2 * p1 + 13 + 3)
            V.tensor_copy(v[:, 5, 0:P], context[1]).then_inc(s_fb, 1)
            lo(1, KD, 2 * p1 + 15)
            with dve.Fori(0, 2) as h:
                value_pair(h + (p1 + 7), 256 * h + P)
            u1 = UNITS[(1, "mix")][0]
            dve.wait_ge(s_fa, u1 + 2)
            dve.wait_ge(s_fb, u1 + 2)
            def rope_plain(c, r):
                dve.wait_ge(s_fro, r + 1)
                V.tensor_copy(fqn, part(qk, c, 0, NS)).then_inc(s_fn, 2)
                rope(c, r)

            with dve.Fori(0, 4) as c:
                rope_plain(c, c + 8)
            rope_plain(12, 12)
            attention("C")
            attention("D")
            mix_in_lo(8, 14, 0)
            y_phase((1, "mix"), False)
            post_norm(1, 1)
            pre_norm(1, 2)
            ffn(1)
            post_norm(1, 3)

        @block.gpsimd
        def _(pool):
            G = nc.gpsimd

            def scale_rows(n, src):
                pool.wait_ge(s_rec, n + 1)
                with pool.Fori(0, KD // 2) as h:
                    for s in range(2):
                        pool.wait_ge(s_tu, 2 * h + (8 * n + s + 1))
                        G.tensor_tensor(tn[s], chunk(src, 2 * h + s), rec, ALU.mult).then_inc(s_t, 1)

            def rope_sin(n, r0):
                with pool.Fori(r0, r0 + n) as r:
                    pool.wait_ge(s_fsh, r + 1)
                    G.tensor_tensor(ft1, fsh, sin[:, :], ALU.mult).then_inc(s_ft1, 1)

            def clear_q(n):
                for q in (qh, ql):
                    G.memset(q[DH:P, :, 0, :].bitcast(F32), 0.0).then_inc(s_qzero, 1)
                    G.memset(q[0:DH, :, 1, :].bitcast(F32), 0.0).then_inc(s_qzero, 1)
                pool.wait_ge(s_qzero, 4 * n)

            def stage_k(slot_, chunk_, before):
                G.tensor_copy(kh[:, slot_, :], chunk(qk, chunk_)).then_inc(s_stage, 1)
                pool.wait_ge(s_stage, before + 1)
                G.tensor_tensor(kl[:, slot_, :], chunk(qk, chunk_), kh[:, slot_, :].bitcast(F32),
                                ALU.subtract).then_inc(s_stage, 1)

            def stage(kind, it, i):
                g0, _, st0 = GROUPS[kind]
                copies = 10 if kind == "D" else 8
                before = 2 * copies * it + (st0 + copies * i)
                qc = {"B": it + 3 * i, "C": 2 * it + i, "D": 2 * it + (4 + i)}[kind]
                pool.wait_ge(s_sc, 2 * JOBS * it + (JOBS * (g0 + i - 1) + 30))
                if kind == "D":
                    pool.wait_ge(s_stage, before)
                    stage_k(i, 2 * it + (8 + i), before)
                    before = before + 2
                    pool.wait_ge(s_stage, before)
                pieces = [(slice(DH * half, DH * half + DH), half, f, src, w)
                          for half in range(2) for f, src, w in ((0, 0, NS), (NS, PR0, NP))]
                for rows, half, f, src, w in pieces:
                    G.tensor_copy(qh[rows, i, half, f:f + w], qk[rows, bass.ds(qc, 1), src:src + w].rearrange(
                        "p a n -> p (a n)")).then_inc(s_stage, 1)
                pool.wait_ge(s_stage, before + 4)
                pool.nop(nofuse=True)
                for rows, half, f, src, w in pieces:
                    G.tensor_tensor(ql[rows, i, half, f:f + w], qk[rows, bass.ds(qc, 1), src:src + w].rearrange(
                        "p a n -> p (a n)"), qh[rows, i, half, f:f + w].bitcast(F32),
                        ALU.subtract).then_inc(s_stage, 1)

            scale_rows(0, x)
            pool.wait_ge(s_hl, 8 + 2)
            G.memset(work[:, 0:2 * AW], 0.0).then_inc(s_azero, 1)
            for c in range(2):
                pool.dma_start(icnt[c], a["icnt"][c]).then_inc(s_icnt, 16)
            pool.wait_ge(s_icnt, 32)
            steps = [0]

            def step(ins):
                steps[0] += 1
                ins.then_inc(s_pool, 1)
                pool.wait_ge(s_pool, steps[0])

            for c in range(2):
                pool.wait_ge(s_fa, c + 3)
                pool.wait_ge(s_fb, c + 3)
                t0, t1 = ptmp
                step(G.tensor_tensor(t0[:, 1:AW], apad[c][:, 0:AW - 1], apad[c][:, 1:AW], ALU.add))
                if c == 1:
                    step(G.tensor_tensor(t1[:, 2:AW - 1], t0[:, 1:AW - 2], t0[:, 3:AW], ALU.add))
                    step(G.tensor_tensor(t0[:, 4:AW - 3], t1[:, 2:AW - 5], t1[:, 6:AW - 1], ALU.add))
                w = 1 << (2 * c)
                lo_edge, hi_edge = 2 * w, AW - 2 * w + 1
                step(G.tensor_tensor(t1[64:P, lo_edge:hi_edge], t0[64:P, lo_edge - w:hi_edge - w],
                                     t0[64:P, lo_edge + w:hi_edge + w], ALU.add))
                for f, src, n in ((0, PAD, NS), (NS, AP0, NP)):
                    for rows, t in ((slice(0, 64), t0), (slice(64, P), t1)):
                        step(G.tensor_tensor(icnt[c][rows, f:f + n], t[rows, src:src + n], icnt[c][rows, f:f + n],
                                             ALU.mult))
                    step(G.tensor_tensor(icnt[c][:, f:f + n], icnt[c][:, f:f + n], apad[c][:, src:src + n],
                                         ALU.subtract))
            assert steps[0] == POOL_STEPS
            pool.wait_ge(s_unit, 12 + 2)
            clear_q(1)
            rope_sin(8, 0)
            pool.wait_ge(s_fro, 8 + 1)
            pool.wait_ge(s_fn, 16)
            pool.wait_ge(s_fa, 12 + 2)
            pool.wait_ge(s_fb, 12 + 2)
            pool.wait_ge(s_ctx, 32)
            pool.dma_start(o["k0"], qk[:, 6:8, PR0:PR0 + NP]).then_inc(s_out, 16)
            pool.dma_start(o["v0"], v[:, 5, 0:2 * P]).then_inc(s_out, 16)
            for i in range(2):
                stage_k(i, 6 + i, 2 * i)
            pool.wait_ge(s_stage, 4)
            with pool.Fori(0, 3) as it:
                for i in range(2):
                    stage("B", it, i)
            pool.wait_ge(s_stage, 52)
            scale_rows(1, y)
            scale_rows(2, x)
            scale_rows(3, y)
            scale_rows(4, x)
            pool.wait_ge(s_unit, UNITS[(1, "in")][0] + 2)
            pool.dma_start(qk[:, 8:13, CTX0:PR0], a["kctx1"]).then_inc(s_ctx1, 16)
            pool.dma_start(v[:, 4, :], a["vctx1"]).then_inc(s_ctx1, 16)
            pool.wait_ge(s_hl, 24 + 2)

            def load_bias(e, head):
                pool.dma_start(erow[e], a["rpb"][head]).then_inc(s_eload[e], 16)

            def mask_bias(e, n):
                pool.wait_ge(s_eload[e], 16 * n)
                r = erow[e].rearrange("p (r c) -> p r c", c=64)
                G.tensor_tensor(r, r, maskd[:, :].unsqueeze(1).to_broadcast([P, 15, 64]), ALU.add).then_inc(s_e, 1)

            for e in range(4):
                load_bias(e, e)
            pool.wait_ge(s_unit, UNITS[(1, "mix")][0] + 2)
            clear_q(2)
            rope_sin(5, 8)
            u1 = UNITS[(1, "mix")][0]
            pool.wait_ge(s_fro, 13 + 1)
            pool.wait_ge(s_fa, u1 + 2)
            pool.wait_ge(s_fb, u1 + 2)
            pool.wait_ge(s_ctx1, 32)
            pool.dma_start(o["k1"], qk[:, 8:13, PR0:PR0 + NP]).then_inc(s_out, 16)
            pool.dma_start(o["v1"], v[:, 5, :]).then_inc(s_out, 16)
            pool.wait_ge(s_sc, JOBS * 6 + 30)
            stage_k(0, 12, 52)
            pool.wait_ge(s_stage, 54)
            with pool.Fori(0, 2) as it:
                for i in range(2):
                    stage("C", it, i)
            pool.wait_ge(s_stage, 86)
            for e in range(4):
                mask_bias(e, 1)
            pool.wait_ge(s_sc, JOBS * 10 + 30)
            for i in range(2):
                stage("D", 0, i)
            for i in range(2):
                pool.wait_ge(s_neg, JOBS * (10 + i + 1))
                for half in range(2):
                    load_bias(2 * i + half, 4 + 2 * i + half)
                stage("D", 1, i)
                pool.wait_ge(s_stage, 86 + 10 * (3 + i))
                for half in range(2):
                    mask_bias(2 * i + half, 2)
            scale_rows(5, y)
            scale_rows(6, x)
            scale_rows(7, y)

        @block.tensor
        def _(pe):
            T = nc.tensor
            for s, credit in ((s_unit, 2), (s_fa, 2), (s_fb, 2), (s_mod, 2), (s_mt, 2), (s_stat, 2), (s_tu, 2), (s_hl, 2),
                              (s_fst, 2), (s_fstd, 2), (s_frec, 1), (s_fro, 1), (s_sc, 30), (s_ss, 2), (s_p, 2), (s_pt, 2),
                              (s_pta, 1), (s_ptb, 1), (s_o, 2), (s_rinv, 2), (s_oe, 2), (s_cv, 2), (s_sg, 1),
                              (s_ffm, 1), (s_ffl, 1)):
                pe.sem_inc(s, credit)

            def unit(s, u, kk, hi, lo):
                pe.wait_ge(s_lo, u + 1)
                pe.wait_ge(s_fa, u + 1)
                pe.wait_ge(s_fb, u + 1)
                for k in range(kk):
                    for n, (w, h) in enumerate(((whi, hi), (whi, lo), (wlo, hi))):
                        st, sp_ = k == 0 and n == 0, k == kk - 1 and n == 2
                        T.matmul(bankA[s], slot(w, s, k), h[:, k, 0:HT], start=st, stop=sp_)
                        last = T.matmul(bankB[s], slot(w, s, k), h[:, k, HT:NT], start=st, stop=sp_)
                last.then_inc(s_unit, 1)

            def first_down(u, f0):
                pe.wait_ge(s_lo, u + 1)
                pe.wait_ge(s_fa, u + 1)
                pe.wait_ge(s_fb, u + 1)
                for k in range(FH):
                    pe.wait_ge(s_ffl, f0 + k + 2)
                    for n, (w, h) in enumerate(((whi, ffh), (whi, ffl), (wlo, ffh))):
                        st, sp_ = k == 0 and n == 0, k == FH - 1 and n == 2
                        T.matmul(bankA[0], slot(w, 0, k), h[:, k, 0:HT], start=st, stop=sp_)
                        last = T.matmul(bankB[0], slot(w, 0, k), h[:, k, HT:NT], start=st, stop=sp_)
                last.then_inc(s_unit, 1)

            def unit_v(s, u):
                pe.wait_ge(s_lo, u + 1)
                pe.wait_ge(s_fa, u + 1)
                pe.wait_ge(s_fb, u + 1)
                for t in range(5):
                    out = latent[s][:, t * P:(t + 1) * P] if t < 4 else context[s]
                    for k in range(KD):
                        for n, (w, h) in enumerate(((whi, hh), (whi, hl), (wlo, hh))):
                            last = T.matmul(out, h[:, k, t * P:(t + 1) * P], slot(w, s, k),
                                            start=k == 0 and n == 0, stop=k == KD - 1 and n == 2)
                last.then_inc(s_unit, 1)

            def pair_v(u):
                pe.wait_ge(s_lo, u + 2)
                pe.wait_ge(s_fa, u + 2)
                pe.wait_ge(s_fb, u + 2)
                for t in range(5):
                    out = ps[:, t // 2, t % 2 * 2 * P:(t % 2 + 1) * 2 * P].rearrange("p (a n) -> p a n", a=2)
                    for k in range(KD):
                        for n, (w, h) in enumerate(((whi, hh), (whi, hl), (wlo, hh))):
                            last = T.matmul(out, h[:, k, t * P:(t + 1) * P], w[:, :, k * P:(k + 1) * P],
                                            start=k == 0 and n == 0, stop=k == KD - 1 and n == 2)
                last.then_inc(s_unit, 2)

            def dense(s, u):
                unit(s, u, KD, hh, hl)

            def stat(n, k, s):
                first, last = (k == 0, k == KD - 1) if isinstance(k, int) else (False, False)
                if first and n:
                    pe.wait_ge(s_std, 2 * n)
                pe.wait_ge(s_sq, k + (8 * n + 1))
                T.matmul(statA, onesd[:, :], sq[s][:, 0:HT], start=first, stop=last)
                T.matmul(statB, onesd[:, :], sq[s][:, HT:NT], start=first, stop=last).then_inc(s_stat, 1)

            pe.wait_ge(s_cst, 2)
            pe.wait_ge(s_const, 16 * n_const)
            def mod_turn(n, b):
                pe.wait_ge(s_mrow, n + 1)
                for j in range(4):
                    last = T.matmul(ps[:, 4, bass.ds(8 * n + 2 * j, 2)], mrow[b][:, j * P:(j + 1) * P],
                                    sel[:, :], start=True, stop=True)
                last.then_inc(s_mt, 1)

            def mod_blocks(h, first=False):
                for b in range(2):
                    for s in range(4):
                        pe.wait_ge(s_mlo, 8 * h + (4 * b + s + 1))
                        for kk in range(2):
                            k = 2 * s + kk
                            T.matmul(ps[0:4, 5 + b, :], cst[:, k, :], mh[:, s % 2, kk * 512:(kk + 1) * 512],
                                     start=k == 0, stop=False)
                            last = T.matmul(ps[0:4, 5 + b, :], cst[:, k, :], ml[:, s % 2, kk * 512:(kk + 1) * 512],
                                            start=False, stop=k == KD - 1)
                        last.then_inc(s_mod, 1)
                        if s == 2 and not (first and b == 0):
                            mod_turn(2 * h + (b - 1), 1 - b)

            mod_blocks(0, True)
            with pe.Fori(1, 12) as h:
                mod_blocks(h)
            mod_turn(23, 1)
            for k in range(KD):
                stat(0, k, k % 2)

            def dense_pairs(u0, n):
                with pe.Fori(0, n) as h:
                    for s in range(2):
                        dense(s, 2 * h + (u0 + s))

            def first_pair(u0, hl0):
                pe.wait_ge(s_lo, u0 + 2)
                pe.wait_ge(s_fa, u0 + 2)
                pe.wait_ge(s_fb, u0 + 2)
                for k in range(KD):
                    pe.wait_ge(s_hl, hl0 + k + 3)
                    for s in range(2):
                        for n, (w, h) in enumerate(((whi, hh), (whi, hl), (wlo, hh))):
                            st, sp_ = k == 0 and n == 0, k == KD - 1 and n == 2
                            T.matmul(bankA[s], slot(w, s, k), h[:, k, 0:HT], start=st, stop=sp_)
                            last = T.matmul(bankB[s], slot(w, s, k), h[:, k, HT:NT], start=st, stop=sp_)
                        if k == KD - 1:
                            last.then_inc(s_unit, 1)

            first_pair(0, 0)
            dense_pairs(2, 4)
            pair_v(10)
            with pe.Fori(0, 4) as h:
                for s in range(2):
                    c = 2 * h + s
                    pe.wait_ge(s_fsq, 2 * c + 2)
                    pe.wait_ge(s_fstd, 2 * c + 2)
                    T.matmul(statA, onesh[:, :], fsq[s][:, 0:HT], start=True, stop=True)
                    T.matmul(statB, onesh[:, :], fsq[s][:, HT:NT], start=True, stop=True).then_inc(s_fst, 1)

            def attention(kind):
                g0, its, st0 = GROUPS[kind]
                nj, jb = 2 * JOBS, JOBS * g0
                copies = 10 if kind == "D" else 8
                ahead = 1 if kind == "B" else 2
                with pe.Fori(0, its) as it:
                    for step in range(-ahead, nj + 1):
                        if step + ahead < nj:
                            job = Job(kind, step + ahead)
                            s = (step + ahead) % 2
                            jv = nj * it + (jb + step + ahead)
                            if (step + ahead) % JOBS == 0:
                                pe.wait_ge(s_stage, 2 * copies * it + (st0 + copies * (job.pair + 1)))
                            if job.scaled:
                                pe.wait_ge(s_ss, jv - 60 + 1)
                            else:
                                pe.wait_ge(s_p, jv + 1)
                            kslot = 0 if kind == "C" else job.pair
                            if job.split:
                                runs = [(ps[:, 2 * s, 0:HT], 0, HT), (ps[:, 2 * s + 1, 0:HT], HT, HT)]
                            else:
                                runs = [(psf[:, 1024 * s + NS:1024 * s + NT], job.kctx, P)]
                                if not job.prompt:
                                    runs.append((psf[:, 1024 * s + job.lo:1024 * s + NS], job.tiles[0] * P,
                                                 NS - job.lo))
                            for n, (q, k) in enumerate(((qh, kh), (qh, kl), (ql, kh))):
                                for out, k0, w in runs:
                                    last = T.matmul(out, q[:, job.pair, job.half, job.q0:job.q0 + P],
                                                    k[:, kslot, k0:k0 + w], start=n == 0, stop=n == 2)
                            last.then_inc(s_sc, 1)
                        if 0 <= step < nj:
                            job = Job(kind, step)
                            s = step % 2
                            jv = nj * it + (jb + step)
                            pe.wait_ge(s_p, jv + 3)
                            pe.wait_ge(s_ptb, jv + 1)
                            if not job.prompt:
                                pe.wait_ge(s_pta, 16 * it + (8 * g0 + job.latent + 1))
                                for c in range(job.lo, NS, P):
                                    T.transpose(ps[:, 4, c:c + P], pb[step % 4][:, c:c + P], ident[:, :])
                            T.transpose(ps[:, 5, 0:P], pb[step % 4][:, NS:NT], ident[:, :]).then_inc(s_pt, 1)
                        if step >= 1:
                            job = Job(kind, step - 1)
                            s = (step - 1) % 2
                            jv = nj * it + (jb + step - 1)
                            pe.wait_ge(s_ptb, jv + 2)
                            if not job.prompt:
                                pe.wait_ge(s_pta, 16 * it + (8 * g0 + job.latent + 2))
                            pe.wait_ge(s_oe, jv + 1)
                            keys = [(job.lo + P * i, t) for i, t in enumerate(job.tiles)] + [(NS, job.vctx)]
                            for i, (c, t) in enumerate(keys):
                                last = T.matmul(ps[:, 6 + s, 0:DH], pts[:, s, c:c + P],
                                                v[:, t, bass.ds(job.v_col(it), DH)], start=i == 0,
                                                stop=i == len(keys) - 1)
                            last.then_inc(s_o, 1)

            attention("B")

            def turn(n, e0, otl0, chunk0):
                for c in range(n):
                    s = c % 2
                    if c >= 2:
                        pe.wait_ge(s_otl, otl0 + 2 * (c - 1) + 2)
                    for t in range(5):
                        out = latent[s][:, t * P:(t + 1) * P] if t < 4 else context[s]
                        last = T.transpose(out, osb[:, t, c * P:(c + 1) * P], ident[:, :])
                    last.then_inc(s_otp, 1)

            pe.wait_ge(s_pool, POOL_STEPS)
            for c in range(2):
                T.matmul(latent[c], wpool[:, c, :], icnt[c][:, 0:NS], start=True, stop=True)
                T.matmul(context[c], wpool[:, c, :], icnt[c][:, NS:NT], start=True, stop=True).then_inc(s_otp, 1)
            pe.wait_ge(s_oe, 60 + 2)
            pe.wait_ge(s_pf, 4)
            turn(6, 2, 0 + 2, 2)

            def y_units(phase, n):
                u0, _ = UNITS[phase]

                def one(h, s):
                    if phase[1] == "mix":
                        dense(s, 2 * h + (u0 + s))
                    else:
                        unit(s, 2 * h + (u0 + s), FH, ffh, ffl)

                if phase[1] == "mix":
                    one(0, 0)
                else:
                    first_down(u0, 22 * phase[0] + FH)
                one(0, 1)
                stat(n, 0, 0)
                with pe.Fori(1, 3) as h:
                    one(h, 0)
                    stat(n, 2 * h - 1, 1)
                    one(h, 1)
                    stat(n, 2 * h, 0)
                one(3, 0)
                stat(n, 5, 1)
                one(3, 1)
                stat(n, 6, 0)
                stat(n, 7, 1)

            def ffn(layer):
                for half in range(2):
                    u0 = UNITS[(layer, f"fin{half}")][0]
                    if half == 0:
                        first_pair(u0, 8 * (2 * layer + 1))
                        dense_pairs(u0 + 2, FH - 1)
                    else:
                        dense_pairs(u0, FH)
                    f0 = 22 * layer + FH * half
                    if half == 0:
                        u0, n = UNITS[(layer, "fout0")]
                        first_down(u0, f0)
                        unit(1, u0 + 1, FH, ffh, ffl)
                        with pe.Fori(1, n // 2) as h:
                            for s in range(2):
                                unit(s, 2 * h + (u0 + s), FH, ffh, ffl)
                    else:
                        y_units((layer, "fout1"), norm_index(layer, 3))

            def stats(n):
                for k in range(KD):
                    stat(n, k, k % 2)

            pe.wait_ge(s_otl, 14 + 2 - 2)
            y_units((0, "mix"), 1)
            stats(2)
            ffn(0)
            stats(4)
            u1 = UNITS[(1, "in")][0]
            first_pair(u1, 16)
            dense_pairs(u1 + 2, 5)
            dense(0, u1 + 12)
            unit_v(1, u1 + 13)
            with pe.Fori(0, 2) as h:
                pair_v(2 * h + (u1 + 14))
            pe.wait_ge(s_p, 60 + 2)
            attention("C")
            attention("D")
            pe.wait_ge(s_oe, 140 + 2)
            turn(8, 8, 14, 0)
            pe.wait_ge(s_otl, 30)
            y_units((1, "mix"), 5)
            stats(6)
            ffn(1)


def kernel(x_prompt, x_sample, cache_b_k, cache_b_v, cache_c_k, cache_c_v, cache_d_k, cache_d_v,
           c, c_ctx, w_mod, b_mod, g_mix_pre, g_mix_post, g_ffn_pre, g_ffn_post,
           w_in_even, w_pool, pool_scale, g_q_b, g_k_b, w_in_odd, sink_c, rpb_d,
           w_mix_out, w_ffn_in, w_ffn_conv, w_ffn_out):
    import numpy as np
    import concourse.bacc as bacc
    from concourse.bass_utils import run_bass_kernel_spmd as run

    (x_prompt, x_sample, cache_b_k, cache_b_v, cache_c_k, cache_c_v, cache_d_k, cache_d_v, c, c_ctx, w_mod, b_mod,
     g_mix_pre, g_mix_post, g_ffn_pre, g_ffn_post, w_in_even, w_pool, pool_scale, g_q_b, g_k_b, w_in_odd, sink_c,
     rpb_d, w_mix_out, w_ffn_in, w_ffn_conv, w_ffn_out) = map(np.asarray, (
         x_prompt, x_sample, cache_b_k, cache_b_v, cache_c_k, cache_c_v, cache_d_k, cache_d_v, c, c_ctx, w_mod, b_mod,
         g_mix_pre, g_mix_post, g_ffn_pre, g_ffn_post, w_in_even, w_pool, pool_scale, g_q_b, g_k_b, w_in_odd, sink_c,
         rpb_d, w_mix_out, w_ffn_in, w_ffn_conv, w_ffn_out))

    def units(w):
        k, n = w.shape
        return w.reshape(k // P, P, n // P, P).transpose(2, 1, 0, 3).reshape(n // P, P, k)

    def feature_major(t):
        return t.T.reshape(-1, P, t.shape[0]).transpose(1, 0, 2)

    def cols(vec):
        return vec.reshape(-1, P).T

    order = [0, 3, 1, 4, 2, 5, 6, 9, 7, 10, 8, 11]
    e = w_in_even[0]
    q = e[:, 256:1024].reshape(D, 12, DH)[:, order].reshape(D, 768)
    even = np.concatenate([e[:, 0:256], q, e[:, 1024:]], axis=1)
    w = w_in_odd[0]
    qc, kc, vc, qd, kd, vd = (w[:, i:j] for i, j in ((0, 512), (512, 640), (640, 768), (768, 1280), (1280, 1792),
                                                     (1792, 2304)))
    qc = qc.reshape(D, 8, DH)[:, [0, 4, 1, 5, 2, 6, 3, 7]].reshape(D, 512)
    odd = np.concatenate([qc, qd, kd, kc, vc, vd], axis=1)
    w8, w11, conv = [], [], []
    for layer, w_in in ((0, even), (1, odd)):
        gate_val = units(w_ffn_in[layer])
        gv = np.stack([gate_val[0:22], gate_val[22:44]], axis=1).reshape(44, P, D)
        down = w_ffn_out[layer].reshape(2, FH * P, D)
        w8 += [units(w_in), units(w_mix_out[layer]), gv]
        w11 += [units(down[0]), units(down[1])]
        taps = w_ffn_conv[layer].reshape(3, 2, 22, P).transpose(3, 2, 1, 0)
        conv.append(taps.reshape(P, 44, 3))

    t = np.arange(NS)
    inv_freq = 10000.0 ** (-np.arange(0, 32, 2) / 32.0)
    ang = np.concatenate([(t // 64)[:, None] * inv_freq, (t % 64)[:, None] * inv_freq], axis=-1)
    feat = np.arange(P) % DH // 2
    cos_t = np.cos(ang)[:, feat].T
    sin_t = np.sin(ang)[:, feat].T * np.where(np.arange(P) % 2 == 0, -1.0, 1.0)[:, None]
    low = -1e30
    i, j = np.arange(P)[:, None], np.arange(P)[None, :]
    before, after, zero = np.where(j >= i, 0.0, low), np.where(j <= i, 0.0, low), np.zeros((P, P))
    maskc_t = np.concatenate([before, zero, after, zero, before, zero, zero], axis=1)
    qcol, kcol = (np.arange(P) % 64)[:, None], np.arange(64)[None, :]
    start = np.clip(qcol - 8, 0, 48)
    maskd_t = np.where((kcol >= start) & (kcol < start + 16), 0.0, low)
    counts = np.zeros((2, P, NT))
    for g, win in enumerate((2, 4, 8, 16)):
        for f, n in ((0, NS), (NS, NP)):
            tt = np.arange(n)
            cnt = np.clip(tt - win // 2 + win, 0, n) - np.clip(tt - win // 2, 0, n)
            counts[g // 2, 64 * (g % 2):64 * (g % 2) + 64, f:f + n] = 1.0 / cnt
    half = np.arange(P) // 64

    padded = np.zeros((8, 17, 31 + 96), np.float32)
    padded[:, 1:16, 48:79] = rpb_d[0]
    qp = np.arange(P)
    row = 1 + np.arange(15)[None, :, None] - (qp // 64)[:, None, None]
    off = np.arange(64)[None, None, :] - (qp % 64)[:, None, None] + 15 + 48
    rpb_rows = padded[:, row, off].reshape(8, P, RPB)

    wp = np.zeros((P, 2, P), np.float32)
    for g in range(4):
        r = 64 * (g % 2)
        wp[r:r + 64, g // 2, r:r + 64] = w_pool[0, g]
    small_in = np.concatenate([cols(pool_scale[0]), np.tile(g_q_b[0], 2)[:, None], np.tile(g_k_b[0], 2)[:, None],
                               np.broadcast_to(sink_c[0], (P, 8))], axis=1)
    gains_in = np.stack([np.stack([cols(g[layer]) for g in (g_mix_pre, g_mix_post, g_ffn_pre, g_ffn_post)], axis=1)
                         for layer in range(2)], axis=1)
    tokens = np.concatenate([x_sample[0], x_prompt[0]], axis=0)
    odd_k = np.concatenate([cache_d_k[0, 0].reshape(NP, 512), cache_c_k[0, 0].reshape(NP, 128)], axis=1)
    odd_v = np.concatenate([cache_c_v[0, 0].reshape(NP, 128), cache_d_v[0, 0].reshape(NP, 512)], axis=1)
    arrays = {
        "x": feature_major(tokens).reshape(P, KD * NT),
        "w8": np.concatenate(w8, axis=0), "w11": np.concatenate(w11, axis=0),
        "wmod": w_mod.reshape(2, 4, 2, P, 12, 512).transpose(0, 4, 1, 3, 2, 5).reshape(96, P, 1024),
        "sel": np.array([[1, 0], [0, 1], [1, 0], [0, 1]]),
        "bmod": np.concatenate([cols(b_mod[0]), cols(b_mod[1])], axis=1),
        "cvec": np.stack([cols(c[0]), cols(c_ctx)], axis=2).reshape(P, 2 * KD),
        "gains": gains_in, "small": small_in, "wpool": wp, "wconv": np.concatenate(conv, axis=1),
        "kctx0": feature_major(cache_b_k[0, 0].reshape(NP, 256)), "vctx0": cache_b_v[0, 0].reshape(NP, 256),
        "kctx1": feature_major(odd_k), "vctx1": odd_v, "rpb": rpb_rows,
        "cos": cos_t, "sin": sin_t, "maskc": maskc_t, "maskd": maskd_t, "icnt": counts, "ident": np.eye(P),
        "onesd": np.full((P, P), 1.0 / D), "onesh": (half[:, None] == half[None, :]) / 64.0,
    }
    arrays = {n: np.ascontiguousarray(t, dtype=np.float32) for n, t in arrays.items()}
    shapes = {"x": (P, KD * NT), "k0": (P, 2, NP), "v0": (P, 256), "k1": (P, 5, NP), "v1": (P, NT)}

    nc = bacc.Bacc("TRN2", target_bir_lowering=False, num_devices=1)
    ins = {n: nc.dram_tensor(f"in_{n}", t.shape, F32, kind="ExternalInput").ap() for n, t in arrays.items()}
    outs = {n: nc.dram_tensor(f"out_{n}", s, F32, kind="ExternalOutput").ap() for n, s in shapes.items()}
    program(nc, ins, outs)
    r = run(nc, [{f"in_{n}": t for n, t in arrays.items()}], core_ids=[0]).results[0]

    def token_major(t):
        return t.transpose(2, 1, 0).reshape(t.shape[2], -1)

    xo = token_major(r["out_x"].reshape(P, KD, NT))
    k0, v0 = token_major(r["out_k0"]), r["out_v0"]
    k1, v1 = token_major(r["out_k1"]), r["out_v1"]
    return (xo[NS:][None], xo[:NS][None],
            k0.reshape(1, 1, NP, 4, DH), v0.reshape(1, 1, NP, 4, DH),
            k1[:, 512:].reshape(1, 1, NP, 2, DH), v1[:, :128].reshape(1, 1, NP, 2, DH),
            k1[:, :512].reshape(1, 1, NP, 8, DH), v1[:, 128:].reshape(1, 1, NP, 8, DH))
```

```python
from contextlib import ExitStack

import concourse.bass as bass
from concourse import mybir
from concourse.alu_op_type import AluOpType as ALU

F32 = mybir.dt.float32
F32R = mybir.dt.float32r
ACT = mybir.ActivationFunctionType
AX = mybir.AxisListType

P = 128
D = 1024
KD = D // P
NS = 512
NP = 128
NT = NS + NP
HT = NT // 2
DH = 64
SCALE = DH ** -0.5
EPS = 1e-6
FH = 11
PAD = 8
AW = PAD + NS + 2 * PAD + NP + PAD
AP0 = PAD + NS + 2 * PAD
UW = 1 + NS + 2 + NP + 1
UP0 = 1 + NS + 2
CW = UW - 2
CP0 = UP0 - 1
SLOT = FH * P
CTX0, PR0 = NS, NS + NP
POOL_STEPS = 18
RPB = 15 * 64

UNITS = {}
NU = 0
for _l, _in in ((0, 12), (1, 18)):
    for _kind, _count in (("in", _in), ("mix", 8), ("fin0", 22), ("fout0", 8), ("fin1", 22), ("fout1", 8)):
        UNITS[(_l, _kind)] = (NU, _count)
        NU += _count
PHASES = list(UNITS)
RUNS = [(8, 42), (FH, 8), (8, 22), (FH, 8), (8, 48), (FH, 8), (8, 22), (FH, 8)]
GROUPS = {"B": (0, 3, 0), "C": (6, 2, 48), "D": (10, 2, 80)}
JOBS = 10


class Job:

    def __init__(self, kind, step):
        self.kind, self.pair, self.half = kind, step // JOBS, step % 2
        self.t = step % JOBS // 2
        self.prompt = self.t == 4
        near = (max(self.t - 1, 0), min(self.t + 1, 3)) if kind == "C" else (0, 3)
        self.tiles = [] if self.prompt else list(range(near[0], near[1] + 1))
        self.lo = NS - P * len(self.tiles)
        self.scaled = kind != "B"
        self.split = kind != "C" and not self.prompt
        self.q0 = P * self.t
        self.vctx = 5 if self.prompt else 4
        self.kctx = PR0 if self.prompt else CTX0
        self.latent = 8 * self.pair + min(step % JOBS, 8)

    def head_col(self, it):
        if self.kind == "B":
            return DH * it + DH * (6 * self.pair + 3 * self.half)
        if self.kind == "C":
            return DH * 2 * it + DH * (self.pair + 4 * self.half)
        return 4 * DH * it + (512 + DH * (2 * self.pair + self.half))

    def v_col(self, it):
        if self.kind == "B":
            return 0 * it + P * self.pair + DH * self.half
        if self.kind == "C":
            return DH * self.half
        return 4 * DH * it + (P + DH * (2 * self.pair + self.half))

    def mask_from(self):
        return {0: P, 1: 0, 2: 0, 3: 4 * P, 4: 3 * P}[self.t]


def kchunks(phase):
    return FH if phase[1].startswith("fout") else KD


def program(nc, a, o):
    with ExitStack() as ctx:
        place = [16512]

        def at(name, shape, dt, byte):
            return nc.alloc_sbuf_tensor_at(name, shape, dt, offset=byte)

        def sb(name, shape, dt=F32):
            n = 4
            for s in shape[1:]:
                n *= s
            t = at(name, shape, dt, place[0])
            place[0] += (n + 31) // 32 * 32
            return t

        def sem(name):
            return ctx.enter_context(nc.semaphore(name))

        x = sb("x", [P, KD, NT])
        y = sb("y", [P, KD, NT])
        raw = sb("raw", [P, 2, SLOT])
        whi = sb("whi", [P, 2, SLOT], F32R)
        wlo = sb("wlo", [P, 2, SLOT], F32R)
        region_h = place[0]
        hh = sb("hh", [P, KD, NT], F32R)
        hl = sb("hl", [P, KD, NT], F32R)
        region_f = place[0]
        ffh = sb("ffh", [P, FH, NT], F32R)
        ffl = sb("ffl", [P, FH, NT], F32R)
        work = sb("work", [P, 5248])
        cos = sb("cos", [P, NS])
        sin = sb("sin", [P, NS])
        maskc = sb("maskc", [P, 7 * P])
        maskd = sb("maskd", [P, 64])
        ident = sb("ident", [P, P])
        onesd = sb("onesd", [P, P])
        hsel = sb("hsel", [P, 8, 16])
        wpool = sb("wpool", [P, 2, P])
        wconv = sb("wconv", [P, 88, 3])
        cvec = sb("cvec", [P, 2 * KD])
        csilu = sb("csilu", [P, 2 * KD])
        cst = sb("cst", [P, KD, 4], F32R)
        sel = sb("sel", [4, 2])
        bmod = sb("bmod", [P, 96])
        mod = sb("mod", [P, 2, 96, ])
        gains = sb("gains", [P, 2, 4, KD])
        coef = sb("coef", [P, 2, 2, 4, KD])
        small = sb("small", [P, 2 + 2 + 8])
        pscale = small[:, 0:2]
        gqk = small[:, 2:4]
        sink = small[:, 4:12]
        pb4 = sb("pb4", [P, NT])
        stat8 = sb("stat8", [P, 7, 2])
        assert place[0] <= 229368, place[0]
        pos = [region_h]

        def over(name, shape, dt=F32):
            n = 4
            for s in shape[1:]:
                n *= s
            t = at(name, shape, dt, pos[0])
            pos[0] += n
            return t
        qh = over("qh", [P, 2, 2, NT], F32R)
        ql = over("ql", [P, 2, 2, NT], F32R)
        kh = over("kh", [P, 2, 6 * P], F32R)
        kl = over("kl", [P, 2, 6 * P], F32R)
        pb3 = over("pb3", [P, 3, NT])
        pb = [pb3[:, 0, :], pb3[:, 1, :], pb3[:, 2, :], pb4[:, :]]
        assert pos[0] <= region_f
        pos[0] = region_h
        mh = over("mh", [P, 2, 1024], F32R)
        ml = over("ml", [P, 2, 1024], F32R)
        pos[0] = region_f
        qk = over("qk", [P, 13, 6 * P])
        v = over("v", [P, 6, NT])
        assert pos[0] <= region_f + 2 * FH * NT * 4
        osb = y[:, :, :].rearrange("p k n -> p (k n)").rearrange("p (t d) -> p t d", t=5)
        yf = y[:, :, :].rearrange("p k n -> p (k n)")

        def ring(base, n, width, where=work):
            return [where[:, base + i * width:base + (i + 1) * width] for i in range(n)]
        sq = ring(0, 2, NT)
        tn = ring(1280, 2, NT)
        hf = ring(2560, 2, NT)
        std = work[:, 3840:4480]
        rec = work[:, 4480:5120]
        ub = ring(0, 2, UW)
        cb = ring(2 * UW, 2, CW)
        sg = work[:, 2 * UW + 2 * CW:2 * UW + 3 * CW]
        fft = work[:, 2 * UW + 3 * CW:2 * UW + 3 * CW + NT]
        mraw = [work[:, i * 1024:(i + 1) * 1024] for i in range(4)]
        apad = ring(0, 2, AW)
        ptmp = ring(2 * AW, 2, AW)
        pfo = [work[:, i * AW:i * AW + NT] for i in range(2)]
        icnt = ring(4 * AW, 2, NT)
        erow = ring(0, 4, RPB)
        pts = work[:, 3968:5248].rearrange("p (s n) -> p s n", s=2)
        mrow = [yf[0:4, i * 512:(i + 1) * 512] for i in range(2)]
        fsh, ft1, ft2 = (ring(1024 * i, 2, NS, yf) for i in range(3))
        fqn = ring(3072, 2, NS, yf)
        qkf = qk[:, :, :].rearrange("p k n -> p (k n)")
        fback = qkf[0:16, 6144:6144 + 8 * P]
        fstd = qkf[0:16, 7168:7168 + NT]
        frec = qkf[0:16, 7808:7808 + NT]

        ps = ctx.enter_context(nc.psum_tensor("ps", [P, 8, 512], F32))
        psf = ps[:, :, :].rearrange("p b n -> p (b n)")
        bankA = [ps[:, 0, 0:HT], ps[:, 2, 0:HT]]
        bankB = [ps[:, 1, 0:HT], ps[:, 3, 0:HT]]
        latent = [ps[:, 0, :], ps[:, 2, :]]
        context = [ps[:, 1, 0:NP], ps[:, 3, 0:NP]]
        turned = [ps[:, 4, :], ps[:, 6, :]]
        turned_ctx = [ps[:, 5, 0:NP], ps[:, 7, 0:NP]]
        statA, statB = ps[:, 5, 0:HT], ps[:, 6, 0:HT]
        hrecA = [ps[:, 5, 0:HT], ps[:, 3, 0:HT]]
        hrecB = [ps[:, 6, 0:HT], ps[:, 4, 0:HT]]

        s_raw = [sem("weights_loaded_0"), sem("weights_loaded_1")]
        s_hi = sem("weights_hi")
        s_lo = sem("weights_lo")
        s_unit = sem("unit_multiplied")
        s_fa = sem("first_half_read")
        s_fb = sem("second_half_read")
        s_const = sem("constants_loaded")
        s_ctx = sem("cached_context_loaded")
        s_ctx1 = sem("cached_context_1_loaded")
        s_cvec = sem("c_loaded")
        s_x = sem("x_loaded")
        s_azero = sem("pool_pads_zeroed")
        s_uzero = sem("conv_pads_zeroed")
        s_csilu = sem("c_activated")
        s_mraw = [sem(f"mod_weights_loaded_{i}") for i in range(4)]
        s_cst = sem("c_split")
        s_mhi = sem("mod_weights_hi")
        s_mlo = sem("mod_weights_lo")
        s_mod = sem("mod_multiplied")
        s_mrow = sem("mod_rows_copied")
        s_mt = sem("mod_rows_turned")
        s_modb = sem("mod_biased")
        s_coef = sem("coefficients_ready")
        s_sq = sem("square_ready")
        s_stat = sem("square_summed")
        s_std = sem("deviation_ready")
        s_rec = sem("reciprocal_ready")
        s_t = sem("normed_ready")
        s_tu = sem("normed_used")
        s_hh = sem("h_hi")
        s_hl = sem("h_lo")
        s_pool = sem("pool_step")
        s_icnt = sem("pool_counts_loaded")
        s_fsq = sem("head_square")
        s_fst = sem("head_squares_summed")
        s_fstd = sem("head_deviation")
        s_frec = sem("head_reciprocal")
        s_frb = sem("head_reciprocal_spread")
        s_fn = sem("head_normed")
        s_fsh = sem("rope_swapped")
        s_ft1 = sem("rope_sin_part")
        s_ft2 = sem("rope_cos_part")
        s_fro = sem("rope_done")
        s_qzero = sem("staged_q_zeroed")
        s_kh = sem("k_hi")
        s_kl = sem("k_lo")
        s_stage = sem("pair_staged")
        s_sc = sem("scores_ready")
        s_ss = sem("scores_scaled")
        s_mx = sem("max_ready")
        s_neg = sem("neg_max_ready")
        s_es = sem("sink_exp")
        s_p = sem("exp_ready")
        s_pt = sem("probs_turned")
        s_pta = sem("turned_latent_copied")
        s_ptb = sem("turned_ctx_copied")
        s_o = sem("values_summed")
        s_den = sem("denominator_ready")
        s_rinv = sem("inverse_denominator")
        s_oe = sem("attention_out_ready")
        s_otp = sem("out_turned")
        s_pf = sem("pool_out_scaled")
        s_oth = sem("mix_in_hi")
        s_otl = sem("mix_in_lo")
        s_eload = [sem(f"bias_rows_loaded_{i}") for i in range(4)]
        s_e = sem("bias_rows_masked")
        s_c2 = sem("conv_two_taps")
        s_c1 = sem("conv_mid_tap")
        s_cv = sem("conv_done")
        s_sg = sem("gate_activated")
        s_ffm = sem("gated")
        s_ffh = sem("ff_hi")
        s_ffl = sem("ff_lo")
        s_out = sem("new_kv_stored")
        s_outx = sem("x_stored")

        block = ctx.enter_context(nc.Block())

        def slot(t, s, k):
            return t[:, s, k * P:(k + 1) * P]

        CONSTS = [("cos", cos[:, :]), ("sin", sin[:, :]), ("maskc", maskc[:, :]), ("maskd", maskd[:, :]),
                  ("ident", ident[:, :]), ("onesd", onesd[:, :]), ("hsel", hsel[:, :, :]), ("fback", fback),
                  ("wpool", wpool[:, :, :]), ("sel", sel[:, :]),
                  ("wconv", wconv[:, :, :]), ("bmod", bmod[:, :]), ("gains", gains[:, :, :, :]),
                  ("small", small[:, :])]
        n_const = len(CONSTS)

        def chunk(t, k):
            return t[:, bass.ds(k, 1), :].rearrange("p a n -> p (a n)")

        def part(t, k, f, n):
            return t[:, bass.ds(k, 1), f:f + n].rearrange("p a n -> p (a n)")

        def scores_of(job, s):
            if job.split:
                return ps[:, 2 * s:2 * s + 2, 0:HT]
            return psf[:, 1024 * s + job.lo:1024 * s + NT]

        def mod_col(layer, part, stream):
            c = 48 * layer + 8 * part
            return mod[:, stream, c:c + KD]

        SEG = ((0, 0, NS), (1, NS, NT))

        def norm_index(layer, which):
            return 4 * layer + which

        @block.sync
        def _(sp):
            w8, w11 = a["w8"], a["w11"]

            def load(src, s, width):
                return sp.dma_start(raw[:, s, 0:width], src.rearrange("a p n -> (a p) n")).then_inc(s_raw[s], 16)

            sp.dma_start(cvec[:, :], a["cvec"]).then_inc(s_cvec, 16)
            for s in range(4):
                sp.dma_start(mraw[s], a["wmod"][s]).then_inc(s_mraw[s], 16)
            for s in range(2):
                load(w8[s:s + 1], s, KD * P)
            sp.dma_start(x[:, :, :].rearrange("p k n -> p (k n)"), a["x"]).then_inc(s_x, 16)
            with sp.Fori(1, 24) as it:
                for s in range(4):
                    sp.wait_ge(s_mlo, 4 * it + s - 3)
                    sp.dma_start(mraw[s], a["wmod"][bass.ds(4 * it + s, 1)].rearrange("a p n -> (a p) n")
                                 ).then_inc(s_mraw[s], 16)
            u = 0
            base = {8: 0, FH: 0}
            for kk, n in RUNS:
                src = w8 if kk == 8 else w11
                first = 1 if u == 0 else 0
                with sp.Fori(first, n // 2) as h:
                    for s in range(2):
                        sp.wait_ge(s_lo, 2 * h + (u + s - 1))
                        load(src[bass.ds(2 * h + (base[kk] + s), 1)], s, kk * P)
                base[kk] += n
                u += n
            sp.wait_ge(s_tu, 64 + 2)
            sp.dma_start(o["x"], x[:, :, :].rearrange("p k n -> p (k n)")).then_inc(s_outx, 16)
            sp.wait_ge(s_out, 16 * 4)
            sp.wait_ge(s_outx, 16)

        @block.scalar
        def _(act):
            def hi(s, kk, pair):
                act.wait_ge(s_raw[s], 16 * pair + 16)
                act.wait_ge(s_unit, 2 * pair + (s + 1))
                nc.scalar.activation(whi[:, s, 0:kk * P], raw[:, s, 0:kk * P], ACT.Copy).then_inc(s_hi, 1)

            def pairs(phase, evac):
                u0, n = UNITS[phase]
                nxt = PHASES.index(phase) + 1
                kk = kchunks(phase)
                knext = kchunks(PHASES[nxt]) if nxt < len(PHASES) else None

                def body(h, k2):
                    for s in range(2):
                        act.wait_ge(s_unit, 2 * h + (u0 + s + 3))
                        if k2 is not None:
                            hi(s, k2, h + (u0 // 2 + 1))
                        evac(h, s, 2 * h + (u0 + s))
                return body, n // 2, kk, knext

            def run(phase, evac):
                body, n, kk, knext = pairs(phase, evac)
                if knext == kk:
                    with act.Fori(0, n) as h:
                        body(h, kk)
                else:
                    with act.Fori(0, n - 1) as h:
                        body(h, kk)
                    body(n - 1, knext)

            def copy_a(dst, s):
                nc.scalar.activation(dst, bankA[s], ACT.Copy).then_inc(s_fa, 1)

            def square(k, n, src, s):
                act.wait_ge(s_stat, k + (8 * n + 1))
                act.nop(nofuse=True)
                nc.scalar.activation(sq[s], src, ACT.Square).then_inc(s_sq, 1)

            def deviation(n):
                act.wait_ge(s_stat, 8 * n + 10)
                if n:
                    act.wait_ge(s_rec, n)
                nc.scalar.activation(std[:, 0:HT], statA, ACT.Sqrt, bias=EPS).then_inc(s_std, 1)
                nc.scalar.activation(std[:, HT:NT], statB, ACT.Sqrt, bias=EPS).then_inc(s_std, 1)

            def pre_norm(layer, which):
                n = norm_index(layer, which)
                part = 0 if which == 0 else 3
                hidx = 8 * (2 * layer + which // 2)
                deviation(n)
                with act.Fori(0, KD // 2) as h:
                    for s in range(2):
                        act.wait_ge(s_t, 2 * h + (8 * n + s + 1))
                        act.wait_ge(s_hl, 2 * h + (hidx + s + 1))
                        for st, f, t in SEG:
                            last = nc.scalar.activation(
                                hf[s][:, f:t], tn[s][:, f:t], ACT.Identity,
                                scale=coef[:, layer, st, which, bass.ds(2 * h + s, 1)],
                                bias=mod_col(layer, part, st)[:, bass.ds(2 * h + s, 1)])
                        last.then_inc(s_tu, 1)
                        act.wait_ge(s_tu, 2 * h + (8 * n + s + 3))
                        nc.scalar.activation(chunk(hh, 2 * h + s), hf[s], ACT.Copy).then_inc(s_hh, 1)

            def post_norm(layer, which, squares):
                n = norm_index(layer, which)
                deviation(n)
                if squares:
                    with act.Fori(0, 4) as h:
                        for s in range(2):
                            act.wait_ge(s_tu, 2 * h + (8 * n + s + 3))
                            square(2 * h + s, n + 1, chunk(x, 2 * h + s), s)

            act.wait_ge(s_cvec, 16)
            nc.scalar.activation(csilu[:, :], cvec[:, :], ACT.Silu).then_inc(s_csilu, 1)
            act.wait_ge(s_csilu, 1)
            nc.scalar.activation(cst[:, :, 0:2], csilu[:, :].rearrange("p (k s) -> p k s", s=2),
                                 ACT.Copy).then_inc(s_cst, 1)
            with act.Fori(0, 24) as b:
                for s in range(4):
                    act.wait_ge(s_mraw[s], 16 * b + 16)
                    act.wait_ge(s_mod, 4 * b + s + 1)
                    nc.scalar.activation(mh[:, s % 2, :], mraw[s], ACT.Copy).then_inc(s_mhi, 1)
            for s in range(2):
                hi(s, KD, 0)
            act.wait_ge(s_mlo, 96)
            act.wait_ge(s_x, 16)
            with act.Fori(0, 4) as h:
                for s in range(2):
                    square(2 * h + s, 0, chunk(x, 2 * h + s), s)
            act.wait_ge(s_coef, 16)
            pre_norm(0, 0)

            def unit_pair(pair, dsts, k2=KD):
                for s in range(2):
                    act.wait_ge(s_unit, 2 * pair + (s + 3))
                    hi(s, k2, pair + 1)
                    copy_a(dsts[s], s)

            def value_pair(pair, col):
                act.wait_ge(s_unit, 2 * pair + 4)
                for s in range(2):
                    hi(s, KD, pair + 1)
                nc.scalar.activation(v[:, 0:2, bass.ds(col, 2 * P)], ps[:, 0, :], ACT.Copy).then_inc(s_fa, 2)

            act.wait_ge(s_azero, 1)
            unit_pair(0, [apad[s][:, PAD:PAD + HT] for s in range(2)])
            with act.Fori(0, 4) as h:
                unit_pair(h + 1, [part(qk, 2 * h + s, 0, HT) for s in range(2)])
                for s in range(2):
                    act.wait_ge(s_fa, 2 * h + s + 5)
                    act.wait_ge(s_fb, 2 * h + s + 5)
                    act.nop(nofuse=True)
                    for f, src, n in ((0, 0, NS), (NS, PR0, NP)):
                        nc.scalar.activation(part(y, 2 * h + s, f, n), part(qk, 2 * h + s, src, n),
                                             ACT.Square).then_inc(s_fsq, 1)
            act.wait_ge(s_fst, 1)
            nc.scalar.activation(fstd[:, 0:HT], statA[0:16], ACT.Sqrt, bias=EPS).then_inc(s_fstd, 1)
            nc.scalar.activation(fstd[:, HT:NT], statB[0:16], ACT.Sqrt, bias=EPS).then_inc(s_fstd, 1)
            value_pair(5, 0)

            def attention(kind):
                g0, its, _ = GROUPS[kind]
                nj, jb = 2 * JOBS, JOBS * g0
                with act.Fori(0, its) as it:
                    for step in range(nj + 1):
                        if step < nj:
                            job = Job(kind, step)
                            jv = nj * it + (jb + step)
                            s = step % 2
                            act.wait_ge(s_neg, jv + 1)
                            act.wait_ge(s_pt, jv + 1)
                            act.wait_ge(s_rinv, jv + 1)
                            if kind == "C":
                                act.nop(nofuse=True)
                                head = 2 * it + (job.pair + 4 * job.half)
                                nc.scalar.activation(stat8[:, 2, s:s + 1], sink[:, bass.ds(head, 1)], ACT.Exp,
                                                     bias=stat8[:, 1, s:s + 1]).then_inc(s_es, 1)
                            dst = pb[step % 4][:, job.lo:NT]
                            src, sc = (dst, 1.0) if job.scaled else (scores_of(job, s), SCALE)
                            if job.split:
                                dst = dst.rearrange("p (b n) -> p b n", b=2)
                                src = src if not job.scaled else dst
                            nc.scalar.activation(dst, src, ACT.Exp, bias=stat8[:, 1, s:s + 1],
                                                 scale=sc, accum_out=stat8[:, 3, s:s + 1]).then_inc(s_p, 1)
                        if step >= 1:
                            job = Job(kind, step - 1)
                            jv = nj * it + (jb + step - 1)
                            if not job.prompt:
                                act.wait_ge(s_pt, jv + 3)
                                act.wait_ge(s_o, jv + 1)
                                nc.scalar.activation(pts[:, (step - 1) % 2, job.lo:NS], ps[:, 4, job.lo:NS],
                                                     ACT.Copy).then_inc(s_pta, 1)

            act.wait_ge(s_fro, 8 + 2)
            act.wait_ge(s_fn, 16)
            act.wait_ge(s_unit, 12 + 2)
            act.wait_ge(s_ctx, 32)
            for i in range(2):
                nc.scalar.activation(kh[:, i, :], qk[:, 6 + i, :], ACT.Copy).then_inc(s_kh, 1)
            act.wait_ge(s_fa, 12 + 2)
            act.wait_ge(s_fb, 12 + 2)
            act.dma_start(o["k0"], qk[:, 6:8, PR0:PR0 + NP]).then_inc(s_out, 16)
            act.dma_start(o["v0"], v[:, 5, 0:2 * P]).then_inc(s_out, 16)
            attention("B")

            def mix_in_hi(n, first_event, dst0):
                for c in range(n):
                    e = first_event + c
                    s = c % 2
                    act.wait_ge(s_otp, e + 1)
                    nc.scalar.activation(hh[:, dst0 + c, 0:NS], turned[s], ACT.Copy).then_inc(s_oth, 1)
                    nc.scalar.activation(hh[:, dst0 + c, NS:NT], turned_ctx[s], ACT.Copy).then_inc(s_oth, 1)

            for c in range(2):
                act.wait_ge(s_otp, c + 1)
                nc.scalar.activation(pfo[c][:, 0:NS], turned[c], ACT.Copy, scale=pscale[:, c:c + 1]).then_inc(s_pf, 1)
                nc.scalar.activation(pfo[c][:, NS:NT], turned_ctx[c], ACT.Copy, scale=pscale[:, c:c + 1]).then_inc(s_pf, 1)
                act.wait_ge(s_pf, 2 * c + 2)
                nc.scalar.activation(hh[:, c, :], pfo[c], ACT.Copy).then_inc(s_oth, 1)
            mix_in_hi(6, 2, 2)

            def y_phase(phase, norm, copies, squares):
                u0, n = UNITS[phase]

                def f(h, s, u):
                    if copies:
                        copy_a(part(y, 2 * h + s, 0, HT), s)
                    if squares:
                        act.wait_ge(s_fa, u + 3)
                        act.wait_ge(s_fb, u + 3)
                        square(2 * h + s, norm, chunk(y, 2 * h + s), s)
                run(phase, f)

            def ffn_half(layer, half):
                phase = (layer, f"fin{half}")
                u0 = UNITS[phase][0]
                f0 = 22 * layer + FH * half

                def f(h, s, u):
                    fp = h + f0
                    act.wait_ge(s_cv, 2 * h + (2 * f0 + s + 1))
                    copy_a(ub[s][:, 1:1 + HT], s)
                    act.wait_ge(s_fa, u + 3)
                    act.wait_ge(s_fb, u + 3)
                    if s == 0:
                        act.wait_ge(s_sg, fp + 1)
                    act.wait_ge(s_ffm, fp + 1)
                    nc.scalar.activation(cb[s], ub[s][:, 1:1 + CW], ACT.Copy,
                                         scale=wconv[:, bass.ds(2 * h + (2 * f0 + s), 1), 1]).then_inc(s_c1, 1)
                    if s == 1:
                        act.wait_ge(s_cv, 2 * h + (2 * f0 + 3))
                        nc.scalar.activation(sg, cb[0], ACT.Silu).then_inc(s_sg, 1)
                        act.wait_ge(s_ffm, fp + 2)
                        nc.scalar.activation(ffh[:, bass.ds(h, 1), :].rearrange("p a n -> p (a n)"), fft,
                                             ACT.Copy).then_inc(s_ffh, 1)
                run(phase, f)

            def ffn(layer):
                act.wait_ge(s_uzero, 6 * (layer + 1))
                act.wait_ge(s_out, 32 * (layer + 1))
                ffn_half(layer, 0)
                y_phase((layer, "fout0"), None, True, False)
                ffn_half(layer, 1)
                y_phase((layer, "fout1"), norm_index(layer, 3), False, True)

            y_phase((0, "mix"), 1, True, True)
            post_norm(0, 1, True)
            pre_norm(0, 2)
            ffn(0)
            post_norm(0, 3, True)
            pre_norm(1, 0)

            p1 = UNITS[(1, "in")][0] // 2
            with act.Fori(0, 6) as h:
                unit_pair(h + p1, [part(qk, 2 * h + s, 0, HT) for s in range(2)])
            act.wait_ge(s_unit, 2 * p1 + 12 + 3)
            hi(0, KD, p1 + 7)
            copy_a(qk[:, 12, 0:HT], 0)
            act.wait_ge(s_unit, 2 * p1 + 13 + 3)
            hi(1, KD, p1 + 7)
            nc.scalar.activation(v[:, 0:4, 0:P], latent[1], ACT.Copy).then_inc(s_fa, 1)
            with act.Fori(0, 2) as h:
                value_pair(h + (p1 + 7), 256 * h + P)
            u1 = UNITS[(1, "mix")][0]
            act.wait_ge(s_fro, 13 + 2)
            act.wait_ge(s_unit, u1 + 2)
            act.wait_ge(s_ctx1, 32)
            nc.scalar.activation(kh[:, 0, :], qk[:, 12, :], ACT.Copy).then_inc(s_kh, 1)
            act.wait_ge(s_fa, u1 + 2)
            act.wait_ge(s_fb, u1 + 2)
            act.dma_start(o["k1"], qk[:, 8:13, PR0:PR0 + NP]).then_inc(s_out, 16)
            act.dma_start(o["v1"], v[:, 5, :]).then_inc(s_out, 16)
            attention("C")
            attention("D")
            mix_in_hi(8, 8, 0)
            y_phase((1, "mix"), 5, True, True)
            post_norm(1, 1, True)
            pre_norm(1, 2)
            ffn(1)
            post_norm(1, 3, False)

        @block.vector
        def _(dve):
            V = nc.vector

            def lo(s, kk, u):
                dve.wait_ge(s_hi, u + 1)
                V.tensor_tensor(wlo[:, s, 0:kk * P], raw[:, s, 0:kk * P], whi[:, s, 0:kk * P].bitcast(F32),
                                ALU.subtract).then_inc(s_lo, 1)

            def run(phase, evac):
                u0, n = UNITS[phase]
                nxt = PHASES.index(phase) + 1
                kk = kchunks(phase)
                knext = kchunks(PHASES[nxt]) if nxt < len(PHASES) else None

                def body(h, k2):
                    for s in range(2):
                        u = 2 * h + (u0 + s)
                        dve.wait_ge(s_unit, u + 3)
                        evac(h, s, u, lambda: lo(s, k2, u + 2) if k2 is not None else None)
                if knext == kk:
                    with dve.Fori(0, n // 2) as h:
                        body(h, kk)
                else:
                    with dve.Fori(0, n // 2 - 1) as h:
                        body(h, kk)
                    body(n // 2 - 1, knext)

            def copy_b(dsts, s):
                f = 0
                for dst in dsts:
                    n = HT if len(dsts) == 1 else (NS - HT, NP)[f > 0]
                    last = V.tensor_copy(dst, bankB[s][:, f:f + n])
                    f += n
                last.then_inc(s_fb, 1)

            def unit_pair(pair, dsts, k2=KD):
                for s in range(2):
                    dve.wait_ge(s_unit, 2 * pair + (s + 3))
                    copy_b(dsts[s], s)
                    lo(s, k2, 2 * pair + (s + 2))

            def reciprocal(n):
                dve.wait_ge(s_std, 2 * n + 2)
                if n:
                    dve.wait_ge(s_t, 8 * n)
                V.reciprocal(rec, std).then_inc(s_rec, 1)

            def pre_norm(layer, which):
                n = norm_index(layer, which)
                hidx = 8 * (2 * layer + which // 2)
                reciprocal(n)
                with dve.Fori(0, KD // 2) as h:
                    for s in range(2):
                        dve.wait_ge(s_hh, 2 * h + (hidx + s + 1))
                        V.tensor_tensor(chunk(hl, 2 * h + s), hf[s], chunk(hh, 2 * h + s).bitcast(F32),
                                        ALU.subtract).then_inc(s_hl, 1)

            def post_norm(layer, which):
                n = norm_index(layer, which)
                reciprocal(n)
                with dve.Fori(0, KD // 2) as h:
                    for s in range(2):
                        dve.wait_ge(s_t, 2 * h + (8 * n + s + 1))
                        for st, f, t in SEG:
                            xs = part(x, 2 * h + s, f, t - f)
                            last = V.scalar_tensor_tensor(
                                out=xs, in0=tn[s][:, f:t], scalar=coef[:, layer, st, which, bass.ds(2 * h + s, 1)],
                                in1=xs, op0=ALU.mult, op1=ALU.add)
                        last.then_inc(s_tu, 1)

            dve.wait_ge(s_cst, 1)
            V.tensor_tensor(cst[:, :, 2:4], csilu[:, :].rearrange("p (k s) -> p k s", s=2), cst[:, :, 0:2].bitcast(F32),
                            ALU.subtract).then_inc(s_cst, 1)

            def mod_rows(n, b):
                dve.wait_ge(s_mod, 4 * n + 6)
                dve.wait_ge(s_mt, n + 1)
                V.tensor_copy(mrow[b], ps[0:4, 5 + b, :]).then_inc(s_mrow, 1)

            def mod_blocks(h, first=False):
                for b in range(2):
                    for s in range(4):
                        dve.wait_ge(s_mhi, 8 * h + (4 * b + s + 1))
                        V.tensor_tensor(ml[:, s % 2, :], mraw[s], mh[:, s % 2, :].bitcast(F32),
                                        ALU.subtract).then_inc(s_mlo, 1)
                        if s == 1 and not (first and b == 0):
                            mod_rows(2 * h + (b - 1), 1 - b)

            mod_blocks(0, True)
            with dve.Fori(1, 12) as h:
                mod_blocks(h)
            mod_rows(23, 1)
            for s in range(2):
                lo(s, KD, s)
            dve.wait_ge(s_mt, 24 + 2)
            dve.wait_ge(s_const, 16 * n_const)
            for st in range(2):
                V.tensor_tensor(mod[:, st, :], ps[:, 4, 0:192].rearrange("p (c s) -> p s c", s=2)[:, st, :], bmod[:, :],
                                ALU.add).then_inc(s_modb, 1)
            dve.wait_ge(s_modb, 2)
            for layer in range(2):
                for st in range(2):
                    for w in range(4):
                        m = mod_col(layer, (1, 2, 4, 5)[w], st)
                        V.scalar_tensor_tensor(out=coef[:, layer, st, w, :], in0=m, scalar=1.0 if w % 2 == 0 else 0.0,
                                               in1=gains[:, layer, w, :], op0=ALU.add, op1=ALU.mult).then_inc(s_coef, 1)
            pre_norm(0, 0)

            def value_pair(pair, col):
                dve.wait_ge(s_unit, 2 * pair + 4)
                V.tensor_copy(v[:, 2:4, bass.ds(col, 2 * P)], ps[:, 1, :].rearrange("p (t n) -> p t n", t=2))
                V.tensor_copy(v[:, 5, bass.ds(col, 2 * P)], ps[:, 2, 0:2 * P]).then_inc(s_fb, 2)
                for s in range(2):
                    lo(s, KD, 2 * pair + (s + 2))

            dve.wait_ge(s_azero, 1)
            unit_pair(0, [(apad[s][:, PAD + HT:PAD + NS], apad[s][:, AP0:AP0 + NP]) for s in range(2)])
            with dve.Fori(0, 4) as h:
                unit_pair(h + 1, [(part(qk, 2 * h + s, HT, NS - HT), part(qk, 2 * h + s, PR0, NP)) for s in range(2)])
            dve.wait_ge(s_fstd, 2)
            V.reciprocal(frec, fstd).then_inc(s_frec, 1)
            value_pair(5, 0)

            def head_norm(c, g, s):
                dve.wait_ge(s_frb, c + 1)
                dve.wait_ge(s_fro, c + 1)
                for f, n, rec_ in ((0, HT, hrecA[s]), (HT, NS - HT, hrecB[s][:, 0:NS - HT])):
                    last = V.scalar_tensor_tensor(out=fqn[s][:, f:f + n], in0=part(qk, c, f, n), scalar=g, in1=rec_,
                                                  op0=ALU.mult, op1=ALU.mult)
                last.then_inc(s_fn, 1)
                pr = part(qk, c, PR0, NP)
                V.scalar_tensor_tensor(out=pr, in0=pr, scalar=g, in1=hrecB[s][:, NS - HT:HT], op0=ALU.mult,
                                       op1=ALU.mult).then_inc(s_fn, 1)

            def rope_products(r, s):
                dve.wait_ge(s_fro, r + 1)
                dve.wait_ge(s_fn, 2 * r + 2)
                dve.nop(nofuse=True)
                V.stream_shuffle(fsh[s], fqn[s], [i ^ 1 for i in range(32)]).then_inc(s_fsh, 1)
                V.tensor_tensor(ft2[s], fqn[s], cos[:, :], ALU.mult).then_inc(s_ft2, 1)

            def rope_sum(c, r, s):
                dve.wait_ge(s_ft1, r + 1)
                dve.wait_ge(s_ft2, r + 1)
                V.tensor_tensor(part(qk, c, 0, NS), ft1[s], ft2[s], ALU.add).then_inc(s_fro, 1)

            def rope_pair(h, r0, norm):
                for s in range(2):
                    norm(2 * h + s, 2 * h + (r0 + s), s)
                    rope_products(2 * h + (r0 + s), s)
                for s in range(2):
                    rope_sum(2 * h + s, 2 * h + (r0 + s), s)

            with dve.Fori(0, 3) as h:
                rope_pair(h, 0, lambda c, r, s: head_norm(c, gqk[:, 0:1], s))
            rope_pair(3, 0, lambda c, r, s: head_norm(c, gqk[:, 1:2], s))

            def scale_values(job, jv, it, t):
                dve.wait_ge(s_o, jv)
                dve.wait_ge(s_rinv, jv)
                V.tensor_scalar(osb[:, job.t, bass.ds(job.head_col(it), DH)], ps[:, 6 + t, 0:DH],
                                stat8[:, 5, t:t + 1], None, ALU.mult).then_inc(s_oe, 1)

            def attention(kind):
                g0, its, _ = GROUPS[kind]
                nj, jb = 2 * JOBS, JOBS * g0
                with dve.Fori(0, its) as it:
                    for step in range(nj + 3):
                        now, last, old = (Job(kind, i) if 0 <= i < nj else None for i in (step, step - 1, step - 3))
                        jv = nj * it + (jb + step)
                        s, t = step % 2, (step - 1) % 2
                        negm = stat8[:, 1, s:s + 1]
                        sums = stat8[:, 3, t:t + 1]
                        if now:
                            dve.wait_ge(s_sc, jv + 31)
                            dve.wait_ge(s_p, jv + 1)
                            scores = scores_of(now, s)
                            if now.scaled:
                                dve.wait_ge(s_pt, jv - 1)
                                sbuf = pb[step % 4]
                                if kind == "C":
                                    m0 = now.mask_from()
                                    V.scalar_tensor_tensor(out=sbuf[:, now.lo:NT], in0=scores, scalar=SCALE,
                                                           in1=maskc[:, m0:m0 + NT - now.lo], op0=ALU.mult,
                                                           op1=ALU.add).then_inc(s_ss, 1)
                                else:
                                    if not now.prompt:
                                        e = 2 * now.pair + now.half
                                        dve.wait_ge(s_e, 4 * it + (e + 1))
                                        r0 = (7 - 2 * now.t) * 64
                                        for b, f, n in ((0, 0, HT), (1, HT, NS - HT)):
                                            V.scalar_tensor_tensor(out=sbuf[:, f:f + n], in0=ps[:, 2 * s + b, 0:n],
                                                                   scalar=SCALE, in1=erow[e][:, r0 + f:r0 + f + n],
                                                                   op0=ALU.mult, op1=ALU.add)
                                        scores = ps[:, 2 * s + 1, NS - HT:HT]
                                    V.tensor_scalar(sbuf[:, NS:NT], scores, SCALE, None, ALU.mult).then_inc(s_ss, 1)
                                scores = sbuf[:, now.lo:NT]
                        if old and kind != "B":
                            scale_values(old, jv, it, t)
                        if now:
                            if now.scaled:
                                dve.wait_ge(s_ss, jv - 60 + 3)
                            V.tensor_reduce(stat8[:, 0, s:s + 1], scores, AX.XY if now.split and not now.scaled
                                            else AX.X, ALU.max).then_inc(s_mx, 1)
                        if last and kind == "C":
                            dve.wait_ge(s_p, jv + 2)
                            V.tensor_tensor(stat8[:, 4, t:t + 1], sums, stat8[:, 2, t:t + 1],
                                            ALU.add).then_inc(s_den, 1)
                        if now:
                            dve.wait_ge(s_mx, jv + 1)
                            if kind == "C":
                                V.tensor_scalar(negm, stat8[:, 0, s:s + 1],
                                                sink[:, bass.ds(2 * it + (now.pair + 4 * now.half), 1)], -1.0,
                                                ALU.max, ALU.mult).then_inc(s_neg, 1)
                            else:
                                V.tensor_scalar(negm, stat8[:, 0, s:s + 1], -1.0 if now.scaled else -SCALE, None,
                                                ALU.mult).then_inc(s_neg, 1)
                        if old and kind == "B":
                            scale_values(old, jv, it, t)
                        if last:
                            if kind == "C":
                                dve.wait_ge(s_den, nj * it + step)
                                sums = stat8[:, 4, t:t + 1]
                            dve.wait_ge(s_p, jv + 2)
                            dve.wait_ge(s_oe, jv)
                            V.reciprocal(stat8[:, 5, t:t + 1], sums).then_inc(s_rinv, 1)
                            dve.wait_ge(s_pt, jv + 2)
                            dve.wait_ge(s_o, jv)
                            V.tensor_copy(pts[:, t, NS:NT], ps[:, 5, 0:NP]).then_inc(s_ptb, 1)

            def prepare_attention(n, slots):
                for q in (qh, ql):
                    V.memset(q[DH:P, :, 0, :].bitcast(F32), 0.0).then_inc(s_qzero, 1)
                    V.memset(q[0:DH, :, 1, :].bitcast(F32), 0.0).then_inc(s_qzero, 1)
                for i, (slot_, chunk_) in enumerate(slots):
                    dve.wait_ge(s_kh, 2 * n + i + 1)
                    V.tensor_tensor(kl[:, slot_, :], qk[:, chunk_, :], kh[:, slot_, :].bitcast(F32),
                                    ALU.subtract).then_inc(s_kl, 1)

            dve.wait_ge(s_unit, 12 + 2)
            prepare_attention(0, ((0, 6), (1, 7)))
            attention("B")

            def mix_in_lo(n, oth0, dst0):
                for c in range(n):
                    s = c % 2
                    dve.wait_ge(s_oth, oth0 + 2 * c + 2)
                    V.tensor_tensor(hl[:, dst0 + c, 0:NS], turned[s], hh[:, dst0 + c, 0:NS].bitcast(F32),
                                    ALU.subtract).then_inc(s_otl, 1)
                    V.tensor_tensor(hl[:, dst0 + c, NS:NT], turned_ctx[s], hh[:, dst0 + c, NS:NT].bitcast(F32),
                                    ALU.subtract).then_inc(s_otl, 1)

            for c in range(2):
                dve.wait_ge(s_oth, c + 1)
                V.tensor_tensor(hl[:, c, :], pfo[c], hh[:, c, :].bitcast(F32), ALU.subtract).then_inc(s_otl, 1)
            mix_in_lo(6, 2, 2)

            def y_phase(phase, add):
                u0, n = UNITS[phase]
                if add:
                    dve.wait_ge(s_fa, u0 + 2)
                    dve.wait_ge(s_fb, u0 + 2)

                def f(h, s, u, split):
                    if add:
                        ya = part(y, 2 * h + s, 0, HT)
                        yb = part(y, 2 * h + s, HT, HT)
                        V.tensor_tensor(ya, bankA[s], ya, ALU.add).then_inc(s_fa, 1)
                        V.tensor_tensor(yb, bankB[s], yb, ALU.add).then_inc(s_fb, 1)
                    else:
                        copy_b([part(y, 2 * h + s, HT, HT)], s)
                    split()
                run(phase, f)

            def ffn_half(layer, half):
                f0 = 22 * layer + FH * half

                def f(h, s, u, split):
                    fp = h + f0
                    cu = 2 * h + (2 * f0 + s)
                    dve.wait_ge(s_cv, cu + 1)
                    copy_b([ub[s][:, 1 + HT:1 + NS], ub[s][:, UP0:UP0 + NP]], s)
                    split()
                    dve.wait_ge(s_c1, cu + 1)
                    V.scalar_tensor_tensor(out=cb[s], in0=ub[s][:, 0:CW], scalar=wconv[:, bass.ds(cu, 1), 0], in1=cb[s],
                                           op0=ALU.mult, op1=ALU.add).then_inc(s_c2, 1)
                    dve.wait_ge(s_c2, cu + 1)
                    V.scalar_tensor_tensor(out=cb[s], in0=ub[s][:, 2:UW], scalar=wconv[:, bass.ds(cu, 1), 2], in1=cb[s],
                                           op0=ALU.mult, op1=ALU.add).then_inc(s_cv, 1)
                    if s == 1:
                        dve.wait_ge(s_cv, cu + 3)
                        dve.wait_ge(s_sg, fp + 2)
                        dve.wait_ge(s_ffl, fp + 1)
                        V.tensor_tensor(fft[:, 0:NS], sg[:, 0:NS], cb[1][:, 0:NS], ALU.mult)
                        V.tensor_tensor(fft[:, NS:NT], sg[:, CP0:CW], cb[1][:, CP0:CW], ALU.mult).then_inc(s_ffm, 1)
                        dve.wait_ge(s_ffh, fp + 1)
                        V.tensor_tensor(chunk(ffl, h), fft, chunk(ffh, h).bitcast(F32), ALU.subtract).then_inc(s_ffl, 1)
                run((layer, f"fin{half}"), f)

            def ffn(layer):
                dve.wait_ge(s_hl, 8 * (2 * layer + 2) + 2)
                for s in range(2):
                    for f, n in ((0, 1), (1 + NS, 2), (UW - 1, 1)):
                        V.memset(ub[s][:, f:f + n], 0.0).then_inc(s_uzero, 1)
                dve.wait_ge(s_uzero, 6 * (layer + 1))
                dve.wait_ge(s_out, 32 * (layer + 1))
                ffn_half(layer, 0)
                y_phase((layer, "fout0"), False)
                ffn_half(layer, 1)
                y_phase((layer, "fout1"), True)

            y_phase((0, "mix"), False)
            post_norm(0, 1)
            pre_norm(0, 2)
            ffn(0)
            post_norm(0, 3)
            pre_norm(1, 0)
            p1 = UNITS[(1, "in")][0] // 2

            def take_plain(c, r, s):
                dve.wait_ge(s_fa, c + (2 * p1 + 3))
                dve.wait_ge(s_fb, c + (2 * p1 + 3))
                dve.wait_ge(s_fro, r + 1)
                V.tensor_copy(fqn[s], part(qk, c, 0, NS)).then_inc(s_fn, 2)

            def qk_pair(h, first):
                unit_pair(h + (p1 + first // 2), [(part(qk, 2 * h + (first + s), HT, NS - HT),
                                                   part(qk, 2 * h + (first + s), PR0, NP)) for s in range(2)])

            with dve.Fori(0, 2) as h:
                qk_pair(h, 0)
                rope_pair(h, 8, take_plain)
            with dve.Fori(0, 4) as h:
                qk_pair(h, 4)
            dve.wait_ge(s_unit, 2 * p1 + 12 + 3)
            copy_b((qk[:, 12, HT:NS], qk[:, 12, PR0:PR0 + NP]), 0)
            lo(0, KD, 2 * p1 + 14)
            dve.wait_ge(s_unit, 2 * p1 + 13 + 3)
            V.tensor_copy(v[:, 5, 0:P], context[1]).then_inc(s_fb, 1)
            lo(1, KD, 2 * p1 + 15)
            take_plain(12, 12, 0)
            rope_products(12, 0)
            rope_sum(12, 12, 0)
            with dve.Fori(0, 2) as h:
                value_pair(h + (p1 + 7), 256 * h + P)
            dve.wait_ge(s_unit, UNITS[(1, "mix")][0] + 2)
            prepare_attention(1, ((0, 12),))
            attention("C")
            attention("D")
            mix_in_lo(8, 14, 0)
            y_phase((1, "mix"), False)
            post_norm(1, 1)
            pre_norm(1, 2)
            ffn(1)
            post_norm(1, 3)

        @block.gpsimd
        def _(pool):
            G = nc.gpsimd

            def scale_rows(n, src):
                pool.wait_ge(s_rec, n + 1)
                with pool.Fori(0, KD // 2) as h:
                    for s in range(2):
                        pool.wait_ge(s_tu, 2 * h + (8 * n + s + 1))
                        G.tensor_tensor(tn[s], chunk(src, 2 * h + s), rec, ALU.mult).then_inc(s_t, 1)

            def rope_sin(pairs, r0):
                with pool.Fori(0, pairs) as h:
                    for s in range(2):
                        pool.wait_ge(s_fsh, 2 * h + (r0 + s + 1))
                        G.tensor_tensor(ft1[s], fsh[s], sin[:, :], ALU.mult).then_inc(s_ft1, 1)

            def stage_k(slot_, chunk_, before):
                G.tensor_copy(kh[:, slot_, :], chunk(qk, chunk_)).then_inc(s_stage, 1)
                pool.wait_ge(s_stage, before + 1)
                G.tensor_tensor(kl[:, slot_, :], chunk(qk, chunk_), kh[:, slot_, :].bitcast(F32),
                                ALU.subtract).then_inc(s_stage, 1)

            def stage(kind, it, i):
                g0, _, st0 = GROUPS[kind]
                copies = 10 if kind == "D" else 8
                before = 2 * copies * it + (st0 + copies * i)
                qc = {"B": it + 3 * i, "C": 2 * it + i, "D": 2 * it + (4 + i)}[kind]
                pool.wait_ge(s_sc, 2 * JOBS * it + (JOBS * (g0 + i - 1) + 30))
                if kind == "D":
                    pool.wait_ge(s_stage, before)
                    stage_k(i, 2 * it + (8 + i), before)
                    before = before + 2
                    pool.wait_ge(s_stage, before)
                pieces = [(slice(DH * half, DH * half + DH), half, f, src, w)
                          for half in range(2) for f, src, w in ((0, 0, NS), (NS, PR0, NP))]
                for rows, half, f, src, w in pieces:
                    G.tensor_copy(qh[rows, i, half, f:f + w], qk[rows, bass.ds(qc, 1), src:src + w].rearrange(
                        "p a n -> p (a n)")).then_inc(s_stage, 1)
                pool.wait_ge(s_stage, before + 4)
                pool.nop(nofuse=True)
                for rows, half, f, src, w in pieces:
                    G.tensor_tensor(ql[rows, i, half, f:f + w], qk[rows, bass.ds(qc, 1), src:src + w].rearrange(
                        "p a n -> p (a n)"), qh[rows, i, half, f:f + w].bitcast(F32),
                        ALU.subtract).then_inc(s_stage, 1)

            for name, dst in CONSTS:
                pool.dma_start(dst, a[name]).then_inc(s_const, 16)
            pool.dma_start(qk[:, 6:8, CTX0:PR0], a["kctx0"]).then_inc(s_ctx, 16)
            pool.dma_start(v[:, 4, 0:2 * P], a["vctx0"]).then_inc(s_ctx, 16)
            scale_rows(0, x)
            pool.wait_ge(s_hl, 8 + 2)
            G.memset(work[:, 0:2 * AW], 0.0).then_inc(s_azero, 1)
            for c in range(2):
                pool.dma_start(icnt[c], a["icnt"][c]).then_inc(s_icnt, 16)
            pool.wait_ge(s_icnt, 32)
            steps = [0]

            def step(ins):
                steps[0] += 1
                ins.then_inc(s_pool, 1)
                pool.wait_ge(s_pool, steps[0])

            for c in range(2):
                pool.wait_ge(s_fa, c + 3)
                pool.wait_ge(s_fb, c + 3)
                t0, t1 = ptmp
                step(G.tensor_tensor(t0[:, 1:AW], apad[c][:, 0:AW - 1], apad[c][:, 1:AW], ALU.add))
                if c == 1:
                    step(G.tensor_tensor(t1[:, 2:AW - 1], t0[:, 1:AW - 2], t0[:, 3:AW], ALU.add))
                    step(G.tensor_tensor(t0[:, 4:AW - 3], t1[:, 2:AW - 5], t1[:, 6:AW - 1], ALU.add))
                w = 1 << (2 * c)
                lo_edge, hi_edge = 2 * w, AW - 2 * w + 1
                step(G.tensor_tensor(t1[64:P, lo_edge:hi_edge], t0[64:P, lo_edge - w:hi_edge - w],
                                     t0[64:P, lo_edge + w:hi_edge + w], ALU.add))
                for f, src, n in ((0, PAD, NS), (NS, AP0, NP)):
                    for rows, t in ((slice(0, 64), t0), (slice(64, P), t1)):
                        step(G.tensor_tensor(icnt[c][rows, f:f + n], t[rows, src:src + n], icnt[c][rows, f:f + n],
                                             ALU.mult))
                    step(G.tensor_tensor(icnt[c][:, f:f + n], icnt[c][:, f:f + n], apad[c][:, src:src + n],
                                         ALU.subtract))
            assert steps[0] == POOL_STEPS
            rope_sin(4, 0)
            pool.wait_ge(s_fro, 8 + 2)
            pool.wait_ge(s_fn, 16)
            pool.wait_ge(s_unit, 12 + 2)
            with pool.Fori(0, 3) as it:
                for i in range(2):
                    stage("B", it, i)
            pool.wait_ge(s_stage, 48)
            scale_rows(1, y)
            scale_rows(2, x)
            scale_rows(3, y)
            scale_rows(4, x)
            pool.wait_ge(s_unit, UNITS[(1, "in")][0] + 2)
            pool.dma_start(qk[:, 8:13, CTX0:PR0], a["kctx1"]).then_inc(s_ctx1, 16)
            pool.dma_start(v[:, 4, :], a["vctx1"]).then_inc(s_ctx1, 16)
            pool.wait_ge(s_hl, 24 + 2)

            def load_bias(e, head):
                pool.dma_start(erow[e], a["rpb"][head]).then_inc(s_eload[e], 16)

            def mask_bias(e, n):
                pool.wait_ge(s_eload[e], 16 * n)
                r = erow[e].rearrange("p (r c) -> p r c", c=64)
                G.tensor_tensor(r, r, maskd[:, :].unsqueeze(1).to_broadcast([P, 15, 64]), ALU.add).then_inc(s_e, 1)

            for e in range(4):
                load_bias(e, e)
            rope_sin(2, 8)
            pool.wait_ge(s_fsh, 13)
            G.tensor_tensor(ft1[0], fsh[0], sin[:, :], ALU.mult).then_inc(s_ft1, 1)
            pool.wait_ge(s_fro, 13 + 2)
            pool.wait_ge(s_unit, UNITS[(1, "mix")][0] + 2)
            with pool.Fori(0, 2) as it:
                for i in range(2):
                    stage("C", it, i)
            pool.wait_ge(s_stage, 80)
            for e in range(4):
                mask_bias(e, 1)
            pool.wait_ge(s_sc, JOBS * 10 + 30)
            for i in range(2):
                stage("D", 0, i)
            for i in range(2):
                pool.wait_ge(s_neg, JOBS * (10 + i + 1))
                for half in range(2):
                    load_bias(2 * i + half, 4 + 2 * i + half)
                stage("D", 1, i)
                pool.wait_ge(s_stage, 80 + 10 * (3 + i))
                for half in range(2):
                    mask_bias(2 * i + half, 2)
            scale_rows(5, y)
            scale_rows(6, x)
            scale_rows(7, y)

        @block.tensor
        def _(pe):
            T = nc.tensor
            for s, credit in ((s_unit, 2), (s_fa, 2), (s_fb, 2), (s_mod, 2), (s_mt, 2), (s_stat, 2), (s_tu, 2), (s_hl, 2),
                              (s_fro, 2), (s_sc, 30), (s_ss, 2), (s_p, 2), (s_pt, 2),
                              (s_pta, 1), (s_ptb, 1), (s_o, 2), (s_rinv, 2), (s_oe, 2), (s_cv, 2), (s_sg, 1),
                              (s_ffm, 1), (s_ffl, 1)):
                pe.sem_inc(s, credit)

            def unit(s, u, kk, hi, lo):
                pe.wait_ge(s_lo, u + 1)
                pe.wait_ge(s_fa, u + 1)
                pe.wait_ge(s_fb, u + 1)
                for k in range(kk):
                    for n, (w, h) in enumerate(((whi, hi), (whi, lo), (wlo, hi))):
                        st, sp_ = k == 0 and n == 0, k == kk - 1 and n == 2
                        T.matmul(bankA[s], slot(w, s, k), h[:, k, 0:HT], start=st, stop=sp_)
                        last = T.matmul(bankB[s], slot(w, s, k), h[:, k, HT:NT], start=st, stop=sp_)
                last.then_inc(s_unit, 1)

            def first_down(u, f0):
                pe.wait_ge(s_lo, u + 1)
                pe.wait_ge(s_fa, u + 1)
                pe.wait_ge(s_fb, u + 1)
                for k in range(FH):
                    pe.wait_ge(s_ffl, f0 + k + 2)
                    for n, (w, h) in enumerate(((whi, ffh), (whi, ffl), (wlo, ffh))):
                        st, sp_ = k == 0 and n == 0, k == FH - 1 and n == 2
                        T.matmul(bankA[0], slot(w, 0, k), h[:, k, 0:HT], start=st, stop=sp_)
                        last = T.matmul(bankB[0], slot(w, 0, k), h[:, k, HT:NT], start=st, stop=sp_)
                last.then_inc(s_unit, 1)

            def unit_v(s, u):
                pe.wait_ge(s_lo, u + 1)
                pe.wait_ge(s_fa, u + 1)
                pe.wait_ge(s_fb, u + 1)
                for t in range(5):
                    out = latent[s][:, t * P:(t + 1) * P] if t < 4 else context[s]
                    for k in range(KD):
                        for n, (w, h) in enumerate(((whi, hh), (whi, hl), (wlo, hh))):
                            last = T.matmul(out, h[:, k, t * P:(t + 1) * P], slot(w, s, k),
                                            start=k == 0 and n == 0, stop=k == KD - 1 and n == 2)
                last.then_inc(s_unit, 1)

            def pair_v(u):
                pe.wait_ge(s_lo, u + 2)
                pe.wait_ge(s_fa, u + 2)
                pe.wait_ge(s_fb, u + 2)
                for t in range(5):
                    out = ps[:, t // 2, t % 2 * 2 * P:(t % 2 + 1) * 2 * P].rearrange("p (a n) -> p a n", a=2)
                    for k in range(KD):
                        for n, (w, h) in enumerate(((whi, hh), (whi, hl), (wlo, hh))):
                            last = T.matmul(out, h[:, k, t * P:(t + 1) * P], w[:, :, k * P:(k + 1) * P],
                                            start=k == 0 and n == 0, stop=k == KD - 1 and n == 2)
                last.then_inc(s_unit, 2)

            def dense(s, u):
                unit(s, u, KD, hh, hl)

            def stat(n, k, s):
                first, last = (k == 0, k == KD - 1) if isinstance(k, int) else (False, False)
                if first and n:
                    pe.wait_ge(s_std, 2 * n)
                pe.wait_ge(s_sq, k + (8 * n + 1))
                T.matmul(statA, onesd[:, :], sq[s][:, 0:HT], start=first, stop=last)
                T.matmul(statB, onesd[:, :], sq[s][:, HT:NT], start=first, stop=last).then_inc(s_stat, 1)

            pe.wait_ge(s_cst, 2)
            def mod_turn(n, b):
                pe.wait_ge(s_mrow, n + 1)
                for j in range(4):
                    last = T.matmul(ps[:, 4, bass.ds(8 * n + 2 * j, 2)], mrow[b][:, j * P:(j + 1) * P],
                                    sel[:, :], start=True, stop=True)
                last.then_inc(s_mt, 1)

            def mod_blocks(h, first=False):
                for b in range(2):
                    for s in range(4):
                        pe.wait_ge(s_mlo, 8 * h + (4 * b + s + 1))
                        for kk in range(2):
                            k = 2 * s + kk
                            T.matmul(ps[0:4, 5 + b, :], cst[:, k, :], mh[:, s % 2, kk * 512:(kk + 1) * 512],
                                     start=k == 0, stop=False)
                            last = T.matmul(ps[0:4, 5 + b, :], cst[:, k, :], ml[:, s % 2, kk * 512:(kk + 1) * 512],
                                            start=False, stop=k == KD - 1)
                        last.then_inc(s_mod, 1)
                        if first and b == 0 and s == 3:
                            pe.wait_ge(s_const, 16 * n_const)
                        if s == 2 and not (first and b == 0):
                            mod_turn(2 * h + (b - 1), 1 - b)

            mod_blocks(0, True)
            with pe.Fori(1, 12) as h:
                mod_blocks(h)
            mod_turn(23, 1)
            for k in range(KD):
                stat(0, k, k % 2)

            def dense_pairs(u0, n):
                with pe.Fori(0, n) as h:
                    for s in range(2):
                        dense(s, 2 * h + (u0 + s))

            def pair_chunk(k):
                for s in range(2):
                    for n, (w, h) in enumerate(((whi, hh), (whi, hl), (wlo, hh))):
                        st, sp_ = k == 0 and n == 0, k == KD - 1 and n == 2
                        T.matmul(bankA[s], slot(w, s, k), h[:, k, 0:HT], start=st, stop=sp_)
                        last = T.matmul(bankB[s], slot(w, s, k), h[:, k, HT:NT], start=st, stop=sp_)
                    if k == KD - 1:
                        last.then_inc(s_unit, 1)

            def first_pair(u0, hl0):
                pe.wait_ge(s_lo, u0 + 2)
                pe.wait_ge(s_fa, u0 + 2)
                pe.wait_ge(s_fb, u0 + 2)
                for k in range(KD):
                    pe.wait_ge(s_hl, hl0 + k + 3)
                    pair_chunk(k)

            first_pair(0, 0)
            dense_pairs(2, 4)
            pe.wait_ge(s_fsq, 2 * 8)
            for c in range(8):
                T.matmul(statA[0:16], hsel[:, c, :], y[:, c, 0:HT], start=c == 0, stop=c == 7)
                last = T.matmul(statB[0:16], hsel[:, c, :], y[:, c, HT:NT], start=c == 0, stop=c == 7)
            last.then_inc(s_fst, 1)
            pair_v(10)
            pe.wait_ge(s_frec, 1)
            for c in range(8):
                if c >= 2:
                    pe.wait_ge(s_fn, 2 * (c - 1))
                s = c % 2
                T.matmul(hrecA[s], fback[:, c * P:(c + 1) * P], frec[:, 0:HT], start=True, stop=True)
                T.matmul(hrecB[s], fback[:, c * P:(c + 1) * P], frec[:, HT:NT], start=True, stop=True).then_inc(s_frb, 1)

            def attention(kind):
                g0, its, st0 = GROUPS[kind]
                nj, jb = 2 * JOBS, JOBS * g0
                copies = 10 if kind == "D" else 8
                ahead = 1 if kind == "B" else 2
                with pe.Fori(0, its) as it:
                    for step in range(-ahead, nj + 1):
                        if step + ahead < nj:
                            job = Job(kind, step + ahead)
                            s = (step + ahead) % 2
                            jv = nj * it + (jb + step + ahead)
                            if (step + ahead) % JOBS == 0:
                                pe.wait_ge(s_stage, 2 * copies * it + (st0 + copies * (job.pair + 1)))
                            if job.scaled:
                                pe.wait_ge(s_ss, jv - 60 + 1)
                            else:
                                pe.wait_ge(s_p, jv + 1)
                            kslot = 0 if kind == "C" else job.pair
                            if job.split:
                                runs = [(ps[:, 2 * s, 0:HT], 0, HT), (ps[:, 2 * s + 1, 0:HT], HT, HT)]
                            else:
                                runs = [(psf[:, 1024 * s + NS:1024 * s + NT], job.kctx, P)]
                                if not job.prompt:
                                    runs.append((psf[:, 1024 * s + job.lo:1024 * s + NS], job.tiles[0] * P,
                                                 NS - job.lo))
                            for n, (q, k) in enumerate(((qh, kh), (qh, kl), (ql, kh))):
                                for out, k0, w in runs:
                                    last = T.matmul(out, q[:, job.pair, job.half, job.q0:job.q0 + P],
                                                    k[:, kslot, k0:k0 + w], start=n == 0, stop=n == 2)
                            last.then_inc(s_sc, 1)
                        if 0 <= step < nj:
                            job = Job(kind, step)
                            s = step % 2
                            jv = nj * it + (jb + step)
                            pe.wait_ge(s_p, jv + 3)
                            pe.wait_ge(s_ptb, jv + 1)
                            if not job.prompt:
                                pe.wait_ge(s_pta, 16 * it + (8 * g0 + job.latent + 1))
                                for c in range(job.lo, NS, P):
                                    T.transpose(ps[:, 4, c:c + P], pb[step % 4][:, c:c + P], ident[:, :])
                            T.transpose(ps[:, 5, 0:P], pb[step % 4][:, NS:NT], ident[:, :]).then_inc(s_pt, 1)
                        if step >= 1:
                            job = Job(kind, step - 1)
                            s = (step - 1) % 2
                            jv = nj * it + (jb + step - 1)
                            pe.wait_ge(s_ptb, jv + 2)
                            if not job.prompt:
                                pe.wait_ge(s_pta, 16 * it + (8 * g0 + job.latent + 2))
                            pe.wait_ge(s_oe, jv + 1)
                            keys = [(job.lo + P * i, t) for i, t in enumerate(job.tiles)] + [(NS, job.vctx)]
                            for i, (c, t) in enumerate(keys):
                                last = T.matmul(ps[:, 6 + s, 0:DH], pts[:, s, c:c + P],
                                                v[:, t, bass.ds(job.v_col(it), DH)], start=i == 0,
                                                stop=i == len(keys) - 1)
                            last.then_inc(s_o, 1)

            pe.wait_ge(s_qzero, 4)
            pe.wait_ge(s_kl, 2)
            attention("B")

            def turn(n, otl0, u0, ready):
                for c in range(n + 2):
                    s = c % 2
                    if 2 <= c < n:
                        pe.wait_ge(s_otl, otl0 + 2 * (c - 1))
                    if c < n:
                        for t in range(5):
                            out = turned[s][:, t * P:(t + 1) * P] if t < 4 else turned_ctx[s]
                            last = T.transpose(out, osb[:, t, c * P:(c + 1) * P], ident[:, :])
                        last.then_inc(s_otp, 1)
                    k = c + KD - n - 2
                    if k == 0:
                        pe.wait_ge(s_lo, u0 + 2)
                        pe.wait_ge(s_fa, u0 + 2)
                        pe.wait_ge(s_fb, u0 + 2)
                    if k >= 0:
                        pe.wait_ge(s_otl, ready(k))
                        pair_chunk(k)

            pe.wait_ge(s_pool, POOL_STEPS)
            pe.wait_ge(s_oe, 60 + 2)
            for c in range(2):
                T.matmul(turned[c], wpool[:, c, :], icnt[c][:, 0:NS], start=True, stop=True)
                T.matmul(turned_ctx[c], wpool[:, c, :], icnt[c][:, NS:NT], start=True, stop=True).then_inc(s_otp, 1)
            pe.wait_ge(s_pf, 4)
            turn(6, 2, UNITS[(0, "mix")][0], lambda k: k + 1 if k < 2 else 2 * k)

            def y_units(phase, n):
                u0, _ = UNITS[phase]

                def one(h, s):
                    if phase[1] == "mix":
                        dense(s, 2 * h + (u0 + s))
                    else:
                        unit(s, 2 * h + (u0 + s), FH, ffh, ffl)

                if phase[1] != "mix":
                    first_down(u0, 22 * phase[0] + FH)
                    one(0, 1)
                stat(n, 0, 0)
                with pe.Fori(1, 3) as h:
                    one(h, 0)
                    stat(n, 2 * h - 1, 1)
                    one(h, 1)
                    stat(n, 2 * h, 0)
                one(3, 0)
                stat(n, 5, 1)
                one(3, 1)
                stat(n, 6, 0)
                stat(n, 7, 1)

            def ffn(layer):
                for half in range(2):
                    u0 = UNITS[(layer, f"fin{half}")][0]
                    if half == 0:
                        first_pair(u0, 8 * (2 * layer + 1))
                        dense_pairs(u0 + 2, FH - 1)
                    else:
                        dense_pairs(u0, FH)
                    f0 = 22 * layer + FH * half
                    if half == 0:
                        u0, n = UNITS[(layer, "fout0")]
                        first_down(u0, f0)
                        unit(1, u0 + 1, FH, ffh, ffl)
                        with pe.Fori(1, n // 2) as h:
                            for s in range(2):
                                unit(s, 2 * h + (u0 + s), FH, ffh, ffl)
                    else:
                        y_units((layer, "fout1"), norm_index(layer, 3))

            def stats(n):
                for k in range(KD):
                    stat(n, k, k % 2)

            y_units((0, "mix"), 1)
            stats(2)
            ffn(0)
            stats(4)
            u1 = UNITS[(1, "in")][0]
            first_pair(u1, 16)
            dense_pairs(u1 + 2, 5)
            dense(0, u1 + 12)
            unit_v(1, u1 + 13)
            with pe.Fori(0, 2) as h:
                pair_v(2 * h + (u1 + 14))
            pe.wait_ge(s_p, 60 + 2)
            pe.wait_ge(s_qzero, 8)
            pe.wait_ge(s_kl, 3)
            attention("C")
            attention("D")
            pe.wait_ge(s_oe, 140 + 2)
            turn(8, 14, UNITS[(1, "mix")][0], lambda k: 14 + 2 * (k + 1))
            y_units((1, "mix"), 5)
            stats(6)
            ffn(1)


def kernel(x_prompt, x_sample, cache_b_k, cache_b_v, cache_c_k, cache_c_v, cache_d_k, cache_d_v,
           c, c_ctx, w_mod, b_mod, g_mix_pre, g_mix_post, g_ffn_pre, g_ffn_post,
           w_in_even, w_pool, pool_scale, g_q_b, g_k_b, w_in_odd, sink_c, rpb_d,
           w_mix_out, w_ffn_in, w_ffn_conv, w_ffn_out):
    import numpy as np
    import concourse.bacc as bacc
    from concourse.bass_utils import run_bass_kernel_spmd as run

    (x_prompt, x_sample, cache_b_k, cache_b_v, cache_c_k, cache_c_v, cache_d_k, cache_d_v, c, c_ctx, w_mod, b_mod,
     g_mix_pre, g_mix_post, g_ffn_pre, g_ffn_post, w_in_even, w_pool, pool_scale, g_q_b, g_k_b, w_in_odd, sink_c,
     rpb_d, w_mix_out, w_ffn_in, w_ffn_conv, w_ffn_out) = map(np.asarray, (
         x_prompt, x_sample, cache_b_k, cache_b_v, cache_c_k, cache_c_v, cache_d_k, cache_d_v, c, c_ctx, w_mod, b_mod,
         g_mix_pre, g_mix_post, g_ffn_pre, g_ffn_post, w_in_even, w_pool, pool_scale, g_q_b, g_k_b, w_in_odd, sink_c,
         rpb_d, w_mix_out, w_ffn_in, w_ffn_conv, w_ffn_out))

    def units(w):
        k, n = w.shape
        return w.reshape(k // P, P, n // P, P).transpose(2, 1, 0, 3).reshape(n // P, P, k)

    def feature_major(t):
        return t.T.reshape(-1, P, t.shape[0]).transpose(1, 0, 2)

    def cols(vec):
        return vec.reshape(-1, P).T

    order = [0, 3, 1, 4, 2, 5, 6, 9, 7, 10, 8, 11]
    e = w_in_even[0]
    q = e[:, 256:1024].reshape(D, 12, DH)[:, order].reshape(D, 768)
    even = np.concatenate([e[:, 0:256], q, e[:, 1024:]], axis=1)
    w = w_in_odd[0]
    qc, kc, vc, qd, kd, vd = (w[:, i:j] for i, j in ((0, 512), (512, 640), (640, 768), (768, 1280), (1280, 1792),
                                                     (1792, 2304)))
    qc = qc.reshape(D, 8, DH)[:, [0, 4, 1, 5, 2, 6, 3, 7]].reshape(D, 512)
    odd = np.concatenate([qc, qd, kd, kc, vc, vd], axis=1)
    w8, w11, conv = [], [], []
    for layer, w_in in ((0, even), (1, odd)):
        gate_val = units(w_ffn_in[layer])
        gv = np.stack([gate_val[0:22], gate_val[22:44]], axis=1).reshape(44, P, D)
        down = w_ffn_out[layer].reshape(2, FH * P, D)
        w8 += [units(w_in), units(w_mix_out[layer]), gv]
        w11 += [units(down[0]), units(down[1])]
        taps = w_ffn_conv[layer].reshape(3, 2, 22, P).transpose(3, 2, 1, 0)
        conv.append(taps.reshape(P, 44, 3))

    t = np.arange(NS)
    inv_freq = 10000.0 ** (-np.arange(0, 32, 2) / 32.0)
    ang = np.concatenate([(t // 64)[:, None] * inv_freq, (t % 64)[:, None] * inv_freq], axis=-1)
    feat = np.arange(P) % DH // 2
    cos_t = np.cos(ang)[:, feat].T
    sin_t = np.sin(ang)[:, feat].T * np.where(np.arange(P) % 2 == 0, -1.0, 1.0)[:, None]
    low = -1e30
    i, j = np.arange(P)[:, None], np.arange(P)[None, :]
    before, after, zero = np.where(j >= i, 0.0, low), np.where(j <= i, 0.0, low), np.zeros((P, P))
    maskc_t = np.concatenate([before, zero, after, zero, before, zero, zero], axis=1)
    qcol, kcol = (np.arange(P) % 64)[:, None], np.arange(64)[None, :]
    start = np.clip(qcol - 8, 0, 48)
    maskd_t = np.where((kcol >= start) & (kcol < start + 16), 0.0, low)
    counts = np.zeros((2, P, NT))
    for g, win in enumerate((2, 4, 8, 16)):
        for f, n in ((0, NS), (NS, NP)):
            tt = np.arange(n)
            cnt = np.clip(tt - win // 2 + win, 0, n) - np.clip(tt - win // 2, 0, n)
            counts[g // 2, 64 * (g % 2):64 * (g % 2) + 64, f:f + n] = 1.0 / cnt
    pair, half = np.arange(8)[None, :, None], np.arange(P)[:, None, None] // 64
    hsel_t = (2 * pair + half == np.arange(16)[None, None, :])
    fback_t = hsel_t.transpose(2, 1, 0).reshape(16, 8 * P)

    padded = np.zeros((8, 17, 31 + 96), np.float32)
    padded[:, 1:16, 48:79] = rpb_d[0]
    qp = np.arange(P)
    row = 1 + np.arange(15)[None, :, None] - (qp // 64)[:, None, None]
    off = np.arange(64)[None, None, :] - (qp % 64)[:, None, None] + 15 + 48
    rpb_rows = padded[:, row, off].reshape(8, P, RPB)

    wp = np.zeros((P, 2, P), np.float32)
    for g in range(4):
        r = 64 * (g % 2)
        wp[r:r + 64, g // 2, r:r + 64] = w_pool[0, g]
    small_in = np.concatenate([cols(pool_scale[0]), np.tile(g_q_b[0], 2)[:, None], np.tile(g_k_b[0], 2)[:, None],
                               np.broadcast_to(sink_c[0], (P, 8))], axis=1)
    gains_in = np.stack([np.stack([cols(g[layer]) for g in (g_mix_pre, g_mix_post, g_ffn_pre, g_ffn_post)], axis=1)
                         for layer in range(2)], axis=1)
    tokens = np.concatenate([x_sample[0], x_prompt[0]], axis=0)
    odd_k = np.concatenate([cache_d_k[0, 0].reshape(NP, 512), cache_c_k[0, 0].reshape(NP, 128)], axis=1)
    odd_v = np.concatenate([cache_c_v[0, 0].reshape(NP, 128), cache_d_v[0, 0].reshape(NP, 512)], axis=1)
    arrays = {
        "x": feature_major(tokens).reshape(P, KD * NT),
        "w8": np.concatenate(w8, axis=0), "w11": np.concatenate(w11, axis=0),
        "wmod": w_mod.reshape(2, 4, 2, P, 12, 512).transpose(0, 4, 1, 3, 2, 5).reshape(96, P, 1024),
        "sel": np.array([[1, 0], [0, 1], [1, 0], [0, 1]]),
        "bmod": np.concatenate([cols(b_mod[0]), cols(b_mod[1])], axis=1),
        "cvec": np.stack([cols(c[0]), cols(c_ctx)], axis=2).reshape(P, 2 * KD),
        "gains": gains_in, "small": small_in, "wpool": wp, "wconv": np.concatenate(conv, axis=1),
        "kctx0": feature_major(cache_b_k[0, 0].reshape(NP, 256)), "vctx0": cache_b_v[0, 0].reshape(NP, 256),
        "kctx1": feature_major(odd_k), "vctx1": odd_v, "rpb": rpb_rows,
        "cos": cos_t, "sin": sin_t, "maskc": maskc_t, "maskd": maskd_t, "icnt": counts, "ident": np.eye(P),
        "onesd": np.full((P, P), 1.0 / D), "hsel": hsel_t / 64.0, "fback": fback_t,
    }
    arrays = {n: np.ascontiguousarray(t, dtype=np.float32) for n, t in arrays.items()}
    shapes = {"x": (P, KD * NT), "k0": (P, 2, NP), "v0": (P, 256), "k1": (P, 5, NP), "v1": (P, NT)}

    nc = bacc.Bacc("TRN2", target_bir_lowering=False, num_devices=1)
    ins = {n: nc.dram_tensor(f"in_{n}", t.shape, F32, kind="ExternalInput").ap() for n, t in arrays.items()}
    outs = {n: nc.dram_tensor(f"out_{n}", s, F32, kind="ExternalOutput").ap() for n, s in shapes.items()}
    program(nc, ins, outs)
    r = run(nc, [{f"in_{n}": t for n, t in arrays.items()}], core_ids=[0]).results[0]

    def token_major(t):
        return t.transpose(2, 1, 0).reshape(t.shape[2], -1)

    xo = token_major(r["out_x"].reshape(P, KD, NT))
    k0, v0 = token_major(r["out_k0"]), r["out_v0"]
    k1, v1 = token_major(r["out_k1"]), r["out_v1"]
    return (xo[NS:][None], xo[:NS][None],
            k0.reshape(1, 1, NP, 4, DH), v0.reshape(1, 1, NP, 4, DH),
            k1[:, 512:].reshape(1, 1, NP, 2, DH), v1[:, :128].reshape(1, 1, NP, 2, DH),
            k1[:, :512].reshape(1, 1, NP, 8, DH), v1[:, 128:].reshape(1, 1, NP, 8, DH))
```
